# Optimizing a Trainium2 kernel written in Bass

```python
import math
import jax, jax.numpy as jnp
from jax import lax
import numpy as np

D_MODEL = 1024
BATCH = 1
SEQ = 256
DEPTH = 2

N_META = 16
N_EVEN = (DEPTH + 1) // 2
N_ODD = DEPTH // 2
EPS = 1e-5

D_SSD = D_MODEL // 2
SSD_HEADDIM = 64
SSD_HEADS = D_SSD // SSD_HEADDIM
SSD_GROUPS = 2
SSD_STATE = 128
SSD_CONV = 5
SSD_CHUNK = 128
SSD_CONV_DIM = D_SSD + 2 * SSD_GROUPS * SSD_STATE
D_DIFF = D_MODEL // 2
DIFF_HEADDIM = 64
DIFF_HEADS = D_DIFF // (2 * DIFF_HEADDIM)
ROPE_THETA = 500000.0
ROPE_DIM = DIFF_HEADDIM // 4
Q_BLOCK = 128
IN_AB = D_SSD + SSD_CONV_DIM + 2 * SSD_HEADS + 3 * D_DIFF

D_HYENA = D_MODEL
HYENA_SHORT = 3
HYENA_BANDS = 16
HYENA_EMB = 2 * HYENA_BANDS + 1
HYENA_FILTER_WIDTH = 64
HYENA_SHIFT = 0.05
HYENA_TARGET = 1e-2
HYENA_FAST_DECAY = 0.3
HYENA_SLOW_DECAY = 1.5

D_FF = 2816
N_EXPERTS = 8
TOP_K = 2
D_FF_EXPERT = 3584

kernel_name = 'hybrid_ssd_diffattn_hyena_moe_encoder'

F32 = jnp.float32

def rmsnorm(x, w):
    xf = x.astype(F32)
    y = xf * lax.rsqrt(jnp.mean(xf * xf, axis=-1, keepdims=True) + EPS)
    return y.astype(x.dtype) * w.astype(x.dtype)

def conv_centred(x, w, b):
    K, C = w.shape
    y = lax.conv_general_dilated(x, w[:, None, :].astype(x.dtype), window_strides=(1,),
                                 padding=[(K // 2, K // 2)],
                                 dimension_numbers=('NWC', 'WIO', 'NWC'),
                                 feature_group_count=C)
    return y + b.astype(x.dtype)

def swiglu(x, wg, wu, wd):
    return (jax.nn.silu(x @ wg) * (x @ wu)) @ wd

def rotary_tables(T):
    pos = jnp.arange(T, dtype=F32)
    inv_freq = ROPE_THETA ** (-jnp.arange(0, ROPE_DIM, 2, dtype=F32) / ROPE_DIM)
    ang = pos[:, None] * inv_freq[None, :]
    return jnp.cos(ang), jnp.sin(ang)

def partial_rotary(x, cos, sin):
    half = ROPE_DIM // 2
    c = cos[:, None, None, :].astype(x.dtype)
    s = sin[:, None, None, :].astype(x.dtype)
    x1 = x[..., :half]
    x2 = x[..., half:ROPE_DIM]
    return jnp.concatenate([x1 * c - x2 * s, x2 * c + x1 * s, x[..., ROPE_DIM:]], axis=-1)

def ssd_chunked(xs, dt, A, bm, cm):
    b, L, _, _ = xs.shape
    c = L // SSD_CHUNK
    r = SSD_HEADS // SSD_GROUPS
    xdt = (xs.astype(F32) * dt[..., None]).reshape(b, c, SSD_CHUNK, SSD_GROUPS, r, SSD_HEADDIM)
    a = (dt * A).reshape(b, c, SSD_CHUNK, SSD_GROUPS, r)
    bc = bm.astype(F32).reshape(b, c, SSD_CHUNK, SSD_GROUPS, SSD_STATE)
    cc = cm.astype(F32).reshape(b, c, SSD_CHUNK, SSD_GROUPS, SSD_STATE)
    a_cs = jnp.cumsum(a, axis=2)
    a_t = jnp.moveaxis(a_cs, 2, -1)
    seg = a_t[..., :, None] - a_t[..., None, :]
    lower = jnp.tril(jnp.ones((SSD_CHUNK, SSD_CHUNK), dtype=bool))
    lmat = jnp.exp(jnp.where(lower, seg, -jnp.inf))
    cb = jnp.einsum('bcign,bcjgn->bcgij', cc, bc)
    y_diag = jnp.einsum('bcgrij,bcjgrp->bcigrp', cb[:, :, :, None] * lmat, xdt)
    decay_states = jnp.exp(a_cs[:, :, -1:] - a_cs)
    states = jnp.einsum('bcjgn,bcjgrp->bcgrpn', bc, xdt * decay_states[..., None])
    chunk_decay = jnp.exp(a_cs[:, :, -1])

    def step(h, inp):
        st, dec = inp
        return h * dec[..., None, None] + st, h

    _, prev = lax.scan(step, jnp.zeros_like(states[:, 0]),
                       (jnp.moveaxis(states, 1, 0), jnp.moveaxis(chunk_decay, 1, 0)))
    y_off = jnp.einsum('bcign,cbgrpn->bcigrp', cc, prev) * jnp.exp(a_cs)[..., None]
    return (y_diag + y_off).reshape(b, L, SSD_HEADS, SSD_HEADDIM).astype(xs.dtype)

def ssd_direction(xs, dt, A, bm, cm, reverse):
    T = xs.shape[1]
    pad = SSD_CHUNK - N_META
    if reverse:
        xs, dt, bm, cm = [jnp.flip(t, axis=1) for t in (xs, dt, bm, cm)]
        widths = (0, pad)
    else:
        widths = (pad, 0)
    padf = lambda t: jnp.pad(t, [(0, 0), widths] + [(0, 0)] * (t.ndim - 2))
    y = ssd_chunked(padf(xs), padf(dt), A, padf(bm), padf(cm))
    y = y[:, widths[0]:widths[0] + T]
    return jnp.flip(y, axis=1) if reverse else y

def ssd_mixer(z, xbc, dt_raw, conv_w, conv_b, a_log, dt_bias, d_skip, norm_w):
    b, T, _ = xbc.shape
    xbc = jax.nn.silu(conv_centred(xbc, conv_w, conv_b))
    gn = SSD_GROUPS * SSD_STATE
    xs = xbc[..., :D_SSD].reshape(b, T, SSD_HEADS, SSD_HEADDIM)
    bm = xbc[..., D_SSD:D_SSD + gn].reshape(b, T, SSD_GROUPS, SSD_STATE)
    cm = xbc[..., D_SSD + gn:].reshape(b, T, SSD_GROUPS, SSD_STATE)
    y = (d_skip[0] + d_skip[1]).astype(xs.dtype)[:, None] * xs
    for direction in range(2):
        sl = slice(direction * SSD_HEADS, (direction + 1) * SSD_HEADS)
        dt = jax.nn.softplus(dt_raw[..., sl].astype(F32) + dt_bias[direction].astype(F32))
        A = -jnp.exp(a_log[direction].astype(F32))
        y = y + ssd_direction(xs, dt, A, bm, cm, reverse=(direction == 1))
    y = y.reshape(b, T, D_SSD) * jax.nn.silu(z)
    yg = y.reshape(b, T, SSD_GROUPS, D_SSD // SSD_GROUPS)
    return rmsnorm(yg, norm_w.reshape(SSD_GROUPS, -1)).reshape(b, T, D_SSD)

def diff_attn_block(qb, k, v, lam):
    s = jnp.einsum('bqhmd,bkhmd->bhmqk', qb, k).astype(F32) * (DIFF_HEADDIM ** -0.5)
    p = jax.nn.softmax(s, axis=-1)
    a = p[:, :, 0] - lam * p[:, :, 1]
    return jnp.einsum('bhqk,bkhe->bqhe', a.astype(v.dtype), v)

def diff_attention(qkv, cos, sin, lam_params, subln_w, lambda_init):
    b, T, _ = qkv.shape
    H, d = DIFF_HEADS, DIFF_HEADDIM
    q = partial_rotary(qkv[..., :D_DIFF].reshape(b, T, H, 2, d), cos, sin)
    k = partial_rotary(qkv[..., D_DIFF:2 * D_DIFF].reshape(b, T, H, 2, d), cos, sin)
    v = qkv[..., 2 * D_DIFF:].reshape(b, T, H, 2 * d)
    lp = lam_params.astype(F32)
    lam = jnp.exp(jnp.sum(lp[0] * lp[1])) - jnp.exp(jnp.sum(lp[2] * lp[3])) + lambda_init
    block = lambda qb: diff_attn_block(qb, k, v, lam)
    o_meta = block(q[:, :N_META])
    n_blk = (T - N_META) // Q_BLOCK
    qr = jnp.moveaxis(q[:, N_META:].reshape(b, n_blk, Q_BLOCK, H, 2, d), 1, 0)
    o_real = lax.map(block, qr)
    o_real = jnp.moveaxis(o_real, 0, 1).reshape(b, T - N_META, H, 2 * d)
    o = jnp.concatenate([o_meta, o_real], axis=1)
    o = rmsnorm(o, subln_w) * (1.0 - lambda_init)
    return o.reshape(b, T, D_DIFF)

def hyena_filters(T, w1, b1, w2, b2, w3, b3, w4, freq):
    pos = jnp.arange(T, dtype=F32)
    t = pos / (T - 1)
    bands = jnp.linspace(1e-4, HYENA_BANDS - 1, HYENA_BANDS, dtype=F32)
    ang = (2.0 * math.pi * pos / T)[:, None] * bands[None, :]
    zpos = jnp.concatenate([t[:, None], jnp.cos(ang), -jnp.sin(ang)], axis=-1)
    fr = freq.astype(F32)
    h = jnp.sin(fr[0] * (zpos @ w1.astype(F32) + b1.astype(F32)))
    h = jnp.sin(fr[1] * (h @ w2.astype(F32) + b2.astype(F32)))
    h = jnp.sin(fr[2] * (h @ w3.astype(F32) + b3.astype(F32)))
    h = h @ w4.astype(F32)
    max_decay = math.log(HYENA_TARGET) / HYENA_FAST_DECAY
    min_decay = math.log(HYENA_TARGET) / HYENA_SLOW_DECAY
    deltas = jnp.abs(jnp.linspace(min_decay, max_decay, D_HYENA, dtype=F32))
    decay = jnp.exp(-t[:, None] * deltas[None, :]) + HYENA_SHIFT
    h = h * jnp.concatenate([decay, decay], axis=-1)
    hf, hb = h[:, :D_HYENA], h[:, D_HYENA:]
    k = jnp.concatenate([hf, jnp.zeros((1, D_HYENA), F32), hb[:0:-1]], axis=0)
    return k / jnp.sum(jnp.abs(k), axis=0, keepdims=True)

def hyena_mixer(u, w_in, b_in, conv_w, conv_b, f_w1, f_b1, f_w2, f_b2, f_w3, f_b3, f_w4,
                f_freq, skip, w_out, b_out):
    b, T, _ = u.shape
    p = conv_centred(u @ w_in + b_in, conv_w, conv_b)
    x0 = p[..., :D_HYENA]
    x1 = p[..., D_HYENA:2 * D_HYENA]
    v = p[..., 2 * D_HYENA:] * x1
    k = hyena_filters(T, f_w1, f_b1, f_w2, f_b2, f_w3, f_b3, f_w4, f_freq)
    fv = jnp.fft.rfft(v.astype(F32), n=2 * T, axis=1)
    fk = jnp.fft.rfft(k, n=2 * T, axis=0)
    y = jnp.fft.irfft(fv * fk[None], n=2 * T, axis=1)[:, :T]
    y = (y + v.astype(F32) * skip.astype(F32)).astype(u.dtype) * x0
    return y @ w_out + b_out

def moe_swiglu(x, router, wg, wu, wd):
    b, T, D = x.shape
    xt = x.reshape(b * T, D)
    logits = (xt @ router).astype(F32)
    top_v, top_i = lax.top_k(logits, TOP_K)
    wts = jax.nn.softmax(top_v, axis=-1)
    gates = jnp.sum(jax.nn.one_hot(top_i, N_EXPERTS, dtype=F32) * wts[..., None], axis=1)
    out = jnp.zeros_like(xt)
    for e in range(N_EXPERTS):
        ye = swiglu(xt, wg[e], wu[e], wd[e])
        out = out + ye * gates[:, e:e + 1].astype(xt.dtype)
    return out.reshape(b, T, D)

def setup_inputs(seed: int = 0) -> dict:
    key = jax.random.key(seed)
    keys = jax.random.split(key, 64)
    counter = [0]

    def nk():
        k = keys[counter[0]]
        counter[0] += 1
        return k

    def nrm(shape, scale):
        return jax.random.normal(nk(), shape, F32) * scale

    def gain(shape):
        return 1.0 + 0.01 * jax.random.normal(nk(), shape, F32)

    E, O, D = N_EVEN, N_ODD, D_MODEL
    a_log = jnp.log(jax.random.uniform(nk(), (E, 2, SSD_HEADS), F32, 1.0, 16.0))
    dt0 = jnp.exp(jax.random.uniform(nk(), (E, 2, SSD_HEADS), F32, math.log(1e-3), math.log(1e-1)))
    dt_bias = dt0 + jnp.log(-jnp.expm1(-dt0))
    return {
        'x': nrm((BATCH, SEQ, D), 1.0),
        'meta_tokens': nrm((N_META, D), 1.0),
        'norm_mix_even': gain((E, D)),
        'w_in_ab': nrm((E, D, IN_AB), D ** -0.5),
        'ssd_conv_w': nrm((E, SSD_CONV, SSD_CONV_DIM), SSD_CONV ** -0.5),
        'ssd_conv_b': nrm((E, SSD_CONV_DIM), 0.01),
        'ssd_a_log': a_log,
        'ssd_dt_bias': dt_bias,
        'ssd_d': gain((E, 2, SSD_HEADS)),
        'ssd_norm_w': gain((E, D_SSD)),
        'diff_lambda': nrm((E, 4, DIFF_HEADDIM), 0.1),
        'diff_subln_w': gain((E, 2 * DIFF_HEADDIM)),
        'w_out_ab': nrm((E, D_SSD + D_DIFF, D), (D_SSD + D_DIFF) ** -0.5),
        'norm_ffn_even': gain((E, D)),
        'ffn_w_gate': nrm((E, D, D_FF), D ** -0.5),
        'ffn_w_up': nrm((E, D, D_FF), D ** -0.5),
        'ffn_w_down': nrm((E, D_FF, D), D_FF ** -0.5),
        'norm_mix_odd': gain((O, D)),
        'hy_w_in': nrm((O, D, 3 * D_HYENA), D ** -0.5),
        'hy_b_in': nrm((O, 3 * D_HYENA), 0.01),
        'hy_conv_w': nrm((O, HYENA_SHORT, 3 * D_HYENA), HYENA_SHORT ** -0.5),
        'hy_conv_b': nrm((O, 3 * D_HYENA), 0.01),
        'hy_f_w1': nrm((O, HYENA_EMB, HYENA_FILTER_WIDTH), HYENA_EMB ** -0.5),
        'hy_f_b1': nrm((O, HYENA_FILTER_WIDTH), 0.02),
        'hy_f_w2': nrm((O, HYENA_FILTER_WIDTH, HYENA_FILTER_WIDTH), HYENA_FILTER_WIDTH ** -0.5),
        'hy_f_b2': nrm((O, HYENA_FILTER_WIDTH), 0.02),
        'hy_f_w3': nrm((O, HYENA_FILTER_WIDTH, HYENA_FILTER_WIDTH), HYENA_FILTER_WIDTH ** -0.5),
        'hy_f_b3': nrm((O, HYENA_FILTER_WIDTH), 0.02),
        'hy_f_w4': nrm((O, HYENA_FILTER_WIDTH, 2 * D_HYENA), HYENA_FILTER_WIDTH ** -0.5),
        'hy_f_freq': gain((O, 3, HYENA_FILTER_WIDTH)),
        'hy_skip': nrm((O, D_HYENA), 0.1),
        'hy_w_out': nrm((O, D_HYENA, D), D_HYENA ** -0.5),
        'hy_b_out': nrm((O, D), 0.01),
        'norm_ffn_odd': gain((O, D)),
        'moe_router': nrm((O, D, N_EXPERTS), D ** -0.5),
        'moe_w_gate': nrm((O, N_EXPERTS, D, D_FF_EXPERT), D ** -0.5),
        'moe_w_up': nrm((O, N_EXPERTS, D, D_FF_EXPERT), D ** -0.5),
        'moe_w_down': nrm((O, N_EXPERTS, D_FF_EXPERT, D), D_FF_EXPERT ** -0.5),
        'final_norm': gain((D,)),
    }

def reference(x, meta_tokens, norm_mix_even, w_in_ab, ssd_conv_w, ssd_conv_b, ssd_a_log,
              ssd_dt_bias, ssd_d, ssd_norm_w, diff_lambda, diff_subln_w, w_out_ab,
              norm_ffn_even, ffn_w_gate, ffn_w_up, ffn_w_down, norm_mix_odd, hy_w_in, hy_b_in,
              hy_conv_w, hy_conv_b, hy_f_w1, hy_f_b1, hy_f_w2, hy_f_b2, hy_f_w3, hy_f_b3,
              hy_f_w4, hy_f_freq, hy_skip, hy_w_out, hy_b_out, norm_ffn_odd, moe_router,
              moe_w_gate, moe_w_up, moe_w_down, final_norm):
    b = x.shape[0]
    meta = jnp.broadcast_to(meta_tokens[None].astype(x.dtype), (b, N_META, D_MODEL))
    h = jnp.concatenate([meta, x], axis=1)
    T = h.shape[1]
    cos, sin = rotary_tables(T)
    o0 = D_SSD
    o1 = o0 + SSD_CONV_DIM
    o2 = o1 + 2 * SSD_HEADS
    for layer in range(DEPTH):
        i = layer // 2
        if layer % 2 == 0:
            proj = rmsnorm(h, norm_mix_even[i]) @ w_in_ab[i]
            ssd_out = ssd_mixer(proj[..., :o0], proj[..., o0:o1], proj[..., o1:o2],
                                ssd_conv_w[i], ssd_conv_b[i], ssd_a_log[i], ssd_dt_bias[i],
                                ssd_d[i], ssd_norm_w[i])
            lambda_init = 0.8 - 0.6 * math.exp(-0.3 * layer)
            attn_out = diff_attention(proj[..., o2:], cos, sin, diff_lambda[i],
                                      diff_subln_w[i], lambda_init)
            h = h + jnp.concatenate([ssd_out, attn_out], axis=-1) @ w_out_ab[i]
            h = h + swiglu(rmsnorm(h, norm_ffn_even[i]), ffn_w_gate[i], ffn_w_up[i], ffn_w_down[i])
        else:
            h = h + hyena_mixer(rmsnorm(h, norm_mix_odd[i]), hy_w_in[i], hy_b_in[i],
                                hy_conv_w[i], hy_conv_b[i], hy_f_w1[i], hy_f_b1[i],
                                hy_f_w2[i], hy_f_b2[i], hy_f_w3[i], hy_f_b3[i], hy_f_w4[i],
                                hy_f_freq[i], hy_skip[i], hy_w_out[i], hy_b_out[i])
            h = h + moe_swiglu(rmsnorm(h, norm_ffn_odd[i]), moe_router[i], moe_w_gate[i],
                               moe_w_up[i], moe_w_down[i])
    return rmsnorm(h, final_norm)[:, N_META:]


_drawn_inputs = setup_inputs


def setup_inputs(seed=0):
    import zlib

    import numpy as np

    out = dict(_drawn_inputs(seed))
    spreads = {}
    factors = {'ssd_d': 31.608,
     'diff_subln_w': 14.452,
     'norm_ffn_even': 3.599,
     'norm_mix_odd': 23.207,
     'hy_b_in': 24.781,
     'hy_conv_b': 21.253,
     'hy_f_b1': 8.0,
     'hy_f_b2': 4.483,
     'hy_f_b3': 8.0,
     'hy_f_freq': 8.0,
     'norm_ffn_odd': 110.233,
     'final_norm': 191.666,
     'ssd_conv_b': 6.211,
     'ssd_norm_w': 7.217,
     'hy_b_out': 64.0}
    for name, (base, spread) in spreads.items():
        noise = np.random.default_rng([zlib.crc32(name.encode()), seed]).standard_normal(out[name].shape)
        drawn = base * np.exp(spread * noise) if base else spread * noise
        out[name] = __import__('jax').numpy.asarray(drawn.astype(out[name].dtype))
    for name, factor in factors.items():
        out[name] = (out[name] * factor).astype(out[name].dtype)
    return out
```

```python
from contextlib import ExitStack
import math

import numpy as np

import concourse.bass as bass
from concourse import mybir

F32 = mybir.dt.float32
BF16 = mybir.dt.bfloat16
I32 = mybir.dt.int32
ALU = mybir.AluOpType
ACT = mybir.ActivationFunctionType
AX = mybir.AxisListType

P = 128
D = 1024
KT = D // P
SEQ = 256
META = 16
T = SEQ + META
TOKS = [(0, P), (P, P), (2 * P, T - 2 * P)]
EPS = 1e-5
HEADS = 8
CONV = 5
ATT = 4
FF = 2816
FFT = FF // P
FEXP = 3584
NE = 8
HY = 3 * D
SHORT = 3
RING = 4
SLOT = 11 * 256
CAP = 96
STAGES = FEXP // 256
ITEMS = 2 * NE
LAMBDA_INIT = 0.8 - 0.6 * math.exp(-0.3 * 0)
TWO_PI_A = 6.28125
TWO_PI_B = 2.0 * math.pi - TWO_PI_A
ROUND = 12582912.0

C_NME, C_CW, C_CB, C_SNW, C_SUB, C_NFE, C_NMO, C_BIN, C_SKIP, C_BOUT, C_A = 0, 8, 48, 56, 60, 61, 69, 77, 101, 109, 117
C_HCW, C_HCB, C_NFO, C_FIN, C_B = 128, 200, 224, 232, 240
C_FV = 256

K_SIZES = [("ident", P), ("perm", P), ("cos", T), ("sin", T), ("uf", 3 * T), ("ub", 3 * T), ("cf", 3 * T), ("sf", 3 * T),
           ("ci", 3 * SEQ), ("si", 3 * SEQ), ("us", 2 * SEQ), ("iota", CAP), ("tri", NE * NE), ("cand", 2 * ITEMS)]
K_AT = {}
_at = 0
for _name, _n in K_SIZES:
    K_AT[_name] = (_at, _n)
    _at += _n
K_ALL = _at
K_FIRST = K_AT["uf"][0]


def shape_constants():
    f32 = np.float32
    c = np.zeros((P, K_ALL), f32)

    def put(name, a):
        at, n = K_AT[name]
        c[:a.shape[0], at:at + n] = a.reshape(a.shape[0], n)

    def tiles(a):
        out = np.zeros((3, P) + a.shape[1:], f32)
        out.reshape((3 * P,) + a.shape[1:])[:a.shape[0]] = a
        return out.transpose(1, 0, 2)

    put("ident", np.eye(P, dtype=f32))
    perm = np.zeros((P, P), f32)
    cos = np.ones((P, T), f32)
    sin = np.zeros((P, T), f32)
    pos = np.arange(T, dtype=f32)
    inv = (f32(500000.0) ** (-np.arange(0, 16, 2, dtype=f32) / f32(16))).astype(f32)
    ang = pos[:, None] * inv[None, :]
    for base in (0, 64):
        for i in range(8):
            perm[base + 8 + i, base + i] = -1.0
            perm[base + i, base + 8 + i] = 1.0
            cos[base + i] = cos[base + 8 + i] = np.cos(ang[:, i])
            sin[base + i] = sin[base + 8 + i] = np.sin(ang[:, i])
    put("perm", perm)
    put("cos", cos)
    put("sin", sin)
    j, i = np.arange(T)[:, None], np.arange(T)[None, :]
    put("uf", tiles((j <= i).astype(f32)))
    put("ub", tiles((j >= i).astype(f32)))
    w = 2.0 * np.pi * ((np.arange(T)[None, :] + 0.5) * np.arange(T)[:, None]) / (2 * T)
    put("cf", tiles(np.cos(w).astype(f32)))
    put("sf", tiles(np.sin(w).astype(f32)))
    put("ci", tiles((np.cos(w[META:]).T / T).astype(f32)))
    put("si", tiles((np.sin(w[META:]).T / T).astype(f32)))
    us = (np.arange(SEQ)[:, None] < np.arange(SEQ)[None, :]).astype(f32)
    put("us", us.reshape(2, P, SEQ).transpose(1, 0, 2))
    put("iota", np.tile(np.arange(CAP, dtype=f32), (P, 1)))
    put("tri", np.tile((np.arange(NE)[:, None] > np.arange(NE)[None, :]).astype(f32).reshape(1, -1), (P, 1)))
    cand = np.stack([np.tile(np.arange(NE), 2), np.repeat([CAP, 2 * CAP], NE)]).astype(f32)
    put("cand", np.tile(cand.reshape(1, -1), (P, 1)))
    sel8 = np.repeat(np.eye(HEADS, dtype=f32), P, axis=1)
    t = pos / f32(T - 1)
    bands = np.linspace(1e-4, 15, 16, dtype=f32)
    ang = (f32(2.0 * math.pi) * pos / f32(T))[:, None] * bands[None, :]
    zpos = np.ascontiguousarray(np.concatenate([t[:, None], np.cos(ang), -np.sin(ang)], axis=-1).T.astype(f32))
    lo, hi = math.log(1e-2) / 1.5, math.log(1e-2) / 0.3
    deltas = np.abs(np.linspace(lo, hi, D, dtype=f32))
    window = (np.exp(-t[:, None] * deltas[None, :]) + f32(0.05)).astype(f32)
    return {"k_table": c, "k_sel8": sel8, "k_zpos": zpos, "k_window": np.ascontiguousarray(tiles(window))}


class Steps:

    def __init__(self, eng, chain):
        self.eng, self.chain, self.count, self.i, self.per = eng, chain, {}, None, {}

    def __call__(self, ins, sem=None):
        sem = self.chain if sem is None else sem
        ins.then_inc(sem, 1)
        n = self.count[id(sem)] = self.count.get(id(sem), 0) + 1
        self.eng.wait_ge(sem, n if self.i is None or id(sem) not in self.per else self.per[id(sem)] * self.i + n)

    def credit(self, sem, n):
        self.count[id(sem)] = self.count.get(id(sem), 0) + n

    def loop(self, i, per):
        self.i, self.per = i, {id(s): k for s, k in per}
        self.start = dict(self.count)

    def end(self, times):
        for s, k in self.per.items():
            assert self.count.get(s, 0) - self.start.get(s, 0) == k, (self.count.get(s, 0), self.start.get(s, 0), k)
            self.count[s] = self.start.get(s, 0) + k * times
        self.i = None


def tile_order():
    order = []

    def add(group, first, n=1):
        order.extend((group, k) for k in range(first, first + n))

    add("param", 0)
    add("xin", 0, 5)
    add("ss1", 0)
    add("proj", 0, 12)
    add("dt", 0)
    add("cs", 0, 3)
    add("xs", 0, 3)
    add("cb", 0, 6)
    for s in range(10):
        if s < 8:
            add("row", 2 * s, 2)
        if s < 6:
            add("proj", 12 + 2 * s, 2)
        if s >= 3 and s % 2 == 1:
            add("y", (s - 3) // 2)
    add("rope", 0, 8)
    add("gss", 0, 2)
    add("vt", 0, 3)
    add("score", 0, 6)
    for h in range(ATT):
        if h + 1 < ATT:
            add("score", 6 * h + 6, 6)
        add("at", 3 * h, 3)
        add("o", h)
    add("oss", 0, 4)
    add("wo", 0, 8)
    add("ss2", 0)
    for b in range(FFT // 2):
        add("gate", 2 * b, 2)
        add("up", 2 * b, 2)
    add("down", 0, 8)
    add("mlp", 0, 3)
    add("kt", 0, 12)
    add("kspec", 0, 12)
    add("kn", 0)
    add("ss3", 0)
    add("hy", 0, 24)
    add("vx", 0, 6)
    add("vspec", 0, 12)
    add("inv", 0, 8)
    add("ho", 0, 8)
    add("ss4", 0)
    add("logit", 0)
    add("xk", 0, 4)
    add("pos", 0)
    add("gt", 0, 4)
    return order


ORDER = tile_order()
NUMBER = {key: n for n, key in enumerate(ORDER)}
CREDIT = {"hy": 8, "gate": 4, "up": 4}


def trunk(nc, A, out):
    ctx = ExitStack()
    with ctx:
        sems = {}

        def sem(name):
            if name not in sems:
                sems[name] = ctx.enter_context(nc.semaphore(name))
            return sems[name]

        def sb(name, shape, dt=F32):
            return ctx.enter_context(nc.sbuf_tensor(name, shape, dt))

        ps = [ctx.enter_context(nc.psum_tensor(f"ps{i}", [P, 512], F32)) for i in range(8)]

        hT = sb("hT", [P, KT, T])
        xn = sb("xn", [P, KT, T])
        sq = sb("sq", [P, KT, T])
        rstd = sb("rstd", [P, T])
        ktab = sb("ktab", [P, K_ALL])
        sel8 = sb("sel8", [HEADS, HEADS * P])
        zpos = sb("zpos", [33, T])
        prow = sb("prow", [P, 3, P])
        par = sb("par", [P, 264])
        ones = sb("ones", [P, P])
        eps = sb("eps", [P, 1])
        bcast = sb("bcast", [P, 16 + 16 + 256 + 16 + 4])
        lam = sb("lam", [P, 8])
        wdt = sb("wdt", [P, KT, 16])
        fw1 = sb("fw1", [33, 64])
        fw23 = sb("fw23", [64, 2, 64])
        router = sb("router", [P, KT, NE])
        ring = sb("ring", [P, RING, SLOT])
        arena_n = 25344
        arena = sb("arena", [P, arena_n])

        def const(name, *dims):
            at, n = K_AT[name]
            a = ktab[:, at:at + n]
            return a.rearrange("p (a b) -> p a b", a=dims[0]) if dims else a

        ident, perm, cosT, sinT = const("ident"), const("perm"), const("cos"), const("sin")
        UF, UB, CF, SF = (const(n, 3) for n in ("uf", "ub", "cf", "sf"))
        CI, SI, US = const("ci", 3), const("si", 3), const("us", 2)
        iota, tri, cand = const("iota"), const("tri", NE), const("cand", 2)
        dt_bias, a_log, lam_in = bcast[:, 0:16], bcast[:, 16:32], bcast[:, 32:288]
        d_in, dskip = bcast[:, 288:304], bcast[:, 304:308]

        def area(at, a, b=None, c=None):
            n = a * (b or 1) * (c or 1)
            assert at + n <= arena_n, (at, n)
            v = arena[:, at:at + n]
            if c:
                return v.rearrange("p (a b c) -> p a b c", a=a, b=b)
            return v.rearrange("p (a b) -> p a b", a=a) if b else v

        xp = area(0, 8, T + 4)
        xbc = area(2208, 8, T)
        zs = area(4384, 4, T)
        qk = area(5472, 8, T)
        vf = area(7648, 4, T)
        xT = area(8736, 3, 512)
        vT = area(0, 3, 512)
        CB = area(10272, 6, T)
        M = area(11904, 4, 3, T)
        RB = area(15168, 2, 3, T)
        W = area(16800, 2, 3, T)
        W1 = area(18432, 2, 3, T)
        cat = area(20064, 8, T)
        ysb = area(22240, 4, T)
        dtw = area(23328, 8, 48)
        csr = area(23712, 2, T)
        convt = area(24256, 2, T)
        ropet = area(24800, 2, T)
        xtok = area(11904, 2, D)
        mtok = area(13952, D)
        pr = area(11904, 2, 2, T)
        at_ = area(12992, 2, 3, T)
        aT = area(14624, 2, 3, T)
        osb = area(16256, 4, T)
        stat = area(17344, 24, 4)
        ffh = area(0, FFT, T)
        sg = area(5984, 4, T)
        KR = area(0, 3, D)
        KI = area(3072, 3, D)
        kfb = area(6144, 3, 2 * D)
        KE = area(12288, 3, D)
        KO = area(15360, 3, D)
        win = area(18432, 3, D)
        fw4 = area(21504, 2 * D)
        harg = area(23552, 4, T)
        hyc = area(6144, 24, T)
        pad = area(12672, 8, T + 2)
        vtok = area(14864, 3, D)
        YR = area(17936, 3, D)
        YI = area(21008, 3, D)
        prod = area(12672, 4, 512)
        invn = area(24080, 8)
        ytmp = area(24088, 2, SEQ)
        ering = area(0, 2, 3 * 2048)
        SEL = area(12288, 2, ITEMS, CAP)
        SELG = area(15360, 2, ITEMS, CAP)
        GT = area(18432, ITEMS, SEQ)
        xtk = ring[:, 0, 0:2048].rearrange("p (a b) -> p a b", a=2)
        xg = ring[:, 1, 0:KT * CAP].rearrange("p (a b) -> p a b", a=KT)
        ye = ring[:, 1, 1024:2048]
        esg = ring[:, 2, 0:384].rearrange("p (a b) -> p a b", a=2)
        eh = ring[:, 2, 384:768].rearrange("p (a b) -> p a b", a=2)
        rt = ring[:, 2, 768:2816]
        osb2 = ring[:, 3, 0:2048].rearrange("p (a b) -> p a b", a=2)
        crd = sb("crd", [P, 16])
        zero16 = sb("zero16", [P, 512], BF16)
        tabf = sb("tabf", [1, 16])
        tab = sb("tab", [1, 16], I32)

        def ready(eng, group, k):
            n = NUMBER[(group, k)]
            eng.wait_ge(sem("tile_ready"), n + 1)
            return ps[n % 8]

        def used(group):
            return sem("used_" + group)

        block = ctx.enter_context(nc.Block())

        w_in = A["w_in_ab"][0].rearrange("(k p) n -> p k n", p=P)
        stream = []
        for c in [512 + 256 * b for b in range(4)] + [0, 256] + [1552 + 256 * b for b in range(6)]:
            stream.append((w_in[:, :, c:c + 256], KT))
        w_out = A["w_out_ab"][0].rearrange("(k p) n -> p k n", p=P)
        for b in range(4):
            stream.append((w_out[:, :, 256 * b:256 * b + 256], KT))
        wg0 = A["ffn_w_gate"][0].rearrange("(k p) n -> p k n", p=P)
        wu0 = A["ffn_w_up"][0].rearrange("(k p) n -> p k n", p=P)
        for b in range(FFT // 2):
            stream.append((wg0[:, :, 256 * b:256 * b + 256], KT))
            stream.append((wu0[:, :, 256 * b:256 * b + 256], KT))
        wd0 = A["ffn_w_down"][0].rearrange("(k p) n -> p k n", p=P)
        for b in range(4):
            for half in range(2):
                stream.append((wd0[:, 11 * half:11 * half + 11, 256 * b:256 * b + 256], 11))
        hwi = A["hy_w_in"][0].rearrange("(k p) n -> p k n", p=P)
        for c in [D + 256 * b for b in range(8)] + [256 * b for b in range(4)]:
            stream.append((hwi[:, :, c:c + 256], KT))
        hwo = A["hy_w_out"][0].rearrange("(k p) n -> p k n", p=P)
        for b in range(4):
            stream.append((hwo[:, :, 256 * b:256 * b + 256], KT))
        B_WO, B_FF, B_DN, B_HY, B_HO = 12, 16, 38, 46, 58

        def last_tile(n):
            if n < B_WO:
                return ("proj", 2 * n + 1)
            if n < B_FF:
                return ("wo", 2 * (n - B_WO) + 1)
            if n < B_DN:
                b = n - B_FF
                return ("up" if b % 2 else "gate", b // 2 * 2 + 1)
            if n < B_HY:
                return ("down", (n - B_DN) // 2 * 2 + (n - B_DN) % 2)
            return ("hy", 2 * (n - B_HY) + 1) if n < B_HO else ("ho", 2 * (n - B_HO) + 1)

        slot_in = [sem(f"slot{i}_in") for i in range(RING)]

        def slot(n, k=KT):
            return ring[:, n % RING, 0:k * 256].rearrange("p (k n) -> p k n", k=k)

        moe = {n: A[n] for n in ("moe_w_gate", "moe_w_up", "moe_w_down")}

        @block.sync
        def _(sp):
            for n, (src, k) in enumerate(stream):
                if n >= RING:
                    sp.wait_ge(sem("tile_ready"), NUMBER[last_tile(n - RING)] + 1)
                if n == B_FF + 8:
                    sp.dma_start(win, A["k_window"]).then_inc(sem("window_in"), 16)
                    sp.dma_start(fw4[0:64, :], A["hy_f_w4"][0]).then_inc(sem("window_in"), 16)
                sp.dma_start(slot(n, k), src).then_inc(slot_in[n % RING], 16)
            sp.wait_ge(sem("hyena_done"), 1)

            def item(i, e):
                with sp.Fori(0, STAGES // 2) as q:
                    for p in range(2):
                        s = 14 * i + 2 * q + p
                        g = ering[:, p, 0:2048].rearrange("p (k n) -> p k n", k=KT)
                        u = ering[:, p, 2048:4096].rearrange("p (k n) -> p k n", k=KT)
                        d = ering[:, p, 4096:6144].rearrange("p (k n) -> p k n", k=2)
                        sp.wait_ge(sem("gu_done"), s + 1)
                        for w, dst in (("moe_w_gate", g), ("moe_w_up", u)):
                            src = moe[w][0, bass.ds(e, 1), :, bass.ds(512 * q + 256 * p, 256)]
                            sp.dma_start(dst, src.rearrange("e (k p) n -> p (e k) n", p=P)).then_inc(sem(f"gu_in{p}"), 16)
                        sp.wait_ge(sem("down_done"), s + 1)
                        src = moe["moe_w_down"][0, bass.ds(e, 1), bass.ds(512 * q + 256 * p, 256), :]
                        sp.dma_start(d, src.rearrange("e (k p) n -> p (e k) n", p=P)).then_inc(sem(f"d_in{p}"), 16)

            with sp.Fori(0, NE) as i:
                item(i, i)
            sp.wait_ge(sem("later_count"), 1)
            more = sp.value_load(tab[0:1, 0:1], min_val=0, max_val=NE)
            with sp.If(more > 0):
                sp.wait_ge(sem("later_table"), 1)
                with sp.Fori(0, more) as j:
                    e = sp.value_load(tab[0:1, bass.ds(j + 1, 1)], min_val=0, max_val=NE - 1)
                    item(j + NE, e)
            for tt in range(2):
                sp.wait_ge(sem("out_ready"), 2 * tt + 2)
                sp.dma_start(out[0, tt * P:(tt + 1) * P, :], osb2[:, tt, :]).then_inc(sem("out_done"), 16)
            sp.wait_ge(sem("out_done"), 32)

        @block.gpsimd
        def _(pool):
            g = Steps(pool, sem("pool_chain"))
            g(nc.gpsimd.memset(ones[:], 1.0), sem("pool_consts"))
            g(nc.gpsimd.memset(eps[:], EPS), sem("pool_consts"))
            g(nc.gpsimd.memset(zero16[:], 0.0), sem("pool_consts"))
            pool.wait_ge(sem("table_in"), 32)
            for h in range(HEADS):
                pool.wait_ge(sem("dt_ready"), 1)
                if h >= 2:
                    pool.wait_ge(sem("m_ready"), h - 1)
                for tt, (t0, n) in enumerate(TOKS):
                    g(nc.gpsimd.tensor_scalar(W1[0:n, h % 2, tt, :], UB[0:n, tt, :], dtw[0:n, 4, 16 * tt + 8 + h:16 * tt + 9 + h],
                                              None, ALU.mult), sem("w1_ready"))
            for k in range(6):
                n = TOKS[k // 2][1]
                c = slice(512 * (k % 2), 512 * (k % 2) + 512)
                pool.wait_ge(sem("prod_ready"), 4 * k + 4)
                g(nc.gpsimd.tensor_tensor(YR[0:n, k // 2, c], prod[0:n, 0, :], prod[0:n, 1, :], ALU.subtract), sem("spec_ready"))
                g(nc.gpsimd.tensor_tensor(YI[0:n, k // 2, c], prod[0:n, 2, :], prod[0:n, 3, :], ALU.add), sem("spec_ready"))

        @block.scalar
        def _(act):
            a = Steps(act, sem("act_chain"))

            act.dma_start(ktab[:, 0:K_FIRST], A["k_table"][:, 0:K_FIRST]).then_inc(sem("ident_in"), 16)
            act.dma_start(xtok, A["x"][0].rearrange("(t p) d -> p t d", p=P)).then_inc(sem("x_in"), 16)
            act.dma_start(mtok[0:META, :], A["meta_tokens"]).then_inc(sem("x_in"), 16)
            rows = [(0, C_NME, A["norm_mix_even"].rearrange("e (t p) -> (e t) p", p=P)),
                    (0, C_CW, A["ssd_conv_w"].rearrange("e k (t p) -> (e k t) p", p=P)),
                    (0, C_CB, A["ssd_conv_b"].rearrange("e (t p) -> (e t) p", p=P)),
                    (0, C_SNW, A["ssd_norm_w"].rearrange("e (t p) -> (e t) p", p=P)),
                    (0, C_SUB, A["diff_subln_w"]),
                    (0, C_NFE, A["norm_ffn_even"].rearrange("e (t p) -> (e t) p", p=P)),
                    (0, C_NMO, A["norm_mix_odd"].rearrange("e (t p) -> (e t) p", p=P)),
                    (0, C_BIN, A["hy_b_in"][:, D:].rearrange("e (t p) -> (e t) p", p=P)),
                    (0, C_BIN + 16, A["hy_b_in"][:, 0:D].rearrange("e (t p) -> (e t) p", p=P)),
                    (0, C_SKIP, A["hy_skip"].rearrange("e (t p) -> (e t) p", p=P)),
                    (0, C_BOUT, A["hy_b_out"].rearrange("e (t p) -> (e t) p", p=P)),
                    (1, C_HCB - P, A["hy_conv_b"][:, D:].rearrange("e (t p) -> (e t) p", p=P)),
                    (1, C_HCB - P + 16, A["hy_conv_b"][:, 0:D].rearrange("e (t p) -> (e t) p", p=P)),
                    (1, C_NFO - P, A["norm_ffn_odd"].rearrange("e (t p) -> (e t) p", p=P)),
                    (1, C_FIN - P, A["final_norm"].rearrange("(t p) -> t p", p=P))]
            for k in range(SHORT):
                rows.append((1, 24 * k, A["hy_conv_w"][0, k:k + 1, D:].rearrange("e (t p) -> (e t) p", p=P)))
                rows.append((1, 24 * k + 16, A["hy_conv_w"][0, k:k + 1, 0:D].rearrange("e (t p) -> (e t) p", p=P)))
            for which, at, src in rows:
                act.dma_start(prow[at:at + src.shape[0], which, :], src).then_inc(sem("param_in"), 16)
            for k, name in enumerate(("hy_f_b1", "hy_f_b2", "hy_f_b3")):
                act.dma_start(prow[k:k + 1, 2, 0:64], A[name]).then_inc(sem("param_in"), 16)
            act.dma_start(prow[3:6, 2, 0:64], A["hy_f_freq"][0]).then_inc(sem("param_in"), 16)
            assert len(rows) + 4 == 25
            act.dma_start(wdt[:], w_in[:, :, 1536:1552]).then_inc(sem("dt_in"), 16)
            act.dma_start(dt_bias, A["ssd_dt_bias"].rearrange("e a h -> e (a h)").partition_broadcast(P)).then_inc(sem("dt_in"), 16)
            act.dma_start(a_log, A["ssd_a_log"].rearrange("e a h -> e (a h)").partition_broadcast(P)).then_inc(sem("dt_in"), 16)
            act.dma_start(lam_in, A["diff_lambda"].rearrange("e a h -> e (a h)").partition_broadcast(P)).then_inc(sem("dt_in"), 16)
            act.dma_start(d_in, A["ssd_d"].rearrange("e a h -> e (a h)").partition_broadcast(P)).then_inc(sem("dt_in"), 16)
            act.dma_start(ktab[:, K_FIRST:], A["k_table"][:, K_FIRST:]).then_inc(sem("table_in"), 16)
            act.dma_start(sel8[:], A["k_sel8"]).then_inc(sem("table_in"), 16)
            act.dma_start(zpos[:], A["k_zpos"]).then_inc(sem("filter_in"), 16)
            act.dma_start(fw1[:], A["hy_f_w1"][0]).then_inc(sem("filter_in"), 16)
            act.dma_start(fw23[:, 0, :], A["hy_f_w2"][0]).then_inc(sem("filter_in"), 16)
            act.dma_start(fw23[:, 1, :], A["hy_f_w3"][0]).then_inc(sem("filter_in"), 16)
            act.dma_start(router[:], A["moe_router"][0].rearrange("(k p) n -> p k n", p=P)).then_inc(sem("router_in"), 16)

            def copy(group, k, dst, part=P, cols=slice(0, T), scale=1.0):
                t = ready(act, group, k)
                a(nc.scalar.activation(dst, t[0:part, cols], ACT.Copy, scale=scale), used(group))

            def root(group, k, n, cols=T, part=slice(0, P), sig="rms_ready"):
                t = ready(act, group, k)
                a(nc.scalar.activation(rstd[:, 0:cols], t[:, 0:cols], ACT.Sqrt, bias=eps[:, 0:1], scale=1.0 / n), used(group))

            def square(lo, hi, toks=slice(0, T)):
                a(nc.scalar.activation(sq[:, lo:hi, toks], hT[:, lo:hi, toks], ACT.Square), sem("act_squares"))

            t = ready(act, "param", 0)
            a(nc.scalar.activation(par[:, 0:C_A], t[:, 0:C_A], ACT.Copy))
            a(nc.scalar.activation(par[:, C_HCW:C_B], t[:, C_HCW:C_B], ACT.Copy))
            a(nc.scalar.activation(par[0:64, C_FV:C_FV + 6], t[0:64, C_FV:C_FV + 6], ACT.Copy), used("param"))
            for tt in range(2):
                for half in range(2):
                    t = ready(act, "xin", 2 * tt + half)
                    a(nc.scalar.activation(hT[:, 4 * half:4 * half + 4, META + P * tt:META + P * tt + P],
                                           t[:, :].rearrange("p (a b) -> p a b", a=4), ACT.Copy), used("xin"))
            t = ready(act, "xin", 4)
            a(nc.scalar.activation(hT[:, :, 0:META], t[:, 0:P].rearrange("p (a b) -> p a b", a=8), ACT.Copy), used("xin"))
            square(0, 4)
            act.wait_ge(sem("pool_consts"), 3)
            root("ss1", 0, D)

            def ssd_silu(j):
                act.wait_ge(sem("conv_ready"), j + 1)
                a(nc.scalar.activation(xbc[:, j, :], convt[:, j % 2, :], ACT.Silu), sem("xbc_ready"))

            act.wait_ge(sem("xp_zero"), 1)
            for j in range(8):
                copy("proj", j, xp[:, j, 2:2 + T])
                if j >= 1:
                    ssd_silu(j - 1)
            ssd_silu(7)
            for j in range(4):
                t = ready(act, "proj", 8 + j)
                a(nc.scalar.activation(zs[:, j, :], t[:, 0:T], ACT.Silu), used("proj"))
            act.wait_ge(sem("dt_raw"), 1)
            act.wait_ge(sem("dt_in"), 16 * 5)
            a(nc.scalar.activation(dtw[:, 7, 0:16], a_log, ACT.Exp))
            a(nc.scalar.activation(dtw[:, 2, :], dtw[:, 1, :], ACT.Exp, scale=-1.0))
            a(nc.scalar.activation(dtw[:, 3, :], dtw[:, 2, :], ACT.Ln, bias=1.0), sem("dt_log"))
            for k in range(2):
                copy("cs", k, csr[0:HEADS, k, :], HEADS)
            t = ready(act, "cs", 2)
            a(nc.scalar.activation(dtw[:, 6, 0:32], t[:, 0:32], ACT.Copy))
            a(nc.scalar.activation(dtw[0:META, 6, 32:48], t[0:META, 32:48], ACT.Copy), used("cs"))
            for tt, (t0, n) in enumerate(TOKS):
                copy("xs", tt, xT[0:n, tt, :], n, slice(0, 512))
            for k in range(6):
                n = TOKS[k % 3][1]
                copy("cb", k, CB[0:n, k, :], n)

            def decay_rows(h):
                for way, dst in ((0, M[:, h % 4]), (1, RB[:, h % 2])):
                    if way == 1 and h >= 2:
                        act.wait_ge(sem("decay_sum"), h - 1)
                    t = ready(act, "row", 2 * h + way)
                    for tt, (t0, n) in enumerate(TOKS):
                        a(nc.scalar.activation(dst[0:n, tt, :], t[0:n, 0:T], ACT.Relu, scale=-1.0,
                                               bias=dtw[0:n, 6, 16 * tt + 8 * way + h:16 * tt + 8 * way + h + 1]),
                          used("row") if tt == 2 else None)

            def decay_exp(h):
                act.wait_ge(sem("decay_sum"), h + 1)
                a(nc.scalar.activation(M[:, h % 4, 0:2, :], M[:, h % 4, 0:2, :], ACT.Exp, scale=-1.0))
                a(nc.scalar.activation(M[0:META, h % 4, 2, :], M[0:META, h % 4, 2, :], ACT.Exp, scale=-1.0), sem("decay_ready"))

            for s in range(9):
                if s < 8:
                    if s >= 4:
                        act.wait_ge(sem("tile_ready"), NUMBER[("y", (s - 4) // 2)] + 1)
                    decay_rows(s)
                if s < 6:
                    for j in range(12 + 2 * s, 14 + 2 * s):
                        if j < 16:
                            copy("proj", j, qk[:, j - 12, :], scale=64.0 ** -0.5)
                        elif j < 20:
                            copy("proj", j, qk[:, j - 12, :])
                        else:
                            copy("proj", j, vf[:, j - 20, :])
                if s < 8:
                    decay_exp(s)
            act.wait_ge(sem("yz_ready"), 4)
            a(nc.scalar.activation(sq[:, 0:4, :], ysb, ACT.Square), sem("act_squares"))
            for k in range(2):
                t = ready(act, "gss", k)
                a(nc.scalar.activation(sq[:, 4 + k, :], t[:, 0:T], ACT.Sqrt, bias=eps[:, 0:1], scale=1.0 / 256), used("gss"))
            for tt, (t0, n) in enumerate(TOKS):
                copy("vt", tt, vT[0:n, tt, :], n, slice(0, 512))

            act.wait_ge(sem("lam_sums"), 1)
            a(nc.scalar.activation(lam[:, 2:4], lam[:, 0:2], ACT.Exp), sem("lam_exp"))

            def exps(h):
                for tt, (t0, n) in enumerate(TOKS):
                    for m in range(2):
                        k = 6 * h + 2 * tt + m
                        act.wait_ge(sem("max_ready"), k + 1)
                        t = ready(act, "score", k)
                        if 3 * h + tt >= 2 and m == 0:
                            act.wait_ge(sem("a_ready"), 3 * h + tt - 1)
                        a(nc.scalar.activation(pr[0:n, (3 * h + tt) % 2, m, :], t[0:n, 0:T], ACT.Exp,
                                               bias=stat[0:n, k, 0:1], accum_out=stat[0:n, k, 1:2]), used("score"))

            exps(0)
            for h in range(ATT):
                if h + 1 < ATT:
                    exps(h + 1)
                for kt, (k0, n) in enumerate(TOKS):
                    copy("at", 3 * h + kt, aT[0:n, h % 2, kt, :], n)
            act.wait_ge(used("o"), ATT)
            a(nc.scalar.activation(sq[:, 0:4, :], osb, ACT.Square), sem("act_squares"))
            for k in range(4):
                t = ready(act, "oss", k)
                a(nc.scalar.activation(sq[:, 4 + k, :], t[:, 0:T], ACT.Sqrt, bias=eps[:, 0:1], scale=1.0 / P), used("oss"))

            act.wait_ge(used("wo"), 8)
            square(0, 4)
            root("ss2", 0, D)
            base = NUMBER[("gate", 0)]
            c_gate, c_up = CREDIT["gate"], CREDIT["up"]
            a.credit(used("gate"), c_gate)

            def gate(i, b, first):
                n = base + 4 * (b // 2) + b % 2
                act.wait_ge(sem("tile_ready"), 8 * i + n + 1)
                act.wait_ge(used("up"), 4 * i + b + 1)
                a(nc.scalar.activation(sg[:, b, :], ps[n % 8][:, 0:T], ACT.Silu), used("gate"))

            with act.Fori(0, 5) as i:
                a.loop(i, [(used("gate"), 4)])
                for b in range(4):
                    gate(i, b, False)
                a.end(5)
            for b in range(2):
                gate(5, b, False)

            for k in range(3):
                act.wait_ge(sem("arg_ready"), k + 1)
                a(nc.scalar.activation(harg[0:64, 3, :], harg[0:64, 1, :], ACT.Sin), sem("sin_ready"))
            act.wait_ge(sem("keo_ready"), 2)
            a(nc.scalar.activation(kfb[:, 0:2, :], kfb[:, 0:2, :], ACT.Abs))
            a(nc.scalar.activation(kfb[0:META, 2, :], kfb[0:META, 2, :], ACT.Abs), sem("kabs_ready"))
            for k in range(12):
                ft, half = k // 4, k % 2
                n = TOKS[ft][1]
                dst = KR if k % 4 < 2 else KI
                copy("kspec", k, dst[0:n, ft, 512 * half:512 * half + 512], n, slice(0, 512))

            square(0, 4)
            root("ss3", 0, D)
            a.credit(used("hy"), CREDIT["hy"])
            base = NUMBER[("hy", 0)]
            act.wait_ge(sem("pad_zero"), 1)
            with act.Fori(0, 3) as i:
                a.loop(i, [(used("hy"), 8), (sem("tap0_ready"), 8)])
                for b in range(8):
                    n = base + b
                    act.wait_ge(sem("tile_ready"), 8 * i + n + 1)
                    act.wait_ge(sem("taps_ready"), 8 * i + b + 1)
                    j = 8 * i + b
                    a(nc.scalar.activation(pad[:, b, 1:1 + T], ps[n % 8][:, 0:T], ACT.Identity, bias=par[:, bass.ds(j + C_BIN, 1)]),
                      used("hy"))
                    a(nc.scalar.activation(hyc[:, bass.ds(j, 1), :].rearrange("p a t -> p (a t)"), pad[:, b, 0:T], ACT.Identity,
                                           bias=par[:, bass.ds(j + C_HCB, 1)], scale=par[:, bass.ds(j + C_HCW, 1)]), sem("tap0_ready"))
                a.end(3)
            for k in range(6):
                tt, half = k // 2, k % 2
                n = TOKS[tt][1]
                copy("vx", k, vtok[0:n, tt, 512 * half:512 * half + 512], n, slice(0, 512))

            act.wait_ge(used("ho"), 8)
            square(0, 4, slice(META, T))
            t = ready(act, "ss4", 0)
            a(nc.scalar.activation(rstd[:, 0:SEQ], t[:, 0:SEQ], ACT.Sqrt, bias=eps[:, 0:1], scale=1.0 / D), used("ss4"))
            act.wait_ge(sem("logit_shift"), 1)
            a(nc.scalar.activation(rt[:, 32:48], rt[:, 16:32], ACT.Exp), sem("gate_exp"))
            for k in range(4):
                copy("xk", k, xtk[:, k // 2, 512 * (k % 2):512 * (k % 2) + 512], P, slice(0, 512))
            for k in range(4):
                copy("gt", k, GT[0:CAP, 2 * k:2 * k + 2, :].rearrange("p a b -> p (a b)"), CAP, slice(0, 512))

            def item(i):
                act.wait_ge(sem("gather_ready"), 2 * i + 2)
                a(nc.scalar.activation(xg[:, 4:8, :].rearrange("p a b -> p (a b)"), ps[7][:, 0:4 * CAP], ACT.Copy), sem("xg_act"))
                with act.Fori(0, STAGES // 2) as q:
                    for p in range(2):
                        act.wait_ge(sem("gu_done"), 14 * i + 2 * q + p + 3)
                        nc.scalar.activation(esg[:, p, :], ps[p][:, 0:2 * CAP], ACT.Silu).then_inc(sem("sg_ready"), 1)
                act.wait_ge(sem("ye_ready"), i + 1)
                a(nc.scalar.activation(ye[0:CAP, 512:1024], ps[5][0:CAP, :], ACT.Copy), sem("ye_act"))

            with act.Fori(0, NE) as i:
                a.loop(i, [(sem("xg_act"), 1), (sem("ye_act"), 1)])
                item(i)
                a.end(NE)
            act.wait_ge(sem("later_count"), 1)
            more = act.value_load(tab[0:1, 0:1], min_val=0, max_val=NE)
            with act.If(more > 0):
                for k in range(4):
                    act.wait_ge(sem("later_gt"), k + 1)
                    a(nc.scalar.activation(GT[0:CAP, NE + 2 * k:NE + 2 * k + 2, :].rearrange("p a b -> p (a b)"), ps[2 + k % 2][0:CAP, :],
                                           ACT.Copy), sem("later_gt_used"))
                with act.Fori(0, more) as j:
                    a.loop(j, [(sem("xg_act"), 1), (sem("ye_act"), 1)])
                    item(j + NE)
                    a.end(1)
            act.wait_ge(sem("final_ss"), 1)
            a(nc.scalar.activation(rstd[:, 0:SEQ], ps[0][:, 0:SEQ], ACT.Sqrt, bias=eps[:, 0:1], scale=1.0 / D), sem("final_root"))

        @block.vector
        def _(dve):
            v = Steps(dve, sem("dve_chain"))
            V = nc.vector

            def mult_add(out_, in0, scalar, in1, s=None, op0=ALU.mult, op1=ALU.add):
                v(V.scalar_tensor_tensor(out=out_, in0=in0, scalar=scalar, in1=in1, op0=op0, op1=op1), s)

            def norm(group, col, toks=slice(0, T), s=None, weights=par):
                n = toks.stop - toks.start
                dve.wait_ge(used(group), 1)
                v(V.reciprocal(rstd[:, 0:n], rstd[:, 0:n]))
                for k in range(KT):
                    mult_add(xn[:, k, 0:n], hT[:, k, toks], par[:, col + k:col + k + 1], rstd[:, 0:n], s, ALU.mult, ALU.mult)

            def square(lo, hi, s, toks=slice(0, T)):
                v(V.tensor_tensor(sq[:, lo:hi, toks], hT[:, lo:hi, toks], hT[:, lo:hi, toks], ALU.mult), s)

            v(V.memset(xp, 0.0), sem("xp_zero"))
            V.memset(crd[:, 0:1], 0.0).then_inc(used("up"), CREDIT["up"])
            V.memset(crd[:, 1:2], 0.0).then_inc(sem("taps_ready"), 8)
            v(V.memset(dtw, 0.0))
            dve.wait_ge(used("xin"), 5)
            square(4, 8, sem("dve_squares"))
            norm("ss1", C_NME, s=sem("xn1_ready"))
            dve.wait_ge(sem("dt_in"), 16 * 5)
            v(V.tensor_tensor(lam_in[:, 0:64], lam_in[:, 0:64], lam_in[:, 64:128], ALU.mult))
            v(V.tensor_tensor(lam_in[:, 128:192], lam_in[:, 128:192], lam_in[:, 192:256], ALU.mult))
            v(V.tensor_reduce(lam[:, 0:1], lam_in[:, 0:64], AX.X, ALU.add))
            v(V.tensor_reduce(lam[:, 1:2], lam_in[:, 128:192], AX.X, ALU.add), sem("lam_sums"))
            for odd in range(2):
                r = slice(64 * odd, 64 * odd + 64)
                d2 = d_in[r, :].rearrange("p (w t o) -> p w t o", w=2, o=2)
                v(V.tensor_tensor(dskip[r, :], d2[:, 0, :, odd], d2[:, 1, :, odd], ALU.add))
            for j in range(8):
                dve.wait_ge(used("proj"), j + 1)
                w = lambda k: par[:, C_CW + 8 * k + j:C_CW + 8 * k + j + 1]
                if j >= 2:
                    dve.wait_ge(sem("xbc_ready"), j - 1)
                c = convt[:, j % 2, :]
                v(V.tensor_scalar(c, xp[:, j, 0:T], w(0), par[:, C_CB + j:C_CB + j + 1], ALU.mult, ALU.add))
                for k in range(1, CONV):
                    mult_add(c, xp[:, j, k:k + T], w(k), c, sem("conv_ready") if k == CONV - 1 else None)
            t = ready(dve, "dt", 0)
            v(V.tensor_tensor(dtw[:, 0, 0:16], t[:, 0:16], dt_bias, ALU.add))
            v(V.tensor_tensor(dtw[:, 0, 16:32], t[:, 16:32], dt_bias, ALU.add))
            v(V.tensor_tensor(dtw[0:META, 0, 32:48], t[0:META, 32:48], dt_bias[0:META, :], ALU.add), used("dt"))
            mult_add(dtw[:, 1, :], dtw[:, 0, :], -1.0, dtw[:, 0, :], sem("dt_raw"), ALU.mult, ALU.max)
            dve.wait_ge(sem("dt_log"), 1)
            mult_add(dtw[:, 4, :], dtw[:, 0, :], 0.0, dtw[:, 3, :], sem("dt_ready"), ALU.max, ALU.add)
            for tt in range(3):
                mult_add(dtw[:, 5, 16 * tt:16 * tt + 16], dtw[:, 4, 16 * tt:16 * tt + 16], -1.0, dtw[:, 7, 0:16], sem("a_vec_ready"), ALU.mult, ALU.mult)

            def ssd_out(pair):
                t = ready(dve, "y", pair)
                mult_add(ysb[:, pair, :], xbc[:, pair, :], dskip[:, pair:pair + 1], t[:, 0:T], used("y"))
                v(V.tensor_tensor(ysb[:, pair, :], ysb[:, pair, :], zs[:, pair, :], ALU.mult), sem("yz_ready"))

            dve.wait_ge(sem("table_in"), 32)
            for h in range(HEADS):
                m, wt = M[:, h % 4], W[:, h % 2]
                for tt, (t0, n) in enumerate(TOKS):
                    dve.wait_ge(sem("w1_ready"), 3 * h + tt + 1)
                    mult_add(wt[0:n, tt, :], UF[0:n, tt, :], dtw[0:n, 4, 16 * tt + h:16 * tt + h + 1], W1[0:n, h % 2, tt, :])
                dve.wait_ge(used("row"), 2 * h + 2)
                v(V.tensor_tensor(m[:, 0:2, :], m[:, 0:2, :], RB[:, h % 2, 0:2, :], ALU.add))
                v(V.tensor_tensor(m[0:META, 2, :], m[0:META, 2, :], RB[0:META, h % 2, 2, :], ALU.add), sem("decay_sum"))
                if h == 0:
                    dve.wait_ge(used("cb"), 6)
                g3 = 3 * (h // 4)
                v(V.tensor_tensor(wt[:, 0:2, :], wt[:, 0:2, :], CB[:, g3:g3 + 2, :], ALU.mult))
                v(V.tensor_tensor(wt[0:META, 2, :], wt[0:META, 2, :], CB[0:META, g3 + 2, :], ALU.mult))
                dve.wait_ge(sem("decay_ready"), h + 1)
                v(V.tensor_tensor(m[:, 0:2, :], m[:, 0:2, :], wt[:, 0:2, :], ALU.mult))
                v(V.tensor_tensor(m[0:META, 2, :], m[0:META, 2, :], wt[0:META, 2, :], ALU.mult), sem("m_ready"))
                if h >= 4 and h % 2 == 0:
                    ssd_out((h - 4) // 2)
            for pair in (2, 3):
                ssd_out(pair)
            for j in range(8):
                t = ready(dve, "rope", j)
                v(V.tensor_tensor(ropet[:, 0, :], t[:, 0:T], sinT, ALU.mult), used("rope"))
                v(V.tensor_tensor(ropet[:, 1, :], qk[:, j, :], cosT, ALU.mult))
                v(V.tensor_tensor(qk[:, j, :], ropet[:, 0, :], ropet[:, 1, :], ALU.add), sem("qk_ready"))
            for g in range(2):
                dve.wait_ge(used("gss"), g + 1)
                v(V.reciprocal(sq[:, 4 + g, :], sq[:, 4 + g, :]))
                for k in range(2 * g, 2 * g + 2):
                    mult_add(cat[:, k, :], ysb[:, k, :], par[:, C_SNW + k:C_SNW + k + 1], sq[:, 4 + g, :], sem("cat_ready"), ALU.mult, ALU.mult)
            dve.wait_ge(sem("lam_exp"), 1)
            v(V.tensor_tensor(lam[:, 4:5], lam[:, 3:4], lam[:, 2:3], ALU.subtract))
            v(V.tensor_scalar(lam[:, 4:5], lam[:, 4:5], -LAMBDA_INIT, None, ALU.add))

            def row_max(k):
                n = TOKS[(k % 6) // 2][1]
                t = ready(dve, "score", k)
                v(V.tensor_reduce(stat[0:n, k, 0:1], t[0:n, 0:T], AX.X, ALU.max, negate=True), sem("max_ready"))

            def combine(h, tt):
                n = TOKS[tt][1]
                k = 6 * h + 2 * tt
                dve.wait_ge(used("score"), k + 2)
                v(V.reciprocal(stat[0:n, k:k + 2, 2:3], stat[0:n, k:k + 2, 1:2]))
                v(V.tensor_scalar(stat[0:n, k + 1, 3:4], stat[0:n, k + 1, 2:3], lam[0:n, 4:5], None, ALU.mult))
                pk = pr[0:n, (3 * h + tt) % 2]
                v(V.tensor_scalar(pk[:, 0, :], pk[:, 0, :], stat[0:n, k, 2:3], None, ALU.mult))
                mult_add(at_[0:n, h % 2, tt, :], pk[:, 1, :], stat[0:n, k + 1, 3:4], pk[:, 0, :], sem("a_ready"))

            v(V.tensor_scalar(lam[:, 5:6], par[:, C_SUB:C_SUB + 1], 1.0 - LAMBDA_INIT, None, ALU.mult))

            def softmaxes(h):
                if h >= 2:
                    dve.wait_ge(used("at"), 3 * (h - 1))
                for tt in range(3):
                    row_max(6 * h + 2 * tt)
                    row_max(6 * h + 2 * tt + 1)
                    if tt >= 1:
                        combine(h, tt - 1)
                combine(h, 2)

            softmaxes(0)
            for h in range(ATT):
                if h + 1 < ATT:
                    softmaxes(h + 1)
                t = ready(dve, "o", h)
                v(V.tensor_copy(osb[:, h, :], t[:, 0:T]), used("o"))
            for k in range(4):
                dve.wait_ge(used("oss"), k + 1)
                v(V.reciprocal(sq[:, 4 + k, :], sq[:, 4 + k, :]))
                mult_add(cat[:, 4 + k, :], osb[:, k, :], lam[:, 5:6], sq[:, 4 + k, :], sem("cat_ready"), ALU.mult, ALU.mult)
            for j in range(8):
                t = ready(dve, "wo", j)
                v(V.tensor_tensor(hT[:, j, :], hT[:, j, :], t[:, 0:T], ALU.add), used("wo"))
            square(4, 8, sem("dve_squares"))
            norm("ss2", C_NFE, s=sem("xn2_ready"))
            v.credit(used("up"), CREDIT["up"])
            V.memset(crd[:, 2:3], 0.0).then_inc(used("gate"), CREDIT["gate"])
            base = NUMBER[("up", 0)]

            def up(i, b):
                n = base + 4 * (b // 2) + b % 2
                dve.wait_ge(used("gate"), 4 * i + b + 1 + CREDIT["gate"])
                dve.wait_ge(sem("tile_ready"), 8 * i + n + 1)
                v(V.tensor_tensor(ffh[:, bass.ds(4 * i + b, 1), :].rearrange("p a t -> p (a t)") if not isinstance(i, int) else ffh[:, 4 * i + b, :],
                                  sg[:, b, :], ps[n % 8][:, 0:T], ALU.mult), used("up"))

            with dve.Fori(0, 5) as i:
                v.loop(i, [(used("up"), 4)])
                for b in range(4):
                    up(i, b)
                v.end(5)
            for b in range(2):
                up(5, b)
            for j in range(8):
                t = ready(dve, "down", j)
                v(V.tensor_tensor(hT[:, j, :], hT[:, j, :], t[:, 0:T], ALU.add), used("down"))
            square(4, 8, sem("dve_squares"))

            for k in range(3):
                t = ready(dve, "mlp", k)
                x0, x1, x2 = harg[0:64, 0, :], harg[0:64, 1, :], harg[0:64, 2, :]
                v(V.tensor_scalar(x0, t[0:64, 0:T], par[0:64, C_FV + k:C_FV + k + 1], par[0:64, C_FV + 3 + k:C_FV + 4 + k], ALU.add, ALU.mult), used("mlp"))
                v(V.tensor_scalar(x1, x0, 1.0 / (2.0 * math.pi), ROUND, ALU.mult, ALU.add))
                v(V.tensor_scalar(x1, x1, ROUND, None, ALU.subtract))
                mult_add(x0, x1, -TWO_PI_A, x0)
                mult_add(x2, x1, -TWO_PI_B, x0)
                v(V.tensor_scalar(x1, x2, 3.1415925, -3.1415925, ALU.min, ALU.max), sem("arg_ready"))
            dve.wait_ge(sem("window_in"), 32)
            for k in range(12):
                lt, c = k // 4, k % 4
                n = TOKS[lt][1]
                t = ready(dve, "kt", k)
                v(V.tensor_tensor(kfb[0:n, lt, 512 * c:512 * c + 512], t[0:n, :], win[0:n, lt, 512 * (c % 2):512 * (c % 2) + 512], ALU.mult), used("kt"))
            v(V.memset(kfb[0:1, 0, D:2 * D], 0.0))
            for pp, ts in ((P, slice(0, 2)), (META, slice(2, 3))):
                v(V.tensor_tensor(KE[0:pp, ts, :], kfb[0:pp, ts, 0:D], kfb[0:pp, ts, D:2 * D], ALU.add))
                v(V.tensor_tensor(KO[0:pp, ts, :], kfb[0:pp, ts, 0:D], kfb[0:pp, ts, D:2 * D], ALU.subtract), sem("keo_ready"))
            dve.wait_ge(sem("kabs_ready"), 1)
            for pp, ts in ((P, slice(0, 2)), (META, slice(2, 3))):
                v(V.tensor_tensor(kfb[0:pp, ts, 0:D], kfb[0:pp, ts, 0:D], kfb[0:pp, ts, D:2 * D], ALU.add), sem("kabs_sum"))
            t = ready(dve, "kn", 0)
            v(V.reciprocal(invn, t[:, 0:8]), used("kn"))
            norm("ss3", C_NMO, s=sem("xn3_ready"))
            dve.wait_ge(used("kspec"), 12)
            v(V.memset(pad, 0.0), sem("pad_zero"))
            V.memset(crd[:, 4:5], 0.0).then_inc(used("hy"), CREDIT["hy"])
            v.credit(sem("taps_ready"), 8)
            with dve.Fori(0, 3) as i:
                v.loop(i, [(sem("taps_ready"), 8), (sem("dve_chain"), 8)])
                for b in range(8):
                    j = 8 * i + b
                    dve.wait_ge(sem("tap0_ready"), 8 * i + b + 1)
                    o = hyc[:, bass.ds(j, 1), :].rearrange("p a t -> p (a t)")
                    mult_add(o, pad[:, b, 1:1 + T], par[:, bass.ds(j + C_HCW + 24, 1)], o)
                    mult_add(o, pad[:, b, 2:2 + T], par[:, bass.ds(j + C_HCW + 48, 1)], o, sem("taps_ready"))
                v.end(3)
            v(V.tensor_tensor(hyc[:, 8:16, :], hyc[:, 8:16, :], hyc[:, 0:8, :], ALU.mult), sem("v_ready"))
            for k in range(6):
                ft, half = k // 2, k % 2
                n = TOKS[ft][1]
                c = slice(512 * half, 512 * half + 512)
                if k >= 1:
                    dve.wait_ge(sem("spec_ready"), 2 * k)
                tr = ready(dve, "vspec", 2 * k)
                v(V.tensor_tensor(prod[0:n, 0, :], KR[0:n, ft, c], tr[0:n, :], ALU.mult), sem("prod_ready"))
                v(V.tensor_tensor(prod[0:n, 3, :], KI[0:n, ft, c], tr[0:n, :], ALU.mult), sem("prod_ready"))
                ti = ready(dve, "vspec", 2 * k + 1)
                v(V.tensor_tensor(prod[0:n, 1, :], KI[0:n, ft, c], ti[0:n, :], ALU.mult), sem("prod_ready"))
                v(V.tensor_tensor(prod[0:n, 2, :], KR[0:n, ft, c], ti[0:n, :], ALU.mult), sem("prod_ready"))
            for j in range(8):
                t = ready(dve, "inv", j)
                v(V.tensor_scalar(ytmp[:, 0, :], hyc[:, 8 + j, META:T], par[:, C_SKIP + j:C_SKIP + j + 1], None, ALU.mult))
                mult_add(ytmp[:, 1, :], t[:, 0:SEQ], invn[:, j:j + 1], ytmp[:, 0, :], used("inv"))
                v(V.tensor_tensor(xn[:, j, 0:SEQ], ytmp[:, 1, :], hyc[:, 16 + j, META:T], ALU.mult), sem("yh_ready"))
            v(V.memset(crd[:, 5:6], 0.0), sem("hyena_done"))
            V.memset(crd[:, 6:7], 0.0).then_inc(sem("gu_done"), 2)
            V.memset(crd[:, 7:8], 0.0).then_inc(sem("down_done"), 2)
            for j in range(8):
                t = ready(dve, "ho", j)
                mult_add(hT[:, j, META:T], t[:, 0:SEQ], par[:, C_BOUT + j:C_BOUT + j + 1], hT[:, j, META:T], used("ho"), ALU.add, ALU.add)
            square(4, 8, sem("dve_squares"), slice(META, T))
            norm("ss4", C_NFO, slice(META, T), sem("xn4_ready"))

            lg, sh, ex = rt[:, 0:16], rt[:, 16:32], rt[:, 32:48]
            rank, pick, gatev, posm = rt[:, 48:64], rt[:, 64:80], rt[:, 80:96], rt[:, 96:112]
            m1 = rt[:, 112:128]
            gt_, eq_ = rt[:, 128:256], rt[:, 256:384]
            t = ready(dve, "logit", 0)
            v(V.tensor_copy(lg, t[:, 0:16]), used("logit"))
            for tt in range(2):
                l = lg[:, NE * tt:NE * tt + NE]
                l_f = l.rearrange("p (a f) -> p a f", a=1).to_broadcast([P, NE, NE])
                l_e = l.rearrange("p (e a) -> p e a", a=1).to_broadcast([P, NE, NE])
                gv = gt_[:, 64 * tt:64 * tt + 64].rearrange("p (e f) -> p e f", e=NE)
                ev = eq_[:, 64 * tt:64 * tt + 64].rearrange("p (e f) -> p e f", e=NE)
                v(V.tensor_reduce(m1[:, tt:tt + 1], l, AX.X, ALU.max))
                v(V.tensor_scalar(sh[:, NE * tt:NE * tt + NE], l, m1[:, tt:tt + 1], None, ALU.subtract), sem("logit_shift") if tt == 1 else None)
                v(V.tensor_tensor(gv, l_f, l_e, ALU.is_gt))
                v(V.tensor_tensor(ev, l_f, l_e, ALU.is_equal))
                v(V.tensor_tensor(ev, ev, tri, ALU.mult))
                v(V.tensor_tensor(gv, gv, ev, ALU.add))
                v(V.tensor_reduce(rank[:, NE * tt:NE * tt + NE], gv, AX.X, ALU.add))
            v(V.tensor_scalar(pick, rank, 1.5, None, ALU.is_lt), sem("pick_ready"))
            dve.wait_ge(sem("gate_exp"), 1)
            v(V.tensor_tensor(ex, ex, pick, ALU.mult))
            for tt in range(2):
                e = slice(NE * tt, NE * tt + NE)
                v(V.tensor_reduce(m1[:, 2 + tt:3 + tt], ex[:, e], AX.X, ALU.add))
                v(V.reciprocal(m1[:, 4 + tt:5 + tt], m1[:, 2 + tt:3 + tt]))
                v(V.tensor_scalar(gatev[:, e], ex[:, e], m1[:, 4 + tt:5 + tt], None, ALU.mult))
            t = ready(dve, "pos", 0)
            mult_add(posm, t[:, 0:16], 1.0, pick, None, ALU.add, ALU.mult)
            v(V.tensor_scalar(posm, posm, -1.0, None, ALU.add))
            flag, fpos, ek = rt[:, 384:400], rt[:, 400:416], rt[:, 416:432]
            v(V.tensor_scalar(flag[:, 0:8], t[:, 16:24], float(CAP) + 0.5, None, ALU.is_gt))
            v(V.tensor_scalar(flag[:, 8:16], t[:, 16:24], 2.0 * CAP + 0.5, None, ALU.is_gt), used("pos"))
            v(V.tensor_reduce(tabf[0:1, 0:1], flag[0:1, :], AX.X, ALU.add))
            v(V.tensor_copy(tab[0:1, 0:1], tabf[0:1, 0:1]), sem("later_count"))
            for e in range(NE):
                for tt in range(2):
                    c = NE * tt + e
                    v(V.tensor_scalar(SELG[:, tt, e, :], iota, posm[:, c:c + 1], gatev[:, c:c + 1], ALU.is_equal, ALU.mult), sem("selg_ready"))
            for e in range(NE):
                for tt in range(2):
                    c = NE * tt + e
                    v(V.tensor_scalar(SEL[:, tt, e, :], iota, posm[:, c:c + 1], None, ALU.is_equal), sem("sel_ready"))

            V.memset(crd[:, 8:9], 0.0).then_inc(sem("comb_used"), 4)
            v.credit(sem("comb_used"), 4)

            def item(i):
                dve.wait_ge(sem("gather_ready"), 2 * i + 1)
                V.tensor_copy(xg[:, 0:4, :].rearrange("p a b -> p (a b)"), ps[6][:, 0:4 * CAP]).then_inc(sem("xg_dve"), 1)
                with dve.Fori(0, STAGES // 2) as q:
                    for p in range(2):
                        dve.wait_ge(sem("sg_ready"), 14 * i + 2 * q + p + 1)
                        V.tensor_tensor(eh[:, p, :], esg[:, p, :], ps[p][:, 2 * CAP:4 * CAP], ALU.mult).then_inc(sem("h_ready"), 1)
                dve.wait_ge(sem("ye_ready"), i + 1)
                v(V.tensor_copy(ye[0:CAP, 0:512], ps[4][0:CAP, :]), sem("ye_dve"))
                for c, bank in enumerate((6, 7, 2, 3)):
                    dve.wait_ge(sem("comb_ready"), 4 * i + c + 1)
                    v(V.tensor_tensor(hT[:, 2 * c:2 * c + 2, META:T], hT[:, 2 * c:2 * c + 2, META:T],
                                      ps[bank][:, :].rearrange("p (a b) -> p a b", a=2), ALU.add), sem("comb_used"))

            per = [(sem("ye_dve"), 1), (sem("comb_used"), 4)]
            with dve.Fori(0, NE) as i:
                v.loop(i, per)
                item(i)
                v.end(NE)
            more = dve.value_load(tab[0:1, 0:1], min_val=0, max_val=NE)
            with dve.If(more > 0):
                u = Steps(dve, sem("later_chain"))
                scan = rt[:, 432:448]
                u(V.tensor_tensor_scan(fpos, flag, flag, 0.0, ALU.add, ALU.bypass))
                u(V.tensor_tensor(fpos, fpos, flag, ALU.subtract))
                for k in range(NE):
                    u(V.scalar_tensor_tensor(out=scan, in0=fpos, scalar=float(k), in1=flag, op0=ALU.is_equal, op1=ALU.mult))
                    u(V.tensor_tensor(ek, scan, cand[:, 0, :], ALU.mult))
                    u(V.tensor_reduce(tabf[0:1, 1 + k:2 + k], ek[0:1, :], AX.X, ALU.add))
                    for tt in range(2):
                        for half in range(2):
                            e = slice(NE * half, NE * half + NE)
                            src = slice(NE * tt, NE * tt + NE)
                            u(V.tensor_tensor(ek[:, e], posm[:, src], cand[:, 1, e], ALU.subtract))
                        u(V.tensor_tensor(ek, ek, scan, ALU.mult))
                        u(V.tensor_reduce(m1[:, 8:9], ek, AX.X, ALU.add))
                        for half in range(2):
                            e = slice(NE * half, NE * half + NE)
                            src = slice(NE * tt, NE * tt + NE)
                            u(V.tensor_tensor(ek[:, e], gatev[:, src], scan[:, e], ALU.mult))
                        u(V.tensor_reduce(m1[:, 9:10], ek, AX.X, ALU.add))
                        u(V.tensor_scalar(SEL[:, tt, NE + k, :], iota, m1[:, 8:9], None, ALU.is_equal))
                        u(V.tensor_scalar(SELG[:, tt, NE + k, :], iota, m1[:, 8:9], m1[:, 9:10], ALU.is_equal, ALU.mult), sem("later_sel"))
                u(V.tensor_copy(tab[0:1, 1:1 + NE], tabf[0:1, 1:1 + NE]), sem("later_table"))
                with dve.Fori(0, more) as j:
                    v.loop(j, per)
                    item(j + NE)
                    v.end(1)
            dve.wait_ge(sem("comb_used"), 4 * more + 4 + 4 * NE)
            V.tensor_tensor(sq[:, :, 0:SEQ], hT[:, :, META:T], hT[:, :, META:T], ALU.mult).then_inc(sem("final_squares"), 1)
            dve.wait_ge(sem("final_root"), 1)
            dve.wait_ge(sem("final_squares"), 1)
            f = Steps(dve, sem("final_chain"))
            f(V.reciprocal(rstd[:, 0:SEQ], rstd[:, 0:SEQ]))
            for k in range(KT):
                f(V.scalar_tensor_tensor(out=xn[:, k, 0:SEQ], in0=hT[:, k, META:T], scalar=par[:, C_FIN + k:C_FIN + k + 1],
                                         in1=rstd[:, 0:SEQ], op0=ALU.mult, op1=ALU.mult), sem("final_xn"))
            for k in range(4):
                dve.wait_ge(sem("final_turn"), k + 1)
                f(V.tensor_copy(osb2[:, k // 2, 512 * (k % 2):512 * (k % 2) + 512], ps[1 + k][:, :]), sem("out_ready"))

        @block.tensor
        def _(pe):
            def open_tile(group, k):
                n = NUMBER[(group, k)]
                if n >= 8:
                    g, j = ORDER[n - 8]
                    if g == "vspec":
                        pe.wait_ge(sem("prod_ready"), 2 * j + 2)
                    else:
                        pe.wait_ge(used(g), j + 1 + CREDIT.get(g, 0))
                return ps[n % 8]

            def close(ins):
                ins.then_inc(sem("tile_ready"), 1)

            def mm(o, l, r, start=True, stop=True):
                return nc.tensor.matmul(o, l, r, start=start, stop=stop)

            def turn(o, src, n=P):
                return nc.tensor.transpose(o, src, ident[0:n, 0:n])

            def arrived(n):
                pe.wait_ge(slot_in[n % RING], 16 * (n // RING + 1))

            def linear(group, j0, n, rhs, cols=T):
                arrived(n)
                w = slot(n)
                for j in range(2):
                    o = open_tile(group, j0 + j)
                    for k in range(KT):
                        last = mm(o[:, 0:cols], w[:, k, 128 * j:128 * j + 128], rhs[:, k, 0:cols], k == 0, k == KT - 1)
                    close(last)

            def sum_squares(group, k, lo, hi, cols=slice(0, T)):
                o = open_tile(group, k)
                for q in range(lo, hi):
                    last = mm(o[:, 0:cols.stop - cols.start], ones[:], sq[:, q, cols], q == lo, q == hi - 1)
                close(last)

            pe.wait_ge(sem("ident_in"), 16)
            pe.wait_ge(sem("param_in"), 16 * 25)
            o = open_tile("param", 0)
            turn(o[:, 0:C_A], prow[0:C_A, 0, :], C_A)
            turn(o[:, C_HCW:C_B], prow[0:C_B - P, 1, :], C_B - P)
            close(turn(o[0:64, C_FV:C_FV + 6], prow[0:6, 2, 0:64], 6))
            pe.wait_ge(sem("x_in"), 32)
            for tt in range(2):
                for half in range(2):
                    o = open_tile("xin", 2 * tt + half)
                    for c in range(4):
                        k = 4 * half + c
                        last = turn(o[:, P * c:P * c + P], xtok[:, tt, P * k:P * k + P])
                    close(last)
            o = open_tile("xin", 4)
            for k in range(KT):
                last = turn(o[:, META * k:META * k + META], mtok[0:META, P * k:P * k + P], META)
            close(last)
            pe.wait_ge(sem("pool_consts"), 3)
            pe.wait_ge(sem("act_squares"), 1)
            pe.wait_ge(sem("dve_squares"), 1)
            sum_squares("ss1", 0, 0, KT)
            pe.wait_ge(sem("xn1_ready"), KT)
            for n in range(6):
                linear("proj", 2 * n, n, xn)
            pe.wait_ge(sem("dt_in"), 16 * 5)
            o = open_tile("dt", 0)
            for tt, (t0, n) in enumerate(TOKS):
                for k in range(KT):
                    last = mm(o[0:n, 16 * tt:16 * tt + 16], xn[:, k, t0:t0 + n], wdt[:, k, :], k == 0, k == KT - 1)
            close(last)
            pe.wait_ge(sem("a_vec_ready"), 3)
            pe.wait_ge(sem("table_in"), 32)
            for way, U in enumerate((UF, UB)):
                o = open_tile("cs", way)
                for tt, (t0, n) in enumerate(TOKS):
                    last = mm(o[0:HEADS, 0:T], dtw[0:n, 5, 16 * tt + 8 * way:16 * tt + 8 * way + 8], U[0:n, tt, :], tt == 0, tt == 2)
                close(last)
            o = open_tile("cs", 2)
            for tt, (t0, n) in enumerate(TOKS):
                for way, U in enumerate((UF, UB)):
                    for st, (s0, m) in enumerate(TOKS):
                        last = mm(o[0:n, 16 * tt + 8 * way:16 * tt + 8 * way + 8], U[0:m, st, t0:t0 + n],
                                  dtw[0:m, 5, 16 * st + 8 * way:16 * st + 8 * way + 8], st == 0, st == 2)
            close(last)
            pe.wait_ge(sem("xbc_ready"), 8)
            for tt, (t0, n) in enumerate(TOKS):
                o = open_tile("xs", tt)
                for c in range(4):
                    last = turn(o[0:n, P * c:P * c + P], xbc[:, c, t0:t0 + n])
                close(last)
            for g in range(2):
                for tt, (t0, n) in enumerate(TOKS):
                    o = open_tile("cb", 3 * g + tt)
                    close(mm(o[0:n, 0:T], xbc[:, 4 + g, t0:t0 + n], xbc[:, 6 + g, :]))
            pe.wait_ge(used("cs"), 3)
            pe.wait_ge(used("xs"), 3)
            for s in range(10):
                if s < 8:
                    for way in range(2):
                        o = open_tile("row", 2 * s + way)
                        close(mm(o[:, 0:T], sel8[:, P * s:P * s + P], csr[0:HEADS, way, :]))
                if s < 6:
                    linear("proj", 12 + 2 * s, 6 + s, xn)
                if s >= 3 and s % 2 == 1:
                    pair = (s - 3) // 2
                    o = open_tile("y", pair)
                    for h in (2 * pair, 2 * pair + 1):
                        pe.wait_ge(sem("m_ready"), h + 1)
                        r = 64 * (h % 2)
                        for tt, (t0, n) in enumerate(TOKS):
                            last = mm(o[r:r + 64, 0:T], xT[0:n, tt, 64 * h:64 * h + 64], M[0:n, h % 4, tt, :], tt == 0, tt == 2)
                    close(last)
            pe.wait_ge(used("proj"), 24)
            for j in range(8):
                o = open_tile("rope", j)
                close(mm(o[:, 0:T], perm, qk[:, j, :]))
            pe.wait_ge(sem("act_squares"), 2)
            for g in range(2):
                sum_squares("gss", g, 2 * g, 2 * g + 2)
            for tt, (t0, n) in enumerate(TOKS):
                o = open_tile("vt", tt)
                for c in range(4):
                    last = turn(o[0:n, P * c:P * c + P], vf[:, c, t0:t0 + n])
                close(last)
            pe.wait_ge(sem("qk_ready"), 8)
            pe.wait_ge(used("vt"), 3)

            def scores(h):
                for tt, (t0, n) in enumerate(TOKS):
                    for m in range(2):
                        o = open_tile("score", 6 * h + 2 * tt + m)
                        r = slice(64 * m, 64 * m + 64)
                        close(mm(o[0:n, 0:T], qk[r, h, t0:t0 + n], qk[r, 4 + h, :]))

            scores(0)
            for h in range(ATT):
                if h + 1 < ATT:
                    scores(h + 1)
                pe.wait_ge(sem("a_ready"), 3 * h + 3)
                for kt, (k0, m) in enumerate(TOKS):
                    o = open_tile("at", 3 * h + kt)
                    for tt, (t0, n) in enumerate(TOKS):
                        last = turn(o[0:m, t0:t0 + n], at_[0:n, h % 2, tt, k0:k0 + m], n)
                    close(last)
                o = open_tile("o", h)
                pe.wait_ge(used("at"), 3 * h + 3)
                for kt, (k0, m) in enumerate(TOKS):
                    last = mm(o[:, 0:T], vT[0:m, kt, P * h:P * h + P], aT[0:m, h % 2, kt, :], kt == 0, kt == 2)
                close(last)
            pe.wait_ge(sem("act_squares"), 3)
            for k in range(4):
                sum_squares("oss", k, k, k + 1)
            pe.wait_ge(sem("cat_ready"), 8)
            for b in range(4):
                linear("wo", 2 * b, B_WO + b, cat)
            pe.wait_ge(sem("act_squares"), 4)
            pe.wait_ge(sem("dve_squares"), 2)
            sum_squares("ss2", 0, 0, KT)
            pe.wait_ge(sem("xn2_ready"), KT)
            base = NUMBER[("gate", 0)]
            for n in range(base - 8, base):
                g, j = ORDER[n]
                pe.wait_ge(used(g), j + 1)

            def swiglu_columns(i, c):
                for part in range(2):
                    n = B_FF + 2 * c + part
                    pe.wait_ge(slot_in[n % RING], 16 * (n // RING + 1) + 16 * i)
                    w = slot(n)
                    for j in range(2):
                        pe.wait_ge(used(("gate", "up")[part]), 4 * i + 2 * c + j + 1)
                        o = ps[(base + 4 * c + 2 * part + j) % 8]
                        for k in range(KT):
                            last = mm(o[:, 0:T], w[:, k, P * j:P * j + P], xn[:, k, :], k == 0, k == KT - 1)
                        close(last)

            with pe.Fori(0, 5) as i:
                swiglu_columns(i, 0)
                swiglu_columns(i, 1)
            swiglu_columns(5, 0)
            for b in range(4):
                for half in range(2):
                    n = B_DN + 2 * b + half
                    arrived(n)
                    w = slot(n, 11)
                    if half == 0:
                        o2 = [open_tile("down", 2 * b + j) for j in range(2)]
                        if b == 0:
                            pe.wait_ge(used("up"), FFT + CREDIT["up"])
                    for j in range(2):
                        for k in range(11):
                            last = mm(o2[j][:, 0:T], w[:, k, P * j:P * j + P], ffh[:, 11 * half + k, :],
                                      half == 0 and k == 0, half == 1 and k == 10)
                        if half:
                            close(last)
            pe.wait_ge(sem("filter_in"), 64)
            for k in range(3):
                o = open_tile("mlp", k)
                if k:
                    pe.wait_ge(sem("sin_ready"), k)
                close(mm(o[0:64, 0:T], fw23[:, k - 1, :] if k else fw1[:], harg[0:64, 3, :] if k else zpos[:]))
            pe.wait_ge(sem("sin_ready"), 3)
            pe.wait_ge(sem("window_in"), 32)
            for k in range(12):
                t0, n = TOKS[k // 4]
                o = open_tile("kt", k)
                close(mm(o[0:n, :], harg[0:64, 3, t0:t0 + n], fw4[0:64, 512 * (k % 4):512 * (k % 4) + 512]))
            pe.wait_ge(sem("keo_ready"), 2)
            for k in range(12):
                f0, nf = TOKS[k // 4]
                table, src = (CF, KE) if k % 4 < 2 else (SF, KO)
                o = open_tile("kspec", k)
                for tt, (t0, n) in enumerate(TOKS):
                    last = mm(o[0:nf, :], table[0:n, tt, f0:f0 + nf], src[0:n, tt, 512 * (k % 2):512 * (k % 2) + 512], tt == 0, tt == 2)
                close(last)
            pe.wait_ge(sem("kabs_sum"), 2)
            o = open_tile("kn", 0)
            for c in range(KT):
                for tt, (t0, n) in enumerate(TOKS):
                    last = mm(o[:, c:c + 1], kfb[0:n, tt, P * c:P * c + P], ones[0:n, 0:1], tt == 0, tt == 2)
            close(last)
            pe.wait_ge(sem("act_squares"), 5)
            pe.wait_ge(sem("dve_squares"), 3)
            sum_squares("ss3", 0, 0, KT)
            pe.wait_ge(sem("xn3_ready"), KT)
            base_hy = NUMBER[("hy", 0)]
            for n in range(base_hy - 8, base_hy):
                g, j = ORDER[n]
                pe.wait_ge(used(g), j + 1)
            with pe.Fori(0, 3) as i:
                for b in range(4):
                    n = B_HY + b
                    pe.wait_ge(slot_in[n % RING], 16 * (n // RING + 1) + 16 * i)
                    w = slot(n)
                    for j in range(2):
                        pe.wait_ge(used("hy"), 8 * i + 2 * b + j + 1)
                        o = ps[(base_hy + 2 * b + j) % 8]
                        for k in range(KT):
                            last = mm(o[:, 0:T], w[:, k, P * j:P * j + P], xn[:, k, :], k == 0, k == KT - 1)
                        close(last)
            pe.wait_ge(sem("v_ready"), 1)
            for k in range(6):
                t0, n = TOKS[k // 2]
                o = open_tile("vx", k)
                for c in range(4):
                    last = turn(o[0:n, P * c:P * c + P], hyc[:, 8 + 4 * (k % 2) + c, t0:t0 + n])
                close(last)
            pe.wait_ge(used("vx"), 6)
            for k in range(12):
                f0, nf = TOKS[k // 4]
                half = k // 2 % 2
                o = open_tile("vspec", k)
                for tt, (t0, n) in enumerate(TOKS):
                    last = mm(o[0:nf, :], (CF, SF)[k % 2][0:n, tt, f0:f0 + nf], vtok[0:n, tt, 512 * half:512 * half + 512], tt == 0, tt == 2)
                close(last)
            pe.wait_ge(sem("spec_ready"), 12)
            for j in range(8):
                o = open_tile("inv", j)
                for tt, (f0, nf) in enumerate(TOKS):
                    mm(o[:, 0:SEQ], YR[0:nf, tt, P * j:P * j + P], CI[0:nf, tt, :], tt == 0, False)
                    last = mm(o[:, 0:SEQ], YI[0:nf, tt, P * j:P * j + P], SI[0:nf, tt, :], False, tt == 2)
                close(last)
            pe.wait_ge(sem("yh_ready"), 8)
            for b in range(4):
                linear("ho", 2 * b, B_HO + b, xn, SEQ)
            pe.wait_ge(sem("act_squares"), 6)
            pe.wait_ge(sem("dve_squares"), 4)
            sum_squares("ss4", 0, 0, KT, slice(META, T))
            pe.wait_ge(sem("xn4_ready"), KT)
            pe.wait_ge(sem("router_in"), 16)
            o = open_tile("logit", 0)
            for tt in range(2):
                for k in range(KT):
                    last = mm(o[:, NE * tt:NE * tt + NE], xn[:, k, P * tt:P * tt + P], router[:, k, :], k == 0, k == KT - 1)
            close(last)
            for k in range(4):
                o = open_tile("xk", k)
                for c in range(4):
                    last = turn(o[:, P * c:P * c + P], xn[:, 4 * (k % 2) + c, P * (k // 2):P * (k // 2) + P])
                close(last)
            pe.wait_ge(sem("pick_ready"), 1)
            o = open_tile("pos", 0)
            pick = rt[:, 64:80]
            for tt in range(2):
                for st in range(2):
                    mm(o[:, NE * tt:NE * tt + NE], US[:, st, P * tt:P * tt + P], pick[:, NE * st:NE * st + NE], st == 0, st == 1)
            for st in range(2):
                last = mm(o[:, 16:24], ones[:], pick[:, NE * st:NE * st + NE], st == 0, st == 1)
            close(last)
            for k in range(4):
                o = open_tile("gt", k)
                pe.wait_ge(sem("selg_ready"), 4 * k + 4)
                for e in range(2):
                    for tt in range(2):
                        last = turn(o[0:CAP, SEQ * e + P * tt:SEQ * e + P * tt + P], SELG[:, tt, 2 * k + e, :])
                close(last)

            def item(i):
                pe.wait_ge(sem("comb_used"), 4 * i + 2)
                for d in range(KT):
                    for tt in range(2):
                        last = mm(ps[6 + d // 4][:, CAP * (d % 4):CAP * (d % 4) + CAP], xtk[:, tt, P * d:P * d + P],
                                  SEL[:, tt, bass.ds(i, 1), :].rearrange("p a c -> p (a c)"), tt == 0, tt == 1)
                    if d % 4 == 3:
                        last.then_inc(sem("gather_ready"), 1)
                pe.wait_ge(sem("xg_dve"), i + 1)
                pe.wait_ge(sem("xg_act"), i + 1)
                for bank in (4, 5):
                    nc.tensor.matmul(ps[bank][0:CAP, :], zero16[:, 0:CAP], zero16[:], start=True, stop=False)
                with pe.Fori(0, STAGES // 2) as q:
                    for p in range(2):
                        pe.wait_ge(sem(f"gu_in{p}"), 32 * (7 * i + q + 1))
                        for part in range(2):
                            w = ering[:, p, 2048 * part:2048 * part + 2048].rearrange("p (k n) -> p k n", k=KT)
                            for j in range(2):
                                c = CAP * (2 * part + j)
                                for k in range(KT):
                                    last = mm(ps[p][:, c:c + CAP], w[:, k, P * j:P * j + P], xg[:, k, :], k == 0, k == KT - 1)
                        last.then_inc(sem("gu_done"), 1)
                    for p in range(2):
                        pe.wait_ge(sem(f"d_in{p}"), 16 * (7 * i + q + 1))
                        pe.wait_ge(sem("h_ready"), 14 * i + 2 * q + p + 1)
                        w = ering[:, p, 4096:6144].rearrange("p (k n) -> p k n", k=2)
                        for j in range(2):
                            for half in range(2):
                                last = nc.tensor.matmul(ps[4 + half][0:CAP, :], eh[:, p, CAP * j:CAP * j + CAP],
                                                        w[:, j, 512 * half:512 * half + 512], start=False, stop=False)
                        last.then_inc(sem("down_done"), 1)
                for bank in (4, 5):
                    last = nc.tensor.matmul(ps[bank][0:CAP, :], zero16[:, 0:CAP], zero16[:], start=False, stop=True)
                last.then_inc(sem("ye_ready"), 1)
                pe.wait_ge(sem("ye_dve"), i + 1)
                pe.wait_ge(sem("ye_act"), i + 1)
                pe.wait_ge(sem("comb_used"), 4 * i + 4)
                for c, bank in enumerate((6, 7, 2, 3)):
                    for d in range(2):
                        last = mm(ps[bank][:, SEQ * d:SEQ * d + SEQ], ye[0:CAP, P * (2 * c + d):P * (2 * c + d) + P],
                                  GT[0:CAP, bass.ds(i, 1), :].rearrange("p a t -> p (a t)"))
                    last.then_inc(sem("comb_ready"), 1)

            pe.wait_ge(used("logit"), 1)
            pe.wait_ge(used("pos"), 1)
            pe.wait_ge(used("xk"), 4)
            pe.wait_ge(used("gt"), 4)
            pe.wait_ge(sem("sel_ready"), 2 * NE)
            with pe.Fori(0, NE) as i:
                item(i)
            pe.wait_ge(sem("later_count"), 1)
            more = pe.value_load(tab[0:1, 0:1], min_val=0, max_val=NE)
            with pe.If(more > 0):
                pe.wait_ge(sem("comb_used"), 4 * NE + 4)
                for k in range(4):
                    pe.wait_ge(sem("later_sel"), 4 * k + 4)
                    if k >= 2:
                        pe.wait_ge(sem("later_gt_used"), k - 1)
                    for e in range(2):
                        for tt in range(2):
                            last = turn(ps[2 + k % 2][0:CAP, SEQ * e + P * tt:SEQ * e + P * tt + P], SELG[:, tt, NE + 2 * k + e, :])
                    last.then_inc(sem("later_gt"), 1)
                pe.wait_ge(sem("later_gt_used"), 4)
                with pe.Fori(0, more) as j:
                    item(j + NE)
            pe.wait_ge(sem("final_squares"), 1)
            for k in range(KT):
                last = mm(ps[0][:, 0:SEQ], ones[:], sq[:, k, 0:SEQ], k == 0, k == KT - 1)
            last.then_inc(sem("final_ss"), 1)
            pe.wait_ge(sem("final_xn"), KT)
            for k in range(4):
                for c in range(4):
                    last = turn(ps[1 + k][:, P * c:P * c + P], xn[:, 4 * (k % 2) + c, P * (k // 2):P * (k // 2) + P])
                last.then_inc(sem("final_turn"), 1)


_INS = ["x", "meta_tokens", "norm_mix_even", "w_in_ab", "ssd_conv_w", "ssd_conv_b", "ssd_a_log", "ssd_dt_bias", "ssd_d",
        "ssd_norm_w", "diff_lambda", "diff_subln_w", "w_out_ab", "norm_ffn_even", "ffn_w_gate", "ffn_w_up", "ffn_w_down",
        "norm_mix_odd", "hy_w_in", "hy_b_in", "hy_conv_w", "hy_conv_b", "hy_f_w1", "hy_f_b1", "hy_f_w2", "hy_f_b2",
        "hy_f_w3", "hy_f_b3", "hy_f_w4", "hy_f_freq", "hy_skip", "hy_w_out", "hy_b_out", "norm_ffn_odd", "moe_router",
        "moe_w_gate", "moe_w_up", "moe_w_down", "final_norm"]


def kernel(**inputs):
    import numpy as _np
    import concourse.bacc as _bacc
    from concourse import mybir as _mybir
    from concourse.bass_utils import run_bass_kernel_spmd as _run

    nc = _bacc.Bacc("TRN2", target_bir_lowering=False, num_devices=1)
    arrays, args = {}, {}
    given = {name: _np.ascontiguousarray(inputs[name]) for name in _INS}
    for name, a in list(given.items()) + list(shape_constants().items()):
        arrays[f"in_{name}_dram"] = a
        args[name] = nc.dram_tensor(f"in_{name}_dram", a.shape, _mybir.dt.from_np(a.dtype), kind="ExternalInput").ap()
    out = nc.dram_tensor("out_0_dram", (1, SEQ, D), _mybir.dt.float32, kind="ExternalOutput").ap()
    trunk(nc, args, out)
    r = _run(nc, [arrays], core_ids=[0])
    return r.results[0]["out_0_dram"]
```

```python
from contextlib import ExitStack
import math

import numpy as np

import concourse.bass as bass
from concourse import mybir

F32 = mybir.dt.float32
F32R = mybir.dt.float32r
BF16 = mybir.dt.bfloat16
I32 = mybir.dt.int32
ALU = mybir.AluOpType
ACT = mybir.ActivationFunctionType
AX = mybir.AxisListType

P = 128
D = 1024
KT = D // P
SEQ = 256
META = 16
T = SEQ + META
TOKS = [(0, P), (P, P), (2 * P, T - 2 * P)]
EPS = 1e-5
HEADS = 8
CONV = 5
ATT = 4
FF = 2816
FFT = FF // P
FEXP = 3584
NE = 8
HY = 3 * D
SHORT = 3
RING = 4
SLOT = 11 * 256
CAP = 128
STAGES = FEXP // 256
LATER = 2 * SEQ // (CAP + 1)
ITEMS = NE + LATER
LAMBDA_INIT = 0.8 - 0.6 * math.exp(-0.3 * 0)
TWO_PI_A = 6.28125
TWO_PI_B = 2.0 * math.pi - TWO_PI_A
ROUND = 12582912.0

C_NME, C_CW, C_CB, C_SNW, C_SUB, C_NFE, C_NMO, C_BIN, C_SKIP, C_BOUT, C_A = 0, 8, 48, 56, 60, 61, 69, 77, 101, 109, 117
C_HCW, C_HCB, C_NFO, C_FIN, C_B = 128, 200, 224, 232, 240
C_FV = 256

K_SIZES = [("ident", P), ("perm", P), ("cos", T), ("sin", T), ("uf", 3 * T), ("ub", 3 * T), ("cf", 3 * T), ("sf", 3 * T),
           ("ci", 3 * SEQ), ("si", 3 * SEQ), ("us", 2 * SEQ), ("iota", CAP), ("tri", NE * NE),
           ("nth", LATER * NE), ("expert", LATER * NE)]
K_AT = {}
_at = 0
for _name, _n in K_SIZES:
    K_AT[_name] = (_at, _n)
    _at += _n
K_ALL = _at
K_FIRST = K_AT["uf"][0]


def shape_constants():
    f32 = np.float32
    c = np.zeros((P, K_ALL), f32)

    def put(name, a):
        at, n = K_AT[name]
        c[:a.shape[0], at:at + n] = a.reshape(a.shape[0], n)

    def tiles(a):
        out = np.zeros((3, P) + a.shape[1:], f32)
        out.reshape((3 * P,) + a.shape[1:])[:a.shape[0]] = a
        return out.transpose(1, 0, 2)

    put("ident", np.eye(P, dtype=f32))
    perm = np.zeros((P, P), f32)
    cos = np.ones((P, T), f32)
    sin = np.zeros((P, T), f32)
    pos = np.arange(T, dtype=f32)
    inv = (f32(500000.0) ** (-np.arange(0, 16, 2, dtype=f32) / f32(16))).astype(f32)
    ang = pos[:, None] * inv[None, :]
    for base in (0, 64):
        for i in range(8):
            perm[base + 8 + i, base + i] = -1.0
            perm[base + i, base + 8 + i] = 1.0
            cos[base + i] = cos[base + 8 + i] = np.cos(ang[:, i])
            sin[base + i] = sin[base + 8 + i] = np.sin(ang[:, i])
    put("perm", perm)
    put("cos", cos)
    put("sin", sin)
    j, i = np.arange(T)[:, None], np.arange(T)[None, :]
    put("uf", tiles((j <= i).astype(f32)))
    put("ub", tiles((j >= i).astype(f32)))
    w = 2.0 * np.pi * ((np.arange(T)[None, :] + 0.5) * np.arange(T)[:, None]) / (2 * T)
    put("cf", tiles(np.cos(w).astype(f32)))
    put("sf", tiles(np.sin(w).astype(f32)))
    put("ci", tiles((np.cos(w[META:]).T / T).astype(f32)))
    put("si", tiles((np.sin(w[META:]).T / T).astype(f32)))
    us = (np.arange(SEQ)[:, None] < np.arange(SEQ)[None, :]).astype(f32)
    put("us", us.reshape(2, P, SEQ).transpose(1, 0, 2))
    put("iota", np.tile(np.arange(CAP, dtype=f32), (P, 1)))
    put("tri", np.tile((np.arange(NE)[:, None] > np.arange(NE)[None, :]).astype(f32).reshape(1, -1), (P, 1)))
    put("nth", np.tile(np.repeat(np.arange(LATER), NE).astype(f32), (P, 1)))
    put("expert", np.tile(np.tile(np.arange(NE), LATER).astype(f32), (P, 1)))
    sel8 = np.repeat(np.eye(HEADS, dtype=f32), P, axis=1)
    t = pos / f32(T - 1)
    bands = np.linspace(1e-4, 15, 16, dtype=f32)
    ang = (f32(2.0 * math.pi) * pos / f32(T))[:, None] * bands[None, :]
    zpos = np.ascontiguousarray(np.concatenate([t[:, None], np.cos(ang), -np.sin(ang)], axis=-1).T.astype(f32))
    lo, hi = math.log(1e-2) / 1.5, math.log(1e-2) / 0.3
    deltas = np.abs(np.linspace(lo, hi, D, dtype=f32))
    window = (np.exp(-t[:, None] * deltas[None, :]) + f32(0.05)).astype(f32)
    return {"k_table": c, "k_sel8": sel8, "k_zpos": zpos, "k_window": np.ascontiguousarray(tiles(window))}


class Steps:

    def __init__(self, eng, chain):
        self.eng, self.chain, self.count, self.i, self.per = eng, chain, {}, None, {}

    def __call__(self, ins, sem=None):
        sem = self.chain if sem is None else sem
        ins.then_inc(sem, 1)
        n = self.count[id(sem)] = self.count.get(id(sem), 0) + 1
        self.eng.wait_ge(sem, n if self.i is None or id(sem) not in self.per else self.per[id(sem)] * self.i + n)

    def credit(self, sem, n):
        self.count[id(sem)] = self.count.get(id(sem), 0) + n

    def loop(self, i, per):
        self.i, self.per = i, {id(s): k for s, k in per}
        self.start = dict(self.count)

    def end(self, times):
        for s, k in self.per.items():
            assert self.count.get(s, 0) - self.start.get(s, 0) == k, (self.count.get(s, 0), self.start.get(s, 0), k)
            self.count[s] = self.start.get(s, 0) + k * times
        self.i = None


def tile_order():
    order = []

    def add(group, first, n=1):
        order.extend((group, k) for k in range(first, first + n))

    add("xin", 0, 5)
    add("param", 0)
    add("ss1", 0)
    add("proj", 0, 12)
    add("dt", 0)
    add("cs", 0, 3)
    add("xs", 0, 3)
    add("cb", 0, 6)
    for s in range(10):
        if s < 8:
            add("row", 2 * s, 2)
        if s < 6:
            add("proj", 12 + 2 * s, 2)
        if s >= 3 and s % 2 == 1:
            add("y", (s - 3) // 2)
    add("rope", 0, 8)
    add("gss", 0, 2)
    add("vt", 0, 3)
    add("score", 0, 6)
    for h in range(ATT):
        if h + 1 < ATT:
            add("score", 6 * h + 6, 6)
        add("at", 3 * h, 3)
        add("o", h)
    add("oss", 0, 4)
    add("mlp", 0)
    add("wo", 0, 8)
    add("ss2", 0)
    add("mlp", 1)
    for b in range(FFT // 2):
        add("gate", 2 * b, 2)
        add("up", 2 * b, 2)
    add("mlp", 2)
    add("down", 0, 8)
    add("ss3", 0)
    add("kt", 0, 12)
    add("kspec", 0, 12)
    add("kn", 0)
    add("hy", 0, 24)
    add("vx", 0, 6)
    add("vspec", 0, 12)
    add("inv", 0, 8)
    add("ho", 0, 8)
    add("ss4", 0)
    add("logit", 0)
    add("xk", 0, 4)
    add("pos", 0)
    return order


ORDER = tile_order()
NUMBER = {key: n for n, key in enumerate(ORDER)}
CREDIT = {"hy": 8, "gate": 4, "up": 4}


def trunk(nc, A, out):
    ctx = ExitStack()
    with ctx:
        sems = {}

        def sem(name):
            if name not in sems:
                sems[name] = ctx.enter_context(nc.semaphore(name))
            return sems[name]

        def sb(name, shape, dt=F32):
            return ctx.enter_context(nc.sbuf_tensor(name, shape, dt))

        ps = [ctx.enter_context(nc.psum_tensor(f"ps{i}", [P, 512], F32)) for i in range(8)]

        hT = sb("hT", [P, KT, T])
        xn = sb("xn", [P, KT, T])
        sq = sb("sq", [P, KT, T])
        rstd = sb("rstd", [P, T])
        ktab = sb("ktab", [P, K_ALL])
        sel8 = sb("sel8", [HEADS, HEADS * P])
        zpos = sb("zpos", [33, T])
        prow = sb("prow", [P, 3, P])
        par = sb("par", [P, 264])
        ones = sb("ones", [P, P])
        eps = sb("eps", [P, 1])
        bcast = sb("bcast", [P, 16 + 16 + 256 + 16 + 4])
        lam = sb("lam", [P, 8])
        wdt = sb("wdt", [P, KT, 16])
        fw1 = sb("fw1", [33, 64])
        fw23 = sb("fw23", [64, 2, 64])
        router = sb("router", [P, KT, NE])
        crd = sb("crd", [P, 16])
        zero16 = sb("zero16", [P, 512], BF16)
        tabf = sb("tabf", [1, 16])
        tab = sb("tab", [1, 16], I32)
        arena_n = 25344
        with ExitStack() as early:
            arena = early.enter_context(nc.sbuf_tensor("arena", [P, arena_n], F32))
            ring = early.enter_context(nc.sbuf_tensor("ring", [P, RING, SLOT], F32))

        def overlay(name, at, *dims):
            with ExitStack() as early:
                if at:
                    early.enter_context(nc.sbuf_tensor(name + "_at", [P, at], F32))
                return early.enter_context(nc.sbuf_tensor(name, [P] + list(dims), F32R))

        ring_hi, ring_lo = overlay("ring_hi", 13600, 2, SLOT), overlay("ring_lo", arena_n, RING, SLOT)
        ffh_hi, ffh_lo = overlay("ffh_hi", 0, FFT, T), overlay("ffh_lo", 5984, FFT, T)
        xn_hi, xn_lo = overlay("xn_hi", 19232, KT, T), overlay("xn_lo", 21408, KT, T)
        with ExitStack() as early:
            raw = early.enter_context(nc.sbuf_tensor("raw", [P, 2, 3, 2048], F32))
        w_lo = sb("w_lo", [P, 2, 3, 2048], F32R)
        w_hi = sb("w_hi", [P, 2, 3, 2048], F32R)
        xg_hi = sb("xg_hi", [P, KT, CAP], F32R)
        xg_lo = sb("xg_lo", [P, KT, CAP], F32R)
        eh_hi = sb("eh_hi", [P, 2, 2, CAP], F32R)
        eh_lo = sb("eh_lo", [P, 2, 2, CAP], F32R)
        xtk = sb("xtk", [P, 2, D])
        ye = sb("ye", [P, D])
        esg = sb("esg", [P, 2, 256])
        eh = sb("eh", [P, 2, 256])
        SEL = sb("SEL", [P, 2, CAP])
        SELG = sb("SELG", [P, 2, CAP])
        GT = sb("GT", [P, SEQ])
        rt = sb("rt", [P, 1024])
        osb2 = sb("osb2", [P, 2, D])

        def const(name, *dims):
            at, n = K_AT[name]
            a = ktab[:, at:at + n]
            return a.rearrange("p (a b) -> p a b", a=dims[0]) if dims else a

        ident, perm, cosT, sinT = const("ident"), const("perm"), const("cos"), const("sin")
        UF, UB, CF, SF = (const(n, 3) for n in ("uf", "ub", "cf", "sf"))
        CI, SI, US = const("ci", 3), const("si", 3), const("us", 2)
        iota, tri, nth, expert = const("iota"), const("tri", NE), const("nth", LATER), const("expert", LATER)
        dt_bias, a_log, lam_in = bcast[:, 0:16], bcast[:, 16:32], bcast[:, 32:288]
        d_in, dskip = bcast[:, 288:304], bcast[:, 304:308]

        def area(at, a, b=None, c=None):
            n = a * (b or 1) * (c or 1)
            assert at + n <= arena_n, (at, n)
            v = arena[:, at:at + n]
            if c:
                return v.rearrange("p (a b c) -> p a b c", a=a, b=b)
            return v.rearrange("p (a b) -> p a b", a=a) if b else v

        xp = area(0, 8, T + 4)
        xbc = area(2208, 8, T)
        zs = area(4384, 4, T)
        qk = area(5472, 8, T)
        vf = area(7648, 4, T)
        xT = area(8736, 3, 512)
        vT = area(0, 3, 512)
        CB = area(10272, 6, T)
        M = area(11904, 4, 3, T)
        RB = area(15168, 2, 3, T)
        W = area(16800, 2, 3, T)
        W1 = area(18432, 2, 3, T)
        cat = area(20064, 8, T)
        ysb = area(22240, 4, T)
        dtw = area(23328, 8, 48)
        csr = area(23712, 2, T)
        convt = area(24256, 2, T)
        ropet = area(24800, 2, T)
        xtok = area(11904, 2, D)
        mtok = area(13952, D)
        pr = area(11904, 2, 2, T)
        at_ = area(12992, 2, 3, T)
        aT = area(14624, 2, 3, T)
        osb = area(16256, 4, T)
        stat = area(17344, 24, 4)
        sg = area(11968, 4, T)
        ffp = area(13056, 2, T)
        KR = area(0, 3, D)
        KI = area(3072, 3, D)
        kfb = area(6144, 3, 2 * D)
        KE = area(12288, 3, D)
        KO = area(15360, 3, D)
        win = area(19232, 3, D)
        fw4 = xn[:].rearrange("p k t -> p (k t)")[:, 0:2 * D]
        harg = area(24256, 4, T)
        hyc = area(6144, 24, T)
        pad = area(12672, 8, T + 2)
        vtok = area(14864, 3, D)
        YR = area(17936, 3, D)
        YI = area(21008, 3, D)
        prod = area(12672, 4, 512)
        invn = area(24080, 8)
        ytmp = area(24088, 2, SEQ)
        def ready(eng, group, k):
            n = NUMBER[(group, k)]
            eng.wait_ge(sem("tile_ready"), n + 1)
            return ps[n % 8]

        def used(group):
            return sem("used_" + group)

        block = ctx.enter_context(nc.Block())

        w_in = A["w_in_ab"][0].rearrange("(k p) n -> p k n", p=P)
        stream = []
        for c in [512 + 256 * b for b in range(4)] + [0, 256] + [1552 + 256 * b for b in range(6)]:
            stream.append((w_in[:, :, c:c + 256], KT))
        w_out = A["w_out_ab"][0].rearrange("(k p) n -> p k n", p=P)
        for b in range(4):
            stream.append((w_out[:, :, 256 * b:256 * b + 256], KT))
        wg0 = A["ffn_w_gate"][0].rearrange("(k p) n -> p k n", p=P)
        wu0 = A["ffn_w_up"][0].rearrange("(k p) n -> p k n", p=P)
        for b in range(FFT // 2):
            stream.append((wg0[:, :, 256 * b:256 * b + 256], KT))
            stream.append((wu0[:, :, 256 * b:256 * b + 256], KT))
        wd0 = A["ffn_w_down"][0].rearrange("(k p) n -> p k n", p=P)
        for b in range(4):
            for half in range(2):
                stream.append((wd0[:, 11 * half:11 * half + 11, 256 * b:256 * b + 256], 11))
        hwi = A["hy_w_in"][0].rearrange("(k p) n -> p k n", p=P)
        for c in [D + 256 * b for b in range(8)] + [256 * b for b in range(4)]:
            stream.append((hwi[:, :, c:c + 256], KT))
        hwo = A["hy_w_out"][0].rearrange("(k p) n -> p k n", p=P)
        for b in range(4):
            stream.append((hwo[:, :, 256 * b:256 * b + 256], KT))
        B_WO, B_FF, B_DN, B_HY, B_HO = 12, 16, 38, 46, 58

        def last_tile(n):
            if n < B_WO:
                return ("proj", 2 * n + 1)
            if n < B_FF:
                return ("wo", 2 * (n - B_WO) + 1)
            if n < B_DN:
                b = n - B_FF
                return ("up" if b % 2 else "gate", b // 2 * 2 + 1)
            if n < B_HY:
                return ("down", (n - B_DN) // 2 * 2 + (n - B_DN) % 2)
            return ("hy", 2 * (n - B_HY) + 1) if n < B_HO else ("ho", 2 * (n - B_HO) + 1)

        slot_in = [sem(f"slot{i}_in") for i in range(RING)]

        def slot(n, k=KT):
            return ring[:, n % RING, 0:k * 256].rearrange("p (k n) -> p k n", k=k)

        moe = {n: A[n] for n in ("moe_w_gate", "moe_w_up", "moe_w_down")}

        @block.sync
        def _(sp):
            sp.wait_ge(sem("x_in"), 32)
            sp.wait_ge(sem("param_in"), 16 * 25)
            for n, (src, k) in enumerate(stream):
                if n >= RING:
                    sp.wait_ge(sem("tile_ready"), NUMBER[last_tile(n - RING)] + 1)
                if n == B_DN + 4:
                    sp.dma_start(win, A["k_window"]).then_inc(sem("window_in"), 16)
                    sp.wait_ge(sem("xn2_ready"), KT)
                    sp.dma_start(fw4[0:64, :], A["hy_f_w4"][0]).then_inc(sem("window_in"), 16)
                sp.dma_start(slot(n, k), src).then_inc(slot_in[n % RING], 16)
            sp.wait_ge(sem("hyena_done"), 1)

            def load(part, i, e, q, p, wait):
                if wait:
                    sp.wait_ge(sem(f"{part}_used"), 14 * i + 2 * q + p - 1)
                c = bass.ds(512 * q + 256 * p, 256)
                name = {"g": "moe_w_gate", "u": "moe_w_up", "d": "moe_w_down"}[part]
                src = moe[name][0, bass.ds(e, 1), c, :] if part == "d" else moe[name][0, bass.ds(e, 1), :, c]
                at = "gud".index(part)
                dst = raw[:, p, at, :].rearrange("p (k n) -> p k n", k=2 if part == "d" else KT)
                sp.dma_start(dst, src.rearrange("e (k p) n -> p (e k) n", p=P)).then_inc(sem(f"{part}_in{p}"), 16)

            def item(i, e, first=False):
                for p in range(2):
                    load("g", i, e, 0, p, not first)
                    load("u", i, e, 0, p, not first)
                load("d", i, e, 0, 0, not first)
                load("g", i, e, 1, 0, True)
                load("u", i, e, 1, 0, True)
                load("d", i, e, 0, 1, not first)
                load("g", i, e, 1, 1, True)
                load("u", i, e, 1, 1, True)
                load("d", i, e, 1, 0, True)
                with sp.Fori(0, STAGES // 2 - 2) as q:
                    load("g", i, e, q + 2, 0, True)
                    load("u", i, e, q + 2, 0, True)
                    load("d", i, e, q + 1, 1, True)
                    load("g", i, e, q + 2, 1, True)
                    load("u", i, e, q + 2, 1, True)
                    load("d", i, e, q + 2, 0, True)
                load("d", i, e, STAGES // 2 - 1, 1, True)

            item(0, 0, True)
            with sp.Fori(1, NE) as i:
                item(i, i)
            sp.wait_ge(sem("later_table"), 1)
            more = sp.value_load(tab[0:1, 0:1], min_val=0, max_val=LATER)
            with sp.If(more > 0):
                with sp.Fori(0, more) as j:
                    e = sp.value_load(tab[0:1, bass.ds(j + 1, 1)], min_val=0, max_val=NE - 1)
                    item(j + NE, e)
            for tt in range(2):
                sp.wait_ge(sem("out_ready"), 2 * tt + 2)
                sp.dma_start(out[0, tt * P:(tt + 1) * P, :], osb2[:, tt, :]).then_inc(sem("out_done"), 16)
            sp.wait_ge(sem("out_done"), 32)

        @block.gpsimd
        def _(pool):
            g = Steps(pool, sem("pool_chain"))
            g(nc.gpsimd.memset(ones[:], 1.0), sem("pool_consts"))
            g(nc.gpsimd.memset(eps[:], EPS), sem("pool_consts"))
            g(nc.gpsimd.memset(zero16[:], 0.0), sem("pool_consts"))
            pool.wait_ge(sem("table_in"), 32)
            for h in range(HEADS):
                pool.wait_ge(sem("dt_ready"), 1)
                if h >= 2:
                    pool.wait_ge(sem("m_ready"), h - 1)
                for tt, (t0, n) in enumerate(TOKS):
                    g(nc.gpsimd.tensor_scalar(W1[0:n, h % 2, tt, :], UB[0:n, tt, :], dtw[0:n, 4, 16 * tt + 8 + h:16 * tt + 9 + h],
                                              None, ALU.mult), sem("w1_ready"))
            for k in range(6):
                n = TOKS[k // 2][1]
                c = slice(512 * (k % 2), 512 * (k % 2) + 512)
                pool.wait_ge(sem("prod_ready"), 4 * k + 4)
                g(nc.gpsimd.tensor_tensor(YR[0:n, k // 2, c], prod[0:n, 0, :], prod[0:n, 1, :], ALU.subtract), sem("spec_ready"))
                g(nc.gpsimd.tensor_tensor(YI[0:n, k // 2, c], prod[0:n, 2, :], prod[0:n, 3, :], ALU.add), sem("spec_ready"))

        @block.scalar
        def _(act):
            a = Steps(act, sem("act_chain"))

            act.dma_start(ktab[:, 0:K_FIRST], A["k_table"][:, 0:K_FIRST]).then_inc(sem("ident_in"), 16)
            act.dma_start(xtok, A["x"][0].rearrange("(t p) d -> p t d", p=P)).then_inc(sem("x_in"), 16)
            act.dma_start(mtok[0:META, :], A["meta_tokens"]).then_inc(sem("x_in"), 16)
            rows = [(0, C_NME, A["norm_mix_even"].rearrange("e (t p) -> (e t) p", p=P)),
                    (0, C_CW, A["ssd_conv_w"].rearrange("e k (t p) -> (e k t) p", p=P)),
                    (0, C_CB, A["ssd_conv_b"].rearrange("e (t p) -> (e t) p", p=P)),
                    (0, C_SNW, A["ssd_norm_w"].rearrange("e (t p) -> (e t) p", p=P)),
                    (0, C_SUB, A["diff_subln_w"]),
                    (0, C_NFE, A["norm_ffn_even"].rearrange("e (t p) -> (e t) p", p=P)),
                    (0, C_NMO, A["norm_mix_odd"].rearrange("e (t p) -> (e t) p", p=P)),
                    (0, C_BIN, A["hy_b_in"][:, D:].rearrange("e (t p) -> (e t) p", p=P)),
                    (0, C_BIN + 16, A["hy_b_in"][:, 0:D].rearrange("e (t p) -> (e t) p", p=P)),
                    (0, C_SKIP, A["hy_skip"].rearrange("e (t p) -> (e t) p", p=P)),
                    (0, C_BOUT, A["hy_b_out"].rearrange("e (t p) -> (e t) p", p=P)),
                    (1, C_HCB - P, A["hy_conv_b"][:, D:].rearrange("e (t p) -> (e t) p", p=P)),
                    (1, C_HCB - P + 16, A["hy_conv_b"][:, 0:D].rearrange("e (t p) -> (e t) p", p=P)),
                    (1, C_NFO - P, A["norm_ffn_odd"].rearrange("e (t p) -> (e t) p", p=P)),
                    (1, C_FIN - P, A["final_norm"].rearrange("(t p) -> t p", p=P))]
            for k in range(SHORT):
                rows.append((1, 24 * k, A["hy_conv_w"][0, k:k + 1, D:].rearrange("e (t p) -> (e t) p", p=P)))
                rows.append((1, 24 * k + 16, A["hy_conv_w"][0, k:k + 1, 0:D].rearrange("e (t p) -> (e t) p", p=P)))
            for which, at, src in rows:
                act.dma_start(prow[at:at + src.shape[0], which, :], src).then_inc(sem("param_in"), 16)
            for k, name in enumerate(("hy_f_b1", "hy_f_b2", "hy_f_b3")):
                act.dma_start(prow[k:k + 1, 2, 0:64], A[name]).then_inc(sem("param_in"), 16)
            act.dma_start(prow[3:6, 2, 0:64], A["hy_f_freq"][0]).then_inc(sem("param_in"), 16)
            assert len(rows) + 4 == 25
            act.dma_start(wdt[:], w_in[:, :, 1536:1552]).then_inc(sem("dt_in"), 16)
            act.dma_start(dt_bias, A["ssd_dt_bias"].rearrange("e a h -> e (a h)").partition_broadcast(P)).then_inc(sem("dt_in"), 16)
            act.dma_start(a_log, A["ssd_a_log"].rearrange("e a h -> e (a h)").partition_broadcast(P)).then_inc(sem("dt_in"), 16)
            act.dma_start(lam_in, A["diff_lambda"].rearrange("e a h -> e (a h)").partition_broadcast(P)).then_inc(sem("dt_in"), 16)
            act.dma_start(d_in, A["ssd_d"].rearrange("e a h -> e (a h)").partition_broadcast(P)).then_inc(sem("dt_in"), 16)
            act.dma_start(ktab[:, K_FIRST:], A["k_table"][:, K_FIRST:]).then_inc(sem("table_in"), 16)
            act.dma_start(sel8[:], A["k_sel8"]).then_inc(sem("table_in"), 16)
            act.dma_start(zpos[:], A["k_zpos"]).then_inc(sem("filter_in"), 16)
            act.dma_start(fw1[:], A["hy_f_w1"][0]).then_inc(sem("filter_in"), 16)
            act.dma_start(fw23[:, 0, :], A["hy_f_w2"][0]).then_inc(sem("filter_in"), 16)
            act.dma_start(fw23[:, 1, :], A["hy_f_w3"][0]).then_inc(sem("filter_in"), 16)
            act.dma_start(router[:], A["moe_router"][0].rearrange("(k p) n -> p k n", p=P)).then_inc(sem("router_in"), 16)

            def copy(group, k, dst, part=P, cols=slice(0, T), scale=1.0):
                t = ready(act, group, k)
                a(nc.scalar.activation(dst, t[0:part, cols], ACT.Copy, scale=scale), used(group))

            def root(group, k, n, cols=T, part=slice(0, P), sig="rms_ready"):
                t = ready(act, group, k)
                a(nc.scalar.activation(rstd[:, 0:cols], t[:, 0:cols], ACT.Sqrt, bias=eps[:, 0:1], scale=1.0 / n), used(group))

            def square(lo, hi, toks=slice(0, T)):
                a(nc.scalar.activation(sq[:, lo:hi, toks], hT[:, lo:hi, toks], ACT.Square), sem("act_squares"))

            for tt in range(2):
                for half in range(2):
                    t = ready(act, "xin", 2 * tt + half)
                    a(nc.scalar.activation(hT[:, 4 * half:4 * half + 4, META + P * tt:META + P * tt + P],
                                           t[:, :].rearrange("p (a b) -> p a b", a=4), ACT.Copy), used("xin"))
            t = ready(act, "xin", 4)
            a(nc.scalar.activation(hT[:, :, 0:META], t[:, 0:P].rearrange("p (a b) -> p a b", a=8), ACT.Copy), used("xin"))
            square(0, 4)
            t = ready(act, "param", 0)
            a(nc.scalar.activation(par[:, 0:C_A], t[:, 0:C_A], ACT.Copy))
            a(nc.scalar.activation(par[:, C_HCW:C_B], t[:, C_HCW:C_B], ACT.Copy))
            a(nc.scalar.activation(par[0:64, C_FV:C_FV + 6], t[0:64, C_FV:C_FV + 6], ACT.Copy), used("param"))
            act.wait_ge(sem("pool_consts"), 3)
            root("ss1", 0, D)

            def ssd_silu(j):
                act.wait_ge(sem("conv_ready"), j + 1)
                a(nc.scalar.activation(xbc[:, j, :], convt[:, j % 2, :], ACT.Silu), sem("xbc_ready"))

            act.wait_ge(sem("xp_zero"), 1)
            for j in range(8):
                copy("proj", j, xp[:, j, 2:2 + T])
                if j >= 1:
                    ssd_silu(j - 1)
            ssd_silu(7)
            for j in range(4):
                t = ready(act, "proj", 8 + j)
                a(nc.scalar.activation(zs[:, j, :], t[:, 0:T], ACT.Silu), used("proj"))
            act.wait_ge(sem("dt_raw"), 1)
            act.wait_ge(sem("dt_in"), 16 * 5)
            a(nc.scalar.activation(dtw[:, 7, 0:16], a_log, ACT.Exp))
            a(nc.scalar.activation(dtw[:, 2, :], dtw[:, 1, :], ACT.Exp, scale=-1.0))
            a(nc.scalar.activation(dtw[:, 3, :], dtw[:, 2, :], ACT.Ln, bias=1.0), sem("dt_log"))
            for k in range(2):
                copy("cs", k, csr[0:HEADS, k, :], HEADS)
            t = ready(act, "cs", 2)
            a(nc.scalar.activation(dtw[:, 6, 0:32], t[:, 0:32], ACT.Copy))
            a(nc.scalar.activation(dtw[0:META, 6, 32:48], t[0:META, 32:48], ACT.Copy), used("cs"))
            for tt, (t0, n) in enumerate(TOKS):
                copy("xs", tt, xT[0:n, tt, :], n, slice(0, 512))
            for k in range(6):
                n = TOKS[k % 3][1]
                copy("cb", k, CB[0:n, k, :], n)

            def decay_rows(h):
                for way, dst in ((0, M[:, h % 4]), (1, RB[:, h % 2])):
                    if way == 1 and h >= 2:
                        act.wait_ge(sem("decay_sum"), h - 1)
                    t = ready(act, "row", 2 * h + way)
                    for tt, (t0, n) in enumerate(TOKS):
                        a(nc.scalar.activation(dst[0:n, tt, :], t[0:n, 0:T], ACT.Relu, scale=-1.0,
                                               bias=dtw[0:n, 6, 16 * tt + 8 * way + h:16 * tt + 8 * way + h + 1]),
                          used("row") if tt == 2 else None)

            def decay_exp(h):
                act.wait_ge(sem("decay_sum"), h + 1)
                a(nc.scalar.activation(M[:, h % 4, 0:2, :], M[:, h % 4, 0:2, :], ACT.Exp, scale=-1.0))
                a(nc.scalar.activation(M[0:META, h % 4, 2, :], M[0:META, h % 4, 2, :], ACT.Exp, scale=-1.0), sem("decay_ready"))

            for s in range(9):
                if s < 8:
                    if s >= 4:
                        act.wait_ge(sem("tile_ready"), NUMBER[("y", (s - 4) // 2)] + 1)
                    decay_rows(s)
                if s < 6:
                    for j in range(12 + 2 * s, 14 + 2 * s):
                        if j < 16:
                            copy("proj", j, qk[:, j - 12, :], scale=64.0 ** -0.5)
                        elif j < 20:
                            copy("proj", j, qk[:, j - 12, :])
                        else:
                            copy("proj", j, vf[:, j - 20, :])
                if s < 8:
                    decay_exp(s)
            act.wait_ge(sem("yz_ready"), 4)
            a(nc.scalar.activation(sq[:, 0:4, :], ysb, ACT.Square), sem("act_squares"))
            for k in range(2):
                t = ready(act, "gss", k)
                a(nc.scalar.activation(sq[:, 4 + k, :], t[:, 0:T], ACT.Sqrt, bias=eps[:, 0:1], scale=1.0 / 256), used("gss"))
            for tt, (t0, n) in enumerate(TOKS):
                copy("vt", tt, vT[0:n, tt, :], n, slice(0, 512))

            act.wait_ge(sem("lam_sums"), 1)
            a(nc.scalar.activation(lam[:, 2:4], lam[:, 0:2], ACT.Exp), sem("lam_exp"))

            def exps(h):
                for tt, (t0, n) in enumerate(TOKS):
                    for m in range(2):
                        k = 6 * h + 2 * tt + m
                        act.wait_ge(sem("max_ready"), k + 1)
                        t = ready(act, "score", k)
                        if 3 * h + tt >= 2 and m == 0:
                            act.wait_ge(sem("a_ready"), 3 * h + tt - 1)
                        a(nc.scalar.activation(pr[0:n, (3 * h + tt) % 2, m, :], t[0:n, 0:T], ACT.Exp,
                                               bias=stat[0:n, k, 0:1], accum_out=stat[0:n, k, 1:2]), used("score"))

            exps(0)
            for h in range(ATT):
                if h + 1 < ATT:
                    exps(h + 1)
                for kt, (k0, n) in enumerate(TOKS):
                    copy("at", 3 * h + kt, aT[0:n, h % 2, kt, :], n)
            act.wait_ge(used("o"), ATT)
            a(nc.scalar.activation(sq[:, 0:4, :], osb, ACT.Square), sem("act_squares"))
            for k in range(4):
                t = ready(act, "oss", k)
                a(nc.scalar.activation(sq[:, 4 + k, :], t[:, 0:T], ACT.Sqrt, bias=eps[:, 0:1], scale=1.0 / P), used("oss"))

            def filter_sine(k):
                act.wait_ge(sem("arg_ready"), k + 1)
                a(nc.scalar.activation(harg[0:64, 3, :], harg[0:64, 1, :], ACT.Sin), sem("sin_ready"))

            def squares(group, s, k, toks=slice(0, T)):
                act.wait_ge(used(group), k + 1)
                a(nc.scalar.activation(sq[:, k, toks], hT[:, k, toks], ACT.Square), sem(s))

            def ring_high(n, i=0, k=KT):
                act.wait_ge(slot_in[n % RING], 16 * (n // RING + 1) + 16 * i)
                nc.scalar.activation(ring_hi[:, n % 2, 0:256 * k], ring[:, n % RING, 0:256 * k], ACT.Copy).then_inc(sem("ring_high"), 1)

            filter_sine(0)
            act.wait_ge(sem("cat_ready"), 8)
            for k in range(KT):
                if k == 6:
                    ring_high(B_FF)
                squares("wo", "squares2", k)
            root("ss2", 0, D)
            for k in range(KT):
                act.wait_ge(sem("xn_plain"), k + 1)
                nc.scalar.activation(xn_hi[:, k, :], xn[:, k, :], ACT.Copy).then_inc(sem("xn_high"), 1)
            ring_high(B_FF + 1)
            filter_sine(1)
            base = NUMBER[("gate", 0)]
            c_gate, c_up = CREDIT["gate"], CREDIT["up"]
            a.credit(used("gate"), c_gate)

            def gate(i, b):
                n = base + 4 * (b // 2) + b % 2
                act.wait_ge(sem("tile_ready"), 8 * i + n + 1)
                act.wait_ge(used("up"), 4 * i + b + 1)
                a(nc.scalar.activation(sg[:, b, :], ps[n % 8][:, 0:T], ACT.Silu), used("gate"))

            def gate_and_up(i, c, k):
                gate(i, 2 * c)
                gate(i, 2 * c + 1)
                ring_high(B_FF + 2 * c + 2, i, k)
                act.wait_ge(sem("tile_ready"), 8 * i + base + 4 * c + 4)
                ring_high(B_FF + 2 * c + 3, i, k)

            with act.Fori(0, 5) as i:
                a.loop(i, [(used("gate"), 4)])
                gate_and_up(i, 0, KT)
                gate_and_up(i, 1, KT)
                a.end(5)
            gate(5, 0)
            gate(5, 1)
            ring_high(B_DN, 0, 11)
            act.wait_ge(sem("tile_ready"), NUMBER[("up", FFT - 1)] + 1)
            ring_high(B_DN + 1, 0, 11)
            filter_sine(2)
            for d in range(8):
                if d % 2 == 0:
                    act.wait_ge(sem("half_done"), d // 2 + 1)
                else:
                    act.wait_ge(sem("tile_ready"), NUMBER[("down", d)] + 1)
                if d < 6:
                    ring_high(B_DN + d + 2, 0, 11)
                if d % 2:
                    squares("down", "squares3", d - 1)
                    squares("down", "squares3", d)
            root("ss3", 0, D)

            act.wait_ge(sem("keo_ready"), 2)
            a(nc.scalar.activation(kfb[:, 0:2, :], kfb[:, 0:2, :], ACT.Abs))
            a(nc.scalar.activation(kfb[0:META, 2, :], kfb[0:META, 2, :], ACT.Abs), sem("kabs_ready"))
            for k in range(12):
                ft, half = k // 4, k % 2
                n = TOKS[ft][1]
                dst = KR if k % 4 < 2 else KI
                copy("kspec", k, dst[0:n, ft, 512 * half:512 * half + 512], n, slice(0, 512))

            a.credit(used("hy"), CREDIT["hy"])
            base = NUMBER[("hy", 0)]
            act.wait_ge(sem("pad_zero"), 1)
            with act.Fori(0, 3) as i:
                a.loop(i, [(used("hy"), 8), (sem("tap0_ready"), 8)])
                for b in range(8):
                    n = base + b
                    act.wait_ge(sem("tile_ready"), 8 * i + n + 1)
                    act.wait_ge(sem("taps_ready"), 8 * i + b + 1)
                    j = 8 * i + b
                    a(nc.scalar.activation(pad[:, b, 1:1 + T], ps[n % 8][:, 0:T], ACT.Identity, bias=par[:, bass.ds(j + C_BIN, 1)]),
                      used("hy"))
                    a(nc.scalar.activation(hyc[:, bass.ds(j, 1), :].rearrange("p a t -> p (a t)"), pad[:, b, 0:T], ACT.Identity,
                                           bias=par[:, bass.ds(j + C_HCB, 1)], scale=par[:, bass.ds(j + C_HCW, 1)]), sem("tap0_ready"))
                a.end(3)
            for k in range(6):
                tt, half = k // 2, k % 2
                n = TOKS[tt][1]
                copy("vx", k, vtok[0:n, tt, 512 * half:512 * half + 512], n, slice(0, 512))

            for k in range(KT):
                squares("ho", "squares4", k, slice(META, T))
            t = ready(act, "ss4", 0)
            a(nc.scalar.activation(rstd[:, 0:SEQ], t[:, 0:SEQ], ACT.Sqrt, bias=eps[:, 0:1], scale=1.0 / D), used("ss4"))
            act.wait_ge(sem("logit_shift"), 1)
            a(nc.scalar.activation(rt[:, 32:48], rt[:, 16:32], ACT.Exp), sem("gate_exp"))
            for k in range(4):
                copy("xk", k, xtk[:, k // 2, 512 * (k % 2):512 * (k % 2) + 512], P, slice(0, 512))

            def high(part, i, q, p):
                act.wait_ge(sem(f"{part}_in{p}"), 16 * (7 * i + q + 1))
                at = "gud".index(part)
                nc.scalar.activation(w_hi[:, p, at, :], raw[:, p, at, :], ACT.Copy).then_inc(sem(f"{part}_high"), 1)

            def silu(n, p):
                act.wait_ge(sem("u_used"), n + 1)
                nc.scalar.activation(esg[:, p, :], ps[p][:, 0:256], ACT.Silu).then_inc(sem("sg_ready"), 1)

            def turned_high(n, p):
                act.wait_ge(sem("turned"), n + 1)
                nc.scalar.activation(eh_hi[:, p].rearrange("p a b -> p (a b)"), ps[2 + p][:, 0:256], ACT.Copy).then_inc(sem("eh_high"), 1)

            def half_ye(i):
                act.wait_ge(sem("d_used"), 14 * i)
                nc.scalar.activation(ye[:, 512:1024], ps[5][:, :], ACT.Copy).then_inc(sem("ye_act"), 1)

            def item(i, first=False):
                high("g", i, 0, 0)
                if not first:
                    turned_high(14 * i - 1, 1)
                high("u", i, 0, 0)
                for half in range(2):
                    act.wait_ge(sem("gather_ready"), 2 * i + half + 1)
                    nc.scalar.activation(xg_hi[:, 4 * half:4 * half + 4, :].rearrange("p a b -> p (a b)"), ps[6 + half][:, :],
                                         ACT.Copy).then_inc(sem("xg_high"), 1)
                high("g", i, 0, 1)
                if not first:
                    half_ye(i)
                high("u", i, 0, 1)
                with act.Fori(0, STAGES // 2 - 1) as q:
                    for p in range(2):
                        silu(14 * i + 2 * q + p, p)
                        high("d", i, q, p)
                        turned_high(14 * i + 2 * q + p, p)
                        high("g", i, q + 1, p)
                        high("u", i, q + 1, p)
                silu(14 * i + 12, 0)
                high("d", i, 6, 0)
                turned_high(14 * i + 12, 0)
                silu(14 * i + 13, 1)
                high("d", i, 6, 1)
                act.wait_ge(sem("gt_turned"), i + 1)
                nc.scalar.activation(GT[:], ps[2][:, 256:512], ACT.Copy).then_inc(sem("gt_ready"), 1)

            item(0, True)
            with act.Fori(1, NE) as i:
                item(i)
            act.wait_ge(sem("later_table"), 1)
            more = act.value_load(tab[0:1, 0:1], min_val=0, max_val=LATER)
            with act.If(more > 0):
                with act.Fori(0, more) as j:
                    item(j + NE)
            turned_high(14 * more + (14 * NE - 1), 1)
            half_ye(more + NE)
            act.wait_ge(sem("final_ss"), 1)
            a(nc.scalar.activation(rstd[:, 0:SEQ], ps[0][:, 0:SEQ], ACT.Sqrt, bias=eps[:, 0:1], scale=1.0 / D), sem("final_root"))

        @block.vector
        def _(dve):
            v = Steps(dve, sem("dve_chain"))
            V = nc.vector

            def mult_add(out_, in0, scalar, in1, s=None, op0=ALU.mult, op1=ALU.add):
                v(V.scalar_tensor_tensor(out=out_, in0=in0, scalar=scalar, in1=in1, op0=op0, op1=op1), s)

            def norm(group, col, toks=slice(0, T), s=None, weights=par):
                n = toks.stop - toks.start
                dve.wait_ge(used(group), 1)
                v(V.reciprocal(rstd[:, 0:n], rstd[:, 0:n]))
                for k in range(KT):
                    mult_add(xn[:, k, 0:n], hT[:, k, toks], par[:, col + k:col + k + 1], rstd[:, 0:n], s, ALU.mult, ALU.mult)

            def square(lo, hi, s, toks=slice(0, T)):
                v(V.tensor_tensor(sq[:, lo:hi, toks], hT[:, lo:hi, toks], hT[:, lo:hi, toks], ALU.mult), s)

            v(V.memset(xp, 0.0), sem("xp_zero"))
            V.memset(crd[:, 0:1], 0.0).then_inc(used("up"), CREDIT["up"])
            V.memset(crd[:, 1:2], 0.0).then_inc(sem("taps_ready"), 8)
            v(V.memset(dtw, 0.0))
            dve.wait_ge(used("xin"), 5)
            square(4, 8, sem("dve_squares"))
            dve.wait_ge(used("param"), 1)
            norm("ss1", C_NME, s=sem("xn1_ready"))
            dve.wait_ge(sem("dt_in"), 16 * 5)
            v(V.tensor_tensor(lam_in[:, 0:64], lam_in[:, 0:64], lam_in[:, 64:128], ALU.mult))
            v(V.tensor_tensor(lam_in[:, 128:192], lam_in[:, 128:192], lam_in[:, 192:256], ALU.mult))
            v(V.tensor_reduce(lam[:, 0:1], lam_in[:, 0:64], AX.X, ALU.add))
            v(V.tensor_reduce(lam[:, 1:2], lam_in[:, 128:192], AX.X, ALU.add), sem("lam_sums"))
            for odd in range(2):
                r = slice(64 * odd, 64 * odd + 64)
                d2 = d_in[r, :].rearrange("p (w t o) -> p w t o", w=2, o=2)
                v(V.tensor_tensor(dskip[r, :], d2[:, 0, :, odd], d2[:, 1, :, odd], ALU.add))
            for j in range(8):
                dve.wait_ge(used("proj"), j + 1)
                w = lambda k: par[:, C_CW + 8 * k + j:C_CW + 8 * k + j + 1]
                if j >= 2:
                    dve.wait_ge(sem("xbc_ready"), j - 1)
                c = convt[:, j % 2, :]
                v(V.tensor_scalar(c, xp[:, j, 0:T], w(0), par[:, C_CB + j:C_CB + j + 1], ALU.mult, ALU.add))
                for k in range(1, CONV):
                    mult_add(c, xp[:, j, k:k + T], w(k), c, sem("conv_ready") if k == CONV - 1 else None)
            t = ready(dve, "dt", 0)
            v(V.tensor_tensor(dtw[:, 0, 0:16], t[:, 0:16], dt_bias, ALU.add))
            v(V.tensor_tensor(dtw[:, 0, 16:32], t[:, 16:32], dt_bias, ALU.add))
            v(V.tensor_tensor(dtw[0:META, 0, 32:48], t[0:META, 32:48], dt_bias[0:META, :], ALU.add), used("dt"))
            mult_add(dtw[:, 1, :], dtw[:, 0, :], -1.0, dtw[:, 0, :], sem("dt_raw"), ALU.mult, ALU.max)
            dve.wait_ge(sem("dt_log"), 1)
            mult_add(dtw[:, 4, :], dtw[:, 0, :], 0.0, dtw[:, 3, :], sem("dt_ready"), ALU.max, ALU.add)
            for tt in range(3):
                mult_add(dtw[:, 5, 16 * tt:16 * tt + 16], dtw[:, 4, 16 * tt:16 * tt + 16], -1.0, dtw[:, 7, 0:16], sem("a_vec_ready"), ALU.mult, ALU.mult)

            def ssd_out(pair):
                t = ready(dve, "y", pair)
                mult_add(ysb[:, pair, :], xbc[:, pair, :], dskip[:, pair:pair + 1], t[:, 0:T], used("y"))
                v(V.tensor_tensor(ysb[:, pair, :], ysb[:, pair, :], zs[:, pair, :], ALU.mult), sem("yz_ready"))

            dve.wait_ge(sem("table_in"), 32)
            for h in range(HEADS):
                m, wt = M[:, h % 4], W[:, h % 2]
                for tt, (t0, n) in enumerate(TOKS):
                    dve.wait_ge(sem("w1_ready"), 3 * h + tt + 1)
                    mult_add(wt[0:n, tt, :], UF[0:n, tt, :], dtw[0:n, 4, 16 * tt + h:16 * tt + h + 1], W1[0:n, h % 2, tt, :])
                dve.wait_ge(used("row"), 2 * h + 2)
                v(V.tensor_tensor(m[:, 0:2, :], m[:, 0:2, :], RB[:, h % 2, 0:2, :], ALU.add))
                v(V.tensor_tensor(m[0:META, 2, :], m[0:META, 2, :], RB[0:META, h % 2, 2, :], ALU.add), sem("decay_sum"))
                if h == 0:
                    dve.wait_ge(used("cb"), 6)
                g3 = 3 * (h // 4)
                v(V.tensor_tensor(wt[:, 0:2, :], wt[:, 0:2, :], CB[:, g3:g3 + 2, :], ALU.mult))
                v(V.tensor_tensor(wt[0:META, 2, :], wt[0:META, 2, :], CB[0:META, g3 + 2, :], ALU.mult))
                dve.wait_ge(sem("decay_ready"), h + 1)
                v(V.tensor_tensor(m[:, 0:2, :], m[:, 0:2, :], wt[:, 0:2, :], ALU.mult))
                v(V.tensor_tensor(m[0:META, 2, :], m[0:META, 2, :], wt[0:META, 2, :], ALU.mult), sem("m_ready"))
                if h >= 4 and h % 2 == 0:
                    ssd_out((h - 4) // 2)
            for pair in (2, 3):
                ssd_out(pair)
            for j in range(8):
                t = ready(dve, "rope", j)
                v(V.tensor_tensor(ropet[:, 0, :], t[:, 0:T], sinT, ALU.mult), used("rope"))
                v(V.tensor_tensor(ropet[:, 1, :], qk[:, j, :], cosT, ALU.mult))
                v(V.tensor_tensor(qk[:, j, :], ropet[:, 0, :], ropet[:, 1, :], ALU.add), sem("qk_ready"))
            for g in range(2):
                dve.wait_ge(used("gss"), g + 1)
                v(V.reciprocal(sq[:, 4 + g, :], sq[:, 4 + g, :]))
                for k in range(2 * g, 2 * g + 2):
                    mult_add(cat[:, k, :], ysb[:, k, :], par[:, C_SNW + k:C_SNW + k + 1], sq[:, 4 + g, :], sem("cat_ready"), ALU.mult, ALU.mult)
            dve.wait_ge(sem("lam_exp"), 1)
            v(V.tensor_tensor(lam[:, 4:5], lam[:, 3:4], lam[:, 2:3], ALU.subtract))
            v(V.tensor_scalar(lam[:, 4:5], lam[:, 4:5], -LAMBDA_INIT, None, ALU.add))

            def row_max(k):
                n = TOKS[(k % 6) // 2][1]
                t = ready(dve, "score", k)
                v(V.tensor_reduce(stat[0:n, k, 0:1], t[0:n, 0:T], AX.X, ALU.max, negate=True), sem("max_ready"))

            def combine(h, tt):
                n = TOKS[tt][1]
                k = 6 * h + 2 * tt
                dve.wait_ge(used("score"), k + 2)
                v(V.reciprocal(stat[0:n, k:k + 2, 2:3], stat[0:n, k:k + 2, 1:2]))
                v(V.tensor_scalar(stat[0:n, k + 1, 3:4], stat[0:n, k + 1, 2:3], lam[0:n, 4:5], None, ALU.mult))
                pk = pr[0:n, (3 * h + tt) % 2]
                v(V.tensor_scalar(pk[:, 0, :], pk[:, 0, :], stat[0:n, k, 2:3], None, ALU.mult))
                mult_add(at_[0:n, h % 2, tt, :], pk[:, 1, :], stat[0:n, k + 1, 3:4], pk[:, 0, :], sem("a_ready"))

            v(V.tensor_scalar(lam[:, 5:6], par[:, C_SUB:C_SUB + 1], 1.0 - LAMBDA_INIT, None, ALU.mult))

            def softmaxes(h):
                if h >= 2:
                    dve.wait_ge(used("at"), 3 * (h - 1))
                for tt in range(3):
                    row_max(6 * h + 2 * tt)
                    row_max(6 * h + 2 * tt + 1)
                    if tt >= 1:
                        combine(h, tt - 1)
                combine(h, 2)

            softmaxes(0)
            for h in range(ATT):
                if h + 1 < ATT:
                    softmaxes(h + 1)
                t = ready(dve, "o", h)
                v(V.tensor_copy(osb[:, h, :], t[:, 0:T]), used("o"))
            for k in range(4):
                dve.wait_ge(used("oss"), k + 1)
                v(V.reciprocal(sq[:, 4 + k, :], sq[:, 4 + k, :]))
                mult_add(cat[:, 4 + k, :], osb[:, k, :], lam[:, 5:6], sq[:, 4 + k, :], sem("cat_ready"), ALU.mult, ALU.mult)
            def filter_argument(k):
                t = ready(dve, "mlp", k)
                x0, x1, x2 = harg[0:64, 0, :], harg[0:64, 1, :], harg[0:64, 2, :]
                v(V.tensor_scalar(x0, t[0:64, 0:T], par[0:64, C_FV + k:C_FV + k + 1], par[0:64, C_FV + 3 + k:C_FV + 4 + k], ALU.add, ALU.mult), used("mlp"))
                v(V.tensor_scalar(x1, x0, 1.0 / (2.0 * math.pi), ROUND, ALU.mult, ALU.add))
                v(V.tensor_scalar(x1, x1, ROUND, None, ALU.subtract))
                mult_add(x0, x1, -TWO_PI_A, x0)
                mult_add(x2, x1, -TWO_PI_B, x0)
                v(V.tensor_scalar(x1, x2, 3.1415925, -3.1415925, ALU.min, ALU.max), sem("arg_ready"))

            def ring_low(n, i=0, k=KT):
                dve.wait_ge(sem("ring_high"), n - B_FF + 1 + 4 * i)
                c = slice(0, 256 * k)
                V.tensor_tensor(ring_lo[:, n % RING, c], ring[:, n % RING, c], ring_hi[:, n % 2, c].bitcast(F32), ALU.subtract).then_inc(sem("ring_split"), 1)

            def add_to_stream(group, j):
                t = ready(dve, group, j)
                v(V.tensor_tensor(hT[:, j, :], hT[:, j, :], t[:, 0:T], ALU.add), used(group))

            filter_argument(0)
            for j in range(8):
                if j == 6:
                    ring_low(B_FF)
                add_to_stream("wo", j)
            dve.wait_ge(used("ss2"), 1)
            v(V.reciprocal(rstd[:], rstd[:]))
            for k in range(KT + 1):
                if k < KT:
                    V.scalar_tensor_tensor(out=xn[:, k, :], in0=hT[:, k, :], scalar=par[:, C_NFE + k:C_NFE + k + 1], in1=rstd[:],
                                           op0=ALU.mult, op1=ALU.mult).then_inc(sem("xn_plain"), 1)
                if k >= 1:
                    dve.wait_ge(sem("xn_high"), k)
                    V.tensor_tensor(xn_lo[:, k - 1, :], xn[:, k - 1, :], xn_hi[:, k - 1, :].bitcast(F32), ALU.subtract).then_inc(sem("xn2_ready"), 1)
            ring_low(B_FF + 1)
            filter_argument(1)
            v.credit(used("up"), CREDIT["up"])
            V.memset(crd[:, 2:3], 0.0).then_inc(used("gate"), CREDIT["gate"])
            base = NUMBER[("up", 0)]

            def up(i, b):
                n = base + 4 * (b // 2) + b % 2
                dve.wait_ge(used("gate"), 4 * i + b + 1 + CREDIT["gate"])
                dve.wait_ge(sem("tile_ready"), 8 * i + n + 1)
                h = ffp[:, b % 2, :]
                hi, lo = (a[:, 4 * i + b, :] if isinstance(i, int) else a[:, bass.ds(4 * i + b, 1), :].rearrange("p a t -> p (a t)")
                          for a in (ffh_hi, ffh_lo))
                v(V.tensor_tensor(h, sg[:, b, :], ps[n % 8][:, 0:T], ALU.mult), used("up"))
                v(V.tensor_copy(hi, h))
                v(V.tensor_tensor(lo, h, hi.bitcast(F32), ALU.subtract), sem("ffh_ready"))

            def gate_and_up(i, c, k):
                ring_low(B_FF + 2 * c + 2, i, k)
                up(i, 2 * c)
                up(i, 2 * c + 1)
                ring_low(B_FF + 2 * c + 3, i, k)

            with dve.Fori(0, 5) as i:
                v.loop(i, [(used("up"), 4), (sem("dve_chain"), 4), (sem("ffh_ready"), 4)])
                gate_and_up(i, 0, KT)
                gate_and_up(i, 1, KT)
                v.end(5)
            ring_low(B_DN, 0, 11)
            up(5, 0)
            up(5, 1)
            ring_low(B_DN + 1, 0, 11)
            filter_argument(2)
            for d in range(8):
                if d % 2:
                    add_to_stream("down", d - 1)
                    add_to_stream("down", d)
                if d < 6:
                    ring_low(B_DN + d + 2, 0, 11)

            dve.wait_ge(sem("window_in"), 32)
            for k in range(12):
                lt, c = k // 4, k % 4
                n = TOKS[lt][1]
                t = ready(dve, "kt", k)
                v(V.tensor_tensor(kfb[0:n, lt, 512 * c:512 * c + 512], t[0:n, :], win[0:n, lt, 512 * (c % 2):512 * (c % 2) + 512], ALU.mult), used("kt"))
            v(V.memset(kfb[0:1, 0, D:2 * D], 0.0))
            for pp, ts in ((P, slice(0, 2)), (META, slice(2, 3))):
                v(V.tensor_tensor(KE[0:pp, ts, :], kfb[0:pp, ts, 0:D], kfb[0:pp, ts, D:2 * D], ALU.add))
                v(V.tensor_tensor(KO[0:pp, ts, :], kfb[0:pp, ts, 0:D], kfb[0:pp, ts, D:2 * D], ALU.subtract), sem("keo_ready"))
            norm("ss3", C_NMO, s=sem("xn3_ready"))
            dve.wait_ge(sem("kabs_ready"), 1)
            for pp, ts in ((P, slice(0, 2)), (META, slice(2, 3))):
                v(V.tensor_tensor(kfb[0:pp, ts, 0:D], kfb[0:pp, ts, 0:D], kfb[0:pp, ts, D:2 * D], ALU.add), sem("kabs_sum"))
            t = ready(dve, "kn", 0)
            v(V.reciprocal(invn, t[:, 0:8]), used("kn"))
            dve.wait_ge(used("kspec"), 12)
            v(V.memset(pad[:, :, 0:1], 0.0))
            v(V.memset(pad[:, :, T + 1:T + 2], 0.0), sem("pad_zero"))
            V.memset(crd[:, 4:5], 0.0).then_inc(used("hy"), CREDIT["hy"])
            v.credit(sem("taps_ready"), 8)
            with dve.Fori(0, 3) as i:
                v.loop(i, [(sem("taps_ready"), 8), (sem("dve_chain"), 8)])
                for b in range(8):
                    j = 8 * i + b
                    dve.wait_ge(sem("tap0_ready"), 8 * i + b + 1)
                    o = hyc[:, bass.ds(j, 1), :].rearrange("p a t -> p (a t)")
                    mult_add(o, pad[:, b, 1:1 + T], par[:, bass.ds(j + C_HCW + 24, 1)], o)
                    mult_add(o, pad[:, b, 2:2 + T], par[:, bass.ds(j + C_HCW + 48, 1)], o, sem("taps_ready"))
                v.end(3)
            v(V.tensor_tensor(hyc[:, 8:16, :], hyc[:, 8:16, :], hyc[:, 0:8, :], ALU.mult), sem("v_ready"))
            for k in range(6):
                ft, half = k // 2, k % 2
                n = TOKS[ft][1]
                c = slice(512 * half, 512 * half + 512)
                if k >= 1:
                    dve.wait_ge(sem("spec_ready"), 2 * k)
                tr = ready(dve, "vspec", 2 * k)
                v(V.tensor_tensor(prod[0:n, 0, :], KR[0:n, ft, c], tr[0:n, :], ALU.mult), sem("prod_ready"))
                v(V.tensor_tensor(prod[0:n, 3, :], KI[0:n, ft, c], tr[0:n, :], ALU.mult), sem("prod_ready"))
                ti = ready(dve, "vspec", 2 * k + 1)
                v(V.tensor_tensor(prod[0:n, 1, :], KI[0:n, ft, c], ti[0:n, :], ALU.mult), sem("prod_ready"))
                v(V.tensor_tensor(prod[0:n, 2, :], KR[0:n, ft, c], ti[0:n, :], ALU.mult), sem("prod_ready"))
            for j in range(8):
                t = ready(dve, "inv", j)
                v(V.tensor_scalar(ytmp[:, 0, :], hyc[:, 8 + j, META:T], par[:, C_SKIP + j:C_SKIP + j + 1], None, ALU.mult))
                mult_add(ytmp[:, 1, :], t[:, 0:SEQ], invn[:, j:j + 1], ytmp[:, 0, :], used("inv"))
                v(V.tensor_tensor(xn[:, j, 0:SEQ], ytmp[:, 1, :], hyc[:, 16 + j, META:T], ALU.mult), sem("yh_ready"))
            v(V.memset(crd[:, 5:6], 0.0), sem("hyena_done"))
            for j in range(8):
                t = ready(dve, "ho", j)
                mult_add(hT[:, j, META:T], t[:, 0:SEQ], par[:, C_BOUT + j:C_BOUT + j + 1], hT[:, j, META:T], used("ho"), ALU.add, ALU.add)
            norm("ss4", C_NFO, slice(META, T), sem("xn4_ready"))

            lg, sh, ex = rt[:, 0:16], rt[:, 16:32], rt[:, 32:48]
            rank, pick = rt[:, 48:64], rt[:, 64:80]
            m1 = rt[:, 112:128]
            NI = ITEMS + 1
            place, gatev = rt[:, 384:384 + 2 * NI], rt[:, 416:416 + 2 * NI]
            place3, gate3 = place.rearrange("p (t i) -> p t i", t=2), gatev.rearrange("p (t i) -> p t i", t=2)
            gt_, eq_ = rt[:, 128:256], rt[:, 256:384]
            t = ready(dve, "logit", 0)
            v(V.tensor_copy(lg, t[:, 0:16]), used("logit"))
            for tt in range(2):
                l = lg[:, NE * tt:NE * tt + NE]
                l_f = l.rearrange("p (a f) -> p a f", a=1).to_broadcast([P, NE, NE])
                l_e = l.rearrange("p (e a) -> p e a", a=1).to_broadcast([P, NE, NE])
                gv = gt_[:, 64 * tt:64 * tt + 64].rearrange("p (e f) -> p e f", e=NE)
                ev = eq_[:, 64 * tt:64 * tt + 64].rearrange("p (e f) -> p e f", e=NE)
                v(V.tensor_reduce(m1[:, tt:tt + 1], l, AX.X, ALU.max))
                v(V.tensor_scalar(sh[:, NE * tt:NE * tt + NE], l, m1[:, tt:tt + 1], None, ALU.subtract), sem("logit_shift") if tt == 1 else None)
                v(V.tensor_tensor(gv, l_f, l_e, ALU.is_gt))
                v(V.tensor_tensor(ev, l_f, l_e, ALU.is_equal))
                v(V.tensor_tensor(ev, ev, tri, ALU.mult))
                v(V.tensor_tensor(gv, gv, ev, ALU.add))
                v(V.tensor_reduce(rank[:, NE * tt:NE * tt + NE], gv, AX.X, ALU.add))
            v(V.tensor_scalar(pick, rank, 1.5, None, ALU.is_lt), sem("pick_ready"))
            dve.wait_ge(sem("gate_exp"), 1)
            v(V.tensor_tensor(ex, ex, pick, ALU.mult))
            for tt in range(2):
                e = slice(NE * tt, NE * tt + NE)
                v(V.tensor_reduce(m1[:, 2 + tt:3 + tt], ex[:, e], AX.X, ALU.add))
                v(V.reciprocal(m1[:, 4 + tt:5 + tt], m1[:, 2 + tt:3 + tt]))
                v(V.tensor_scalar(gatev[:, NI * tt:NI * tt + NE], ex[:, e], m1[:, 4 + tt:5 + tt], None, ALU.mult))
            t = ready(dve, "pos", 0)
            v(V.memset(place, -1.0))
            mult_add(place3[:, :, 0:NE], t[:, 0:16].rearrange("p (t e) -> p t e", t=2), 1.0,
                     pick.rearrange("p (t e) -> p t e", t=2), None, ALU.add, ALU.mult)
            v(V.tensor_scalar(place3[:, :, 0:NE], place3[:, :, 0:NE], -1.0, None, ALU.add))

            def column(table, tt, i):
                return table[:, NI * tt + i:NI * tt + i + 1] if isinstance(i, int) else table[:, bass.ds(i + NI * tt, 1)]

            def select(i):
                for tt in range(2):
                    V.tensor_scalar(SEL[:, tt, :], iota, column(place, tt, i), None, ALU.is_equal).then_inc(sem("sel_ready"), 1)

            select(0)
            flag, nth_at, hit, prod3, place2 = (rt[:, a:a + n] for a, n in ((448, 8), (456, 8), (464, 24), (488, 24), (512, 16)))
            hit3, prod3 = hit.rearrange("p (k e) -> p k e", k=LATER), prod3.rearrange("p (k e) -> p k e", k=LATER)

            def over_k(a):
                return a.rearrange("p (k e) -> p k e", k=1).to_broadcast([P, LATER, NE])

            v(V.tensor_scalar(flag, t[:, 16:24], float(CAP) + 0.5, None, ALU.is_gt), used("pos"))
            v(V.tensor_reduce(tabf[0:1, 0:1], flag[0:1, :], AX.X, ALU.add))
            v(V.tensor_tensor_scan(nth_at, flag, flag, 0.0, ALU.add, ALU.bypass))
            v(V.tensor_tensor(nth_at, nth_at, flag, ALU.subtract))
            v(V.tensor_tensor(hit3, over_k(nth_at), nth, ALU.is_equal))
            v(V.tensor_tensor(hit3, hit3, over_k(flag), ALU.mult))
            v(V.tensor_tensor(prod3, hit3, expert, ALU.mult))
            v(V.tensor_reduce(tabf[0:1, 1:1 + LATER], prod3[0:1], AX.X, ALU.add))
            v(V.tensor_copy(tab[0:1, 0:1 + LATER], tabf[0:1, 0:1 + LATER]), sem("later_table"))
            v(V.tensor_scalar(place2.rearrange("p (t e) -> p t e", t=2), place3[:, :, 0:NE], -float(CAP), None, ALU.add))
            for tt in range(2):
                v(V.tensor_tensor(prod3, hit3, over_k(place2[:, NE * tt:NE * tt + NE]), ALU.mult))
                v(V.tensor_reduce(place3[:, tt, NE:ITEMS], prod3, AX.X, ALU.add))
                v(V.tensor_tensor(prod3, hit3, over_k(gatev[:, NI * tt:NI * tt + NE]), ALU.mult))
                v(V.tensor_reduce(gate3[:, tt, NE:ITEMS], prod3, AX.X, ALU.add))

            def low(part, i, q, p):
                dve.wait_ge(sem(f"{part}_high"), 14 * i + 2 * q + p + 1)
                at = "gud".index(part)
                V.tensor_tensor(w_lo[:, p, at, :], raw[:, p, at, :], w_hi[:, p, at, :].bitcast(F32), ALU.subtract).then_inc(sem(f"{part}_split"), 1)

            def hidden(n, p):
                dve.wait_ge(sem("sg_ready"), n + 1)

                V.tensor_tensor(eh[:, p, :], esg[:, p, :], ps[p][:, 256:512], ALU.mult).then_inc(sem("h_ready"), 1)

            def turned_low(n, p):
                dve.wait_ge(sem("eh_high"), n + 1)
                V.tensor_tensor(eh_lo[:, p].rearrange("p a b -> p (a b)"), ps[2 + p][:, 0:256],
                                eh_hi[:, p].rearrange("p a b -> p (a b)").bitcast(F32), ALU.subtract).then_inc(sem("eh_split"), 1)

            def half_ye(i):
                dve.wait_ge(sem("d_used"), 14 * i)
                V.tensor_copy(ye[:, 0:512], ps[4][:, :]).then_inc(sem("ye_dve"), 1)

            def add_result(i, c):
                dve.wait_ge(sem("comb_ready"), 4 * i - 4 + c + 1)
                V.tensor_tensor(hT[:, 2 * c:2 * c + 2, META:T], hT[:, 2 * c:2 * c + 2, META:T],
                                ps[6 + c % 2][:, :].rearrange("p (a b) -> p a b", a=2), ALU.add).then_inc(sem("comb_used"), 1)

            def stage(i, q, p, ahead=True, turn_too=True):
                low("d", i, q, p)
                if turn_too:
                    turned_low(14 * i + 2 * q + p, p)
                if ahead:
                    low("g", i, q + 1, p)
                    low("u", i, q + 1, p)

            def item(i, first=False):
                low("g", i, 0, 0)
                if not first:
                    turned_low(14 * i - 1, 1)
                low("u", i, 0, 0)
                for half in range(2):
                    dve.wait_ge(sem("xg_high"), 2 * i + half + 1)
                    k = slice(4 * half, 4 * half + 4)
                    V.tensor_tensor(xg_lo[:, k, :].rearrange("p a b -> p (a b)"), ps[6 + half][:, :],
                                    xg_hi[:, k, :].rearrange("p a b -> p (a b)").bitcast(F32), ALU.subtract).then_inc(sem("xg_split"), 1)
                low("g", i, 0, 1)
                if not first:
                    half_ye(i)
                low("u", i, 0, 1)
                hidden(14 * i, 0)
                if not first:
                    add_result(i, 0)
                    add_result(i, 1)
                stage(i, 0, 0)
                hidden(14 * i + 1, 1)
                if not first:
                    add_result(i, 2)
                    add_result(i, 3)
                for tt in range(2):
                    V.tensor_scalar(SELG[:, tt, :], iota, column(place, tt, i), column(gatev, tt, i), ALU.is_equal, ALU.mult).then_inc(sem("selg_ready"), 1)
                select(i + 1)
                stage(i, 0, 1)
                with dve.Fori(0, STAGES // 2 - 2) as q:
                    for p in range(2):
                        hidden(14 * i + 2 * q + 2 + p, p)
                        stage(i, q + 1, p)
                hidden(14 * i + 12, 0)
                stage(i, 6, 0, ahead=False)
                hidden(14 * i + 13, 1)
                stage(i, 6, 1, ahead=False, turn_too=False)

            item(0, True)
            with dve.Fori(1, NE) as i:
                item(i)
            more = dve.value_load(tab[0:1, 0:1], min_val=0, max_val=LATER)
            with dve.If(more > 0):
                with dve.Fori(0, more) as j:
                    item(j + NE)
            turned_low(14 * more + (14 * NE - 1), 1)
            half_ye(more + NE)
            for c in range(4):
                add_result(more + NE, c)
            dve.wait_ge(sem("comb_used"), 4 * more + 4 * NE)
            V.tensor_tensor(sq[:, :, 0:SEQ], hT[:, :, META:T], hT[:, :, META:T], ALU.mult).then_inc(sem("final_squares"), 1)
            dve.wait_ge(sem("final_root"), 1)
            dve.wait_ge(sem("final_squares"), 1)
            f = Steps(dve, sem("final_chain"))
            f(V.reciprocal(rstd[:, 0:SEQ], rstd[:, 0:SEQ]))
            for k in range(KT):
                f(V.scalar_tensor_tensor(out=xn[:, k, 0:SEQ], in0=hT[:, k, META:T], scalar=par[:, C_FIN + k:C_FIN + k + 1],
                                         in1=rstd[:, 0:SEQ], op0=ALU.mult, op1=ALU.mult), sem("final_xn"))
            for k in range(4):
                dve.wait_ge(sem("final_turn"), k + 1)
                f(V.tensor_copy(osb2[:, k // 2, 512 * (k % 2):512 * (k % 2) + 512], ps[1 + k][:, :]), sem("out_ready"))

        @block.tensor
        def _(pe):
            def open_tile(group, k):
                n = NUMBER[(group, k)]
                if n >= 8:
                    g, j = ORDER[n - 8]
                    if g == "vspec":
                        pe.wait_ge(sem("prod_ready"), 2 * j + 2)
                    else:
                        pe.wait_ge(used(g), j + 1 + CREDIT.get(g, 0))
                return ps[n % 8]

            def close(ins):
                ins.then_inc(sem("tile_ready"), 1)

            def mm(o, l, r, start=True, stop=True):
                return nc.tensor.matmul(o, l, r, start=start, stop=stop)

            def product(o, hi, lo, moving, start, stop):
                mm(o, hi, moving[0], start, False)
                mm(o, hi, moving[1], False, False)
                return mm(o, lo, moving[0], False, stop)

            def split_block(n, k=KT):
                return [a.rearrange("p (k n) -> p k n", k=k) for a in (ring_hi[:, n % 2, 0:256 * k], ring_lo[:, n % RING, 0:256 * k])]

            def turn(o, src, n=P):
                return nc.tensor.transpose(o, src, ident[0:n, 0:n])

            def arrived(n):
                pe.wait_ge(slot_in[n % RING], 16 * (n // RING + 1))

            def linear(group, j0, n, rhs, cols=T, coming=None):
                arrived(n)
                w = slot(n)
                for j in range(2):
                    o = open_tile(group, j0 + j)
                    for k in range(KT):
                        if coming is not None and j == 0:
                            pe.wait_ge(coming, k + 1)
                        last = mm(o[:, 0:cols], w[:, k, 128 * j:128 * j + 128], rhs[:, k, 0:cols], k == 0, k == KT - 1)
                    close(last)

            def sum_squares(group, k, lo, hi, cols=slice(0, T)):
                o = open_tile(group, k)
                for q in range(lo, hi):
                    last = mm(o[:, 0:cols.stop - cols.start], ones[:], sq[:, q, cols], q == lo, q == hi - 1)
                close(last)

            def add_squares(group, s, k0, n, toks=slice(0, T)):
                o = open_tile(group, 0) if k0 == 0 else ps[NUMBER[(group, 0)] % 8]
                for k in range(k0, k0 + n):
                    pe.wait_ge(sem(s), k + 1)
                    last = mm(o[:, 0:toks.stop - toks.start], ones[:], sq[:, k, toks], k == 0, k == KT - 1)
                if k0 + n == KT:
                    close(last)

            pe.wait_ge(sem("ident_in"), 16)
            pe.wait_ge(sem("x_in"), 32)
            for tt in range(2):
                for half in range(2):
                    o = open_tile("xin", 2 * tt + half)
                    for c in range(4):
                        k = 4 * half + c
                        last = turn(o[:, P * c:P * c + P], xtok[:, tt, P * k:P * k + P])
                    close(last)
            o = open_tile("xin", 4)
            for k in range(KT):
                last = turn(o[:, META * k:META * k + META], mtok[0:META, P * k:P * k + P], META)
            close(last)
            pe.wait_ge(sem("param_in"), 16 * 25)
            o = open_tile("param", 0)
            turn(o[:, 0:C_A], prow[0:C_A, 0, :], C_A)
            turn(o[:, C_HCW:C_B], prow[0:C_B - P, 1, :], C_B - P)
            close(turn(o[0:64, C_FV:C_FV + 6], prow[0:6, 2, 0:64], 6))
            pe.wait_ge(sem("pool_consts"), 3)
            pe.wait_ge(sem("act_squares"), 1)
            pe.wait_ge(sem("dve_squares"), 1)
            sum_squares("ss1", 0, 0, KT)
            for n in range(6):
                linear("proj", 2 * n, n, xn, coming=sem("xn1_ready") if n == 0 else None)
            pe.wait_ge(sem("dt_in"), 16 * 5)
            o = open_tile("dt", 0)
            for tt, (t0, n) in enumerate(TOKS):
                for k in range(KT):
                    last = mm(o[0:n, 16 * tt:16 * tt + 16], xn[:, k, t0:t0 + n], wdt[:, k, :], k == 0, k == KT - 1)
            close(last)
            pe.wait_ge(sem("a_vec_ready"), 3)
            pe.wait_ge(sem("table_in"), 32)
            for way, U in enumerate((UF, UB)):
                o = open_tile("cs", way)
                for tt, (t0, n) in enumerate(TOKS):
                    last = mm(o[0:HEADS, 0:T], dtw[0:n, 5, 16 * tt + 8 * way:16 * tt + 8 * way + 8], U[0:n, tt, :], tt == 0, tt == 2)
                close(last)
            o = open_tile("cs", 2)
            for tt, (t0, n) in enumerate(TOKS):
                for way, U in enumerate((UF, UB)):
                    for st, (s0, m) in enumerate(TOKS):
                        last = mm(o[0:n, 16 * tt + 8 * way:16 * tt + 8 * way + 8], U[0:m, st, t0:t0 + n],
                                  dtw[0:m, 5, 16 * st + 8 * way:16 * st + 8 * way + 8], st == 0, st == 2)
            close(last)
            pe.wait_ge(sem("xbc_ready"), 8)
            for tt, (t0, n) in enumerate(TOKS):
                o = open_tile("xs", tt)
                for c in range(4):
                    last = turn(o[0:n, P * c:P * c + P], xbc[:, c, t0:t0 + n])
                close(last)
            for g in range(2):
                for tt, (t0, n) in enumerate(TOKS):
                    o = open_tile("cb", 3 * g + tt)
                    close(mm(o[0:n, 0:T], xbc[:, 4 + g, t0:t0 + n], xbc[:, 6 + g, :]))
            pe.wait_ge(used("cs"), 3)
            pe.wait_ge(used("xs"), 3)
            for s in range(10):
                if s < 8:
                    for way in range(2):
                        o = open_tile("row", 2 * s + way)
                        close(mm(o[:, 0:T], sel8[:, P * s:P * s + P], csr[0:HEADS, way, :]))
                if s < 6:
                    linear("proj", 12 + 2 * s, 6 + s, xn)
                if s >= 3 and s % 2 == 1:
                    pair = (s - 3) // 2
                    o = open_tile("y", pair)
                    for h in (2 * pair, 2 * pair + 1):
                        pe.wait_ge(sem("m_ready"), h + 1)
                        r = 64 * (h % 2)
                        for tt, (t0, n) in enumerate(TOKS):
                            last = mm(o[r:r + 64, 0:T], xT[0:n, tt, 64 * h:64 * h + 64], M[0:n, h % 4, tt, :], tt == 0, tt == 2)
                    close(last)
            pe.wait_ge(used("proj"), 24)
            for j in range(8):
                o = open_tile("rope", j)
                close(mm(o[:, 0:T], perm, qk[:, j, :]))
            pe.wait_ge(sem("act_squares"), 2)
            for g in range(2):
                sum_squares("gss", g, 2 * g, 2 * g + 2)
            for tt, (t0, n) in enumerate(TOKS):
                o = open_tile("vt", tt)
                for c in range(4):
                    last = turn(o[0:n, P * c:P * c + P], vf[:, c, t0:t0 + n])
                close(last)
            pe.wait_ge(sem("qk_ready"), 8)
            pe.wait_ge(used("vt"), 3)

            def scores(h):
                for tt, (t0, n) in enumerate(TOKS):
                    for m in range(2):
                        o = open_tile("score", 6 * h + 2 * tt + m)
                        r = slice(64 * m, 64 * m + 64)
                        close(mm(o[0:n, 0:T], qk[r, h, t0:t0 + n], qk[r, 4 + h, :]))

            scores(0)
            for h in range(ATT):
                if h + 1 < ATT:
                    scores(h + 1)
                pe.wait_ge(sem("a_ready"), 3 * h + 3)
                for kt, (k0, m) in enumerate(TOKS):
                    o = open_tile("at", 3 * h + kt)
                    for tt, (t0, n) in enumerate(TOKS):
                        last = turn(o[0:m, t0:t0 + n], at_[0:n, h % 2, tt, k0:k0 + m], n)
                    close(last)
                o = open_tile("o", h)
                pe.wait_ge(used("at"), 3 * h + 3)
                for kt, (k0, m) in enumerate(TOKS):
                    last = mm(o[:, 0:T], vT[0:m, kt, P * h:P * h + P], aT[0:m, h % 2, kt, :], kt == 0, kt == 2)
                close(last)
            pe.wait_ge(sem("act_squares"), 3)
            for k in range(4):
                sum_squares("oss", k, k, k + 1)

            def filter_layer(k):
                o = open_tile("mlp", k)
                if k:
                    pe.wait_ge(sem("sin_ready"), k)
                close(mm(o[0:64, 0:T], fw23[:, k - 1, :] if k else fw1[:], harg[0:64, 3, :] if k else zpos[:]))

            pe.wait_ge(sem("filter_in"), 64)
            pe.wait_ge(sem("cat_ready"), 4)
            filter_layer(0)
            pe.wait_ge(sem("cat_ready"), 8)
            for b in range(4):
                linear("wo", 2 * b, B_WO + b, cat)
                if b:
                    add_squares("ss2", "squares2", 2 * b - 2, 2)
            add_squares("ss2", "squares2", 6, 2)
            filter_layer(1)
            base = NUMBER[("gate", 0)]
            for n in range(base - 8, base):
                g, j = ORDER[n]
                pe.wait_ge(used(g), j + 1)

            def swiglu_columns(i, c):
                for part in range(2):
                    n = B_FF + 2 * c + part
                    pe.wait_ge(sem("ring_split"), 2 * c + part + 1 + 4 * i)
                    w_hi_, w_lo_ = split_block(n)
                    for j in range(2):
                        pe.wait_ge(used(("gate", "up")[part]), 4 * i + 2 * c + j + 1)
                        o = ps[(base + 4 * c + 2 * part + j) % 8]
                        for k in range(KT):
                            if c == 0 and part == 0 and j == 0:
                                pe.wait_ge(sem("xn2_ready"), k + 1)
                            m = slice(P * j, P * j + P)
                            last = product(o[:, 0:T], w_hi_[:, k, m], w_lo_[:, k, m], (xn_hi[:, k, :], xn_lo[:, k, :]), k == 0, k == KT - 1)
                        close(last)

            with pe.Fori(0, 5) as i:
                swiglu_columns(i, 0)
                swiglu_columns(i, 1)
            swiglu_columns(5, 0)
            filter_layer(2)
            for b in range(4):
                for half in range(2):
                    n = B_DN + 2 * b + half
                    pe.wait_ge(sem("ring_split"), n - B_FF + 1)
                    w_hi_, w_lo_ = split_block(n, 11)
                    if half == 0:
                        o2 = [open_tile("down", 2 * b + j) for j in range(2)]
                    for j in range(2):
                        for k in range(11):
                            if b == 0 and j == 0:
                                pe.wait_ge(sem("ffh_ready"), 11 * half + k + 1)
                            m = slice(P * j, P * j + P)
                            last = product(o2[j][:, 0:T], w_hi_[:, k, m], w_lo_[:, k, m], (ffh_hi[:, 11 * half + k, :], ffh_lo[:, 11 * half + k, :]),
                                           half == 0 and k == 0, half == 1 and k == 10)
                        if half:
                            close(last)
                    if half == 0:
                        last.then_inc(sem("half_done"), 1)
                if b:
                    add_squares("ss3", "squares3", 2 * b - 2, 2)
            add_squares("ss3", "squares3", 6, 2)
            pe.wait_ge(sem("sin_ready"), 3)
            pe.wait_ge(sem("window_in"), 32)
            for k in range(12):
                t0, n = TOKS[k // 4]
                o = open_tile("kt", k)
                close(mm(o[0:n, :], harg[0:64, 3, t0:t0 + n], fw4[0:64, 512 * (k % 4):512 * (k % 4) + 512]))
            pe.wait_ge(sem("keo_ready"), 2)
            for k in range(12):
                f0, nf = TOKS[k // 4]
                table, src = (CF, KE) if k % 4 < 2 else (SF, KO)
                o = open_tile("kspec", k)
                for tt, (t0, n) in enumerate(TOKS):
                    last = mm(o[0:nf, :], table[0:n, tt, f0:f0 + nf], src[0:n, tt, 512 * (k % 2):512 * (k % 2) + 512], tt == 0, tt == 2)
                close(last)
            pe.wait_ge(sem("kabs_sum"), 2)
            o = open_tile("kn", 0)
            for c in range(KT):
                for tt, (t0, n) in enumerate(TOKS):
                    last = mm(o[:, c:c + 1], kfb[0:n, tt, P * c:P * c + P], ones[0:n, 0:1], tt == 0, tt == 2)
            close(last)
            pe.wait_ge(sem("xn3_ready"), KT)
            base_hy = NUMBER[("hy", 0)]
            for n in range(base_hy - 8, base_hy):
                g, j = ORDER[n]
                pe.wait_ge(used(g), j + 1)
            with pe.Fori(0, 3) as i:
                for b in range(4):
                    n = B_HY + b
                    pe.wait_ge(slot_in[n % RING], 16 * (n // RING + 1) + 16 * i)
                    w = slot(n)
                    for j in range(2):
                        pe.wait_ge(used("hy"), 8 * i + 2 * b + j + 1)
                        o = ps[(base_hy + 2 * b + j) % 8]
                        for k in range(KT):
                            last = mm(o[:, 0:T], w[:, k, P * j:P * j + P], xn[:, k, :], k == 0, k == KT - 1)
                        close(last)
            pe.wait_ge(sem("v_ready"), 1)
            for k in range(6):
                t0, n = TOKS[k // 2]
                o = open_tile("vx", k)
                for c in range(4):
                    last = turn(o[0:n, P * c:P * c + P], hyc[:, 8 + 4 * (k % 2) + c, t0:t0 + n])
                close(last)
            pe.wait_ge(used("vx"), 6)
            for k in range(12):
                f0, nf = TOKS[k // 4]
                half = k // 2 % 2
                o = open_tile("vspec", k)
                for tt, (t0, n) in enumerate(TOKS):
                    last = mm(o[0:nf, :], (CF, SF)[k % 2][0:n, tt, f0:f0 + nf], vtok[0:n, tt, 512 * half:512 * half + 512], tt == 0, tt == 2)
                close(last)
            pe.wait_ge(sem("spec_ready"), 12)
            for j in range(8):
                o = open_tile("inv", j)
                for tt, (f0, nf) in enumerate(TOKS):
                    mm(o[:, 0:SEQ], YR[0:nf, tt, P * j:P * j + P], CI[0:nf, tt, :], tt == 0, False)
                    last = mm(o[:, 0:SEQ], YI[0:nf, tt, P * j:P * j + P], SI[0:nf, tt, :], False, tt == 2)
                close(last)
            for b in range(4):
                linear("ho", 2 * b, B_HO + b, xn, SEQ, coming=sem("yh_ready") if b == 0 else None)
                if b:
                    add_squares("ss4", "squares4", 2 * b - 2, 2, slice(META, T))
            add_squares("ss4", "squares4", 6, 2, slice(META, T))
            pe.wait_ge(sem("router_in"), 16)
            o = open_tile("logit", 0)
            for tt in range(2):
                for k in range(KT):
                    if tt == 0:
                        pe.wait_ge(sem("xn4_ready"), k + 1)
                    last = mm(o[:, NE * tt:NE * tt + NE], xn[:, k, P * tt:P * tt + P], router[:, k, :], k == 0, k == KT - 1)
            close(last)
            for k in range(4):
                o = open_tile("xk", k)
                for c in range(4):
                    last = turn(o[:, P * c:P * c + P], xn[:, 4 * (k % 2) + c, P * (k // 2):P * (k // 2) + P])
                close(last)
            pe.wait_ge(sem("pick_ready"), 1)
            o = open_tile("pos", 0)
            pick = rt[:, 64:80]
            for tt in range(2):
                for st in range(2):
                    mm(o[:, NE * tt:NE * tt + NE], US[:, st, P * tt:P * tt + P], pick[:, NE * st:NE * st + NE], st == 0, st == 1)
            for st in range(2):
                last = mm(o[:, 16:24], ones[:], pick[:, NE * st:NE * st + NE], st == 0, st == 1)
            close(last)
            def columns(part, n, p):
                pe.wait_ge(sem(f"{part}_split"), n + 1)
                at = "gud".index(part)
                w = [a[:, p, at, :].rearrange("p (k n) -> p k n", k=KT) for a in (w_hi, w_lo)]
                for k in range(KT):
                    last = product(ps[p][:, 256 * at:256 * at + 256], xg_hi[:, k, :], xg_lo[:, k, :], [a[:, k, :] for a in w], k == 0, k == KT - 1)
                last.then_inc(sem(f"{part}_used"), 1)

            def turn_hidden(n, p):
                pe.wait_ge(sem("h_ready"), n + 1)
                for j in range(2):
                    last = turn(ps[2 + p][:, P * j:P * j + P], eh[:, p, P * j:P * j + P])
                last.then_inc(sem("turned"), 1)

            def down(n, p, end=False):
                pe.wait_ge(sem("d_split"), n + 1)
                pe.wait_ge(sem("eh_split"), n + 1)
                w = [a[:, p, 2, :].rearrange("p (k n) -> p k n", k=2) for a in (w_hi, w_lo)]
                for half in range(2):
                    for j in range(2):
                        last = product(ps[4 + half][:, :], eh_hi[:, p, j, :], eh_lo[:, p, j, :],
                                       [a[:, j, 512 * half:512 * half + 512] for a in w], False, end and j == 1)
                last.then_inc(sem("d_used"), 1)

            def add_result(i, c):
                if c >= 2:
                    pe.wait_ge(sem("comb_used"), 4 * i - 4 + c - 1)
                for d in range(2):
                    last = mm(ps[6 + c % 2][:, SEQ * d:SEQ * d + SEQ], ye[:, P * (2 * c + d):P * (2 * c + d) + P], GT[:])
                last.then_inc(sem("comb_ready"), 1)

            def item(i, first=False):
                if not first:
                    turn_hidden(14 * i - 1, 1)
                pe.wait_ge(sem("sel_ready"), 2 * i + 2)
                for d in range(KT):
                    for tt in range(2):
                        last = mm(ps[6 + d // 4][:, CAP * (d % 4):CAP * (d % 4) + CAP], xtk[:, tt, P * d:P * d + P], SEL[:, tt, :], tt == 0, tt == 1)
                    if d % 4 == 3:
                        last.then_inc(sem("gather_ready"), 1)
                if not first:
                    down(14 * i - 1, 1, end=True)
                pe.wait_ge(sem("xg_split"), 2 * i + 2)
                columns("g", 14 * i, 0)
                columns("u", 14 * i, 0)
                if not first:
                    pe.wait_ge(sem("ye_dve"), i)
                    pe.wait_ge(sem("ye_act"), i)
                    pe.wait_ge(sem("gt_ready"), i)
                    add_result(i, 0)
                    add_result(i, 1)
                columns("g", 14 * i + 1, 1)
                turn_hidden(14 * i, 0)
                columns("u", 14 * i + 1, 1)
                if not first:
                    add_result(i, 2)
                    add_result(i, 3)
                for bank in (4, 5):
                    nc.tensor.matmul(ps[bank][:, :], zero16[:, 0:CAP], zero16[:], start=True, stop=False)
                down(14 * i, 0)
                with pe.Fori(0, STAGES // 2 - 1) as q:
                    for p in range(2):
                        n = 14 * i + 2 * q + 2 + p
                        columns("g", n, p)
                        turn_hidden(n - 1, 1 - p)
                        columns("u", n, p)
                        down(n - 1, 1 - p)
                pe.wait_ge(sem("selg_ready"), 2 * i + 2)
                for tt in range(2):
                    last = turn(ps[2][:, SEQ + P * tt:SEQ + P * tt + P], SELG[:, tt, :])
                last.then_inc(sem("gt_turned"), 1)

            pe.wait_ge(used("logit"), 1)
            pe.wait_ge(used("pos"), 1)
            pe.wait_ge(used("xk"), 4)
            item(0, True)
            with pe.Fori(1, NE) as i:
                item(i)
            pe.wait_ge(sem("later_table"), 1)
            more = pe.value_load(tab[0:1, 0:1], min_val=0, max_val=LATER)
            with pe.If(more > 0):
                with pe.Fori(0, more) as j:
                    item(j + NE)
            turn_hidden(14 * more + (14 * NE - 1), 1)
            down(14 * more + (14 * NE - 1), 1, end=True)
            i = more + NE
            pe.wait_ge(sem("ye_dve"), i)
            pe.wait_ge(sem("ye_act"), i)
            pe.wait_ge(sem("gt_ready"), i)
            for c in range(4):
                add_result(i, c)
            pe.wait_ge(sem("final_squares"), 1)
            for k in range(KT):
                last = mm(ps[0][:, 0:SEQ], ones[:], sq[:, k, 0:SEQ], k == 0, k == KT - 1)
            last.then_inc(sem("final_ss"), 1)
            pe.wait_ge(sem("final_xn"), KT)
            for k in range(4):
                for c in range(4):
                    last = turn(ps[1 + k][:, P * c:P * c + P], xn[:, 4 * (k % 2) + c, P * (k // 2):P * (k // 2) + P])
                last.then_inc(sem("final_turn"), 1)


_INS = ["x", "meta_tokens", "norm_mix_even", "w_in_ab", "ssd_conv_w", "ssd_conv_b", "ssd_a_log", "ssd_dt_bias", "ssd_d",
        "ssd_norm_w", "diff_lambda", "diff_subln_w", "w_out_ab", "norm_ffn_even", "ffn_w_gate", "ffn_w_up", "ffn_w_down",
        "norm_mix_odd", "hy_w_in", "hy_b_in", "hy_conv_w", "hy_conv_b", "hy_f_w1", "hy_f_b1", "hy_f_w2", "hy_f_b2",
        "hy_f_w3", "hy_f_b3", "hy_f_w4", "hy_f_freq", "hy_skip", "hy_w_out", "hy_b_out", "norm_ffn_odd", "moe_router",
        "moe_w_gate", "moe_w_up", "moe_w_down", "final_norm"]


def kernel(**inputs):
    import numpy as _np
    import concourse.bacc as _bacc
    from concourse import mybir as _mybir
    from concourse.bass_utils import run_bass_kernel_spmd as _run

    nc = _bacc.Bacc("TRN2", target_bir_lowering=False, num_devices=1)
    arrays, args = {}, {}
    given = {name: _np.ascontiguousarray(inputs[name]) for name in _INS}
    for name, a in list(given.items()) + list(shape_constants().items()):
        arrays[f"in_{name}_dram"] = a
        args[name] = nc.dram_tensor(f"in_{name}_dram", a.shape, _mybir.dt.from_np(a.dtype), kind="ExternalInput").ap()
    out = nc.dram_tensor("out_0_dram", (1, SEQ, D), _mybir.dt.float32, kind="ExternalOutput").ap()
    trunk(nc, args, out)
    r = _run(nc, [arrays], core_ids=[0])
    return r.results[0]["out_0_dram"]
```

```python
from contextlib import ExitStack
import math

import numpy as np

import concourse.bass as bass
from concourse import mybir

F32 = mybir.dt.float32
F32R = mybir.dt.float32r
BF16 = mybir.dt.bfloat16
I32 = mybir.dt.int32
ALU = mybir.AluOpType
ACT = mybir.ActivationFunctionType
AX = mybir.AxisListType

P = 128
D = 1024
KT = D // P
SEQ = 256
META = 16
T = SEQ + META
TOKS = [(0, P), (P, P), (2 * P, T - 2 * P)]
EPS = 1e-5
HEADS = 8
CONV = 5
ATT = 4
FF = 2816
FFT = FF // P
FEXP = 3584
NE = 8
HY = 3 * D
SHORT = 3
RING = 4
SLOT = 11 * 256
CAP = 128
STAGES = FEXP // 256
LATER = 2 * SEQ // (CAP + 1)
ITEMS = NE + LATER
LAMBDA_INIT = 0.8 - 0.6 * math.exp(-0.3 * 0)
TWO_PI_A = 6.28125
TWO_PI_B = 2.0 * math.pi - TWO_PI_A
ROUND = 12582912.0

C_NME, C_CW, C_CB, C_SNW, C_SUB, C_NFE, C_NMO, C_BIN, C_SKIP, C_BOUT, C_A = 0, 8, 48, 56, 60, 61, 69, 77, 101, 109, 117
C_HCW, C_HCB, C_NFO, C_FIN, C_B = 128, 200, 224, 232, 240
C_FV = 256

K_SIZES = [("ident", P), ("perm", P), ("cos", T), ("sin", T), ("uf", 3 * T), ("ub", 3 * T), ("cf", 3 * T), ("sf", 3 * T),
           ("ci", 3 * SEQ), ("si", 3 * SEQ), ("us", 2 * SEQ), ("iota", CAP), ("tri", NE * NE),
           ("nth", LATER * NE), ("expert", LATER * NE)]
K_AT = {}
_at = 0
for _name, _n in K_SIZES:
    K_AT[_name] = (_at, _n)
    _at += _n
K_ALL = _at
K_FIRST = K_AT["uf"][0]


def shape_constants():
    f32 = np.float32
    c = np.zeros((P, K_ALL), f32)

    def put(name, a):
        at, n = K_AT[name]
        c[:a.shape[0], at:at + n] = a.reshape(a.shape[0], n)

    def tiles(a):
        out = np.zeros((3, P) + a.shape[1:], f32)
        out.reshape((3 * P,) + a.shape[1:])[:a.shape[0]] = a
        return out.transpose(1, 0, 2)

    put("ident", np.eye(P, dtype=f32))
    perm = np.zeros((P, P), f32)
    cos = np.ones((P, T), f32)
    sin = np.zeros((P, T), f32)
    pos = np.arange(T, dtype=f32)
    inv = (f32(500000.0) ** (-np.arange(0, 16, 2, dtype=f32) / f32(16))).astype(f32)
    ang = pos[:, None] * inv[None, :]
    for base in (0, 64):
        for i in range(8):
            perm[base + 8 + i, base + i] = -1.0
            perm[base + i, base + 8 + i] = 1.0
            cos[base + i] = cos[base + 8 + i] = np.cos(ang[:, i])
            sin[base + i] = sin[base + 8 + i] = np.sin(ang[:, i])
    put("perm", perm)
    put("cos", cos)
    put("sin", sin)
    j, i = np.arange(T)[:, None], np.arange(T)[None, :]
    put("uf", tiles((j <= i).astype(f32)))
    put("ub", tiles((j >= i).astype(f32)))
    w = 2.0 * np.pi * ((np.arange(T)[None, :] + 0.5) * np.arange(T)[:, None]) / (2 * T)
    put("cf", tiles(np.cos(w).astype(f32)))
    put("sf", tiles(np.sin(w).astype(f32)))
    put("ci", tiles((np.cos(w[META:]).T / T).astype(f32)))
    put("si", tiles((np.sin(w[META:]).T / T).astype(f32)))
    us = (np.arange(SEQ)[:, None] < np.arange(SEQ)[None, :]).astype(f32)
    put("us", us.reshape(2, P, SEQ).transpose(1, 0, 2))
    put("iota", np.tile(np.arange(CAP, dtype=f32), (P, 1)))
    put("tri", np.tile((np.arange(NE)[:, None] > np.arange(NE)[None, :]).astype(f32).reshape(1, -1), (P, 1)))
    put("nth", np.tile(np.repeat(np.arange(LATER), NE).astype(f32), (P, 1)))
    put("expert", np.tile(np.tile(np.arange(NE), LATER).astype(f32), (P, 1)))
    sel8 = np.repeat(np.eye(HEADS, dtype=f32), P, axis=1)
    t = pos / f32(T - 1)
    bands = np.linspace(1e-4, 15, 16, dtype=f32)
    ang = (f32(2.0 * math.pi) * pos / f32(T))[:, None] * bands[None, :]
    zpos = np.ascontiguousarray(np.concatenate([t[:, None], np.cos(ang), -np.sin(ang)], axis=-1).T.astype(f32))
    lo, hi = math.log(1e-2) / 1.5, math.log(1e-2) / 0.3
    deltas = np.abs(np.linspace(lo, hi, D, dtype=f32))
    window = (np.exp(-t[:, None] * deltas[None, :]) + f32(0.05)).astype(f32)
    return {"k_table": c, "k_sel8": sel8, "k_zpos": zpos, "k_window": np.ascontiguousarray(tiles(window))}


class Steps:

    def __init__(self, eng, chain):
        self.eng, self.chain, self.count, self.i, self.per = eng, chain, {}, None, {}

    def __call__(self, ins, sem=None):
        sem = self.chain if sem is None else sem
        ins.then_inc(sem, 1)
        n = self.count[id(sem)] = self.count.get(id(sem), 0) + 1
        self.eng.wait_ge(sem, n if self.i is None or id(sem) not in self.per else self.per[id(sem)] * self.i + n)

    def credit(self, sem, n):
        self.count[id(sem)] = self.count.get(id(sem), 0) + n

    def loop(self, i, per):
        self.i, self.per = i, {id(s): k for s, k in per}
        self.start = dict(self.count)

    def end(self, times):
        for s, k in self.per.items():
            assert self.count.get(s, 0) - self.start.get(s, 0) == k, (self.count.get(s, 0), self.start.get(s, 0), k)
            self.count[s] = self.start.get(s, 0) + k * times
        self.i = None


def tile_order():
    order = []

    def add(group, first, n=1):
        order.extend((group, k) for k in range(first, first + n))

    add("xin", 0, 5)
    add("param", 0)
    add("ss1", 0)
    add("proj", 0, 4)
    add("dt", 0)
    add("proj", 4, 8)
    add("cs", 0, 3)
    add("xs", 0, 3)
    add("cb", 0, 6)
    for s in range(10):
        if s < 8:
            add("row", 2 * s, 2)
        if s < 6:
            add("proj", 12 + 2 * s, 2)
        if s >= 3 and s % 2 == 1:
            add("y", (s - 3) // 2)
    add("rope", 0, 8)
    add("gss", 0, 2)
    add("vt", 0, 3)
    add("score", 0, 6)
    for h in range(ATT):
        if h + 1 < ATT:
            add("score", 6 * h + 6, 6)
        add("at", 3 * h, 3)
        add("o", h)
    add("oss", 0, 4)
    add("mlp", 0)
    add("wo", 0, 4)
    add("mlp", 1)
    add("wo", 4, 4)
    add("ss2", 0)
    for b in range(FFT // 2):
        add("gate", 2 * b, 2)
        add("up", 2 * b, 2)
    add("mlp", 2)
    add("down", 0, 8)
    add("ss3", 0)
    add("kt", 0, 12)
    add("kspec", 0, 12)
    add("kn", 0)
    add("hy", 0, 24)
    add("vx", 0, 6)
    add("vspec", 0, 12)
    add("inv", 0, 8)
    add("ho", 0, 8)
    add("ss4", 0)
    add("xk", 0, 2)
    add("logit", 0)
    add("xk", 2, 2)
    add("pos", 0)
    return order


ORDER = tile_order()
NUMBER = {key: n for n, key in enumerate(ORDER)}
CREDIT = {"hy": 8, "gate": 4, "up": 4}


def trunk(nc, A, out):
    ctx = ExitStack()
    with ctx:
        sems = {}

        def sem(name):
            if name not in sems:
                sems[name] = ctx.enter_context(nc.semaphore(name))
            return sems[name]

        def sb(name, shape, dt=F32):
            return ctx.enter_context(nc.sbuf_tensor(name, shape, dt))

        ps = [ctx.enter_context(nc.psum_tensor(f"ps{i}", [P, 512], F32)) for i in range(8)]

        hT = sb("hT", [P, KT, T])
        xn = sb("xn", [P, KT, T])
        sq = sb("sq", [P, KT, T])
        rstd = sb("rstd", [P, T])
        ktab = sb("ktab", [P, K_ALL])
        sel8 = sb("sel8", [HEADS, HEADS * P])
        zpos = sb("zpos", [33, T])
        prow = sb("prow", [P, 3, P])
        par = sb("par", [P, 264])
        ones = sb("ones", [P, P])
        eps = sb("eps", [P, 1])
        bcast = sb("bcast", [P, 16 + 16 + 256 + 16 + 4])
        lam = sb("lam", [P, 8])
        wdt = sb("wdt", [P, KT, 16])
        fw1 = sb("fw1", [33, 64])
        fw23 = sb("fw23", [64, 2, 64])
        router = sb("router", [P, KT, NE])
        crd = sb("crd", [P, 16])
        zero16 = sb("zero16", [P, 512], BF16)
        tabf = sb("tabf", [1, 16])
        tab = sb("tab", [1, 16], I32)
        arena_n = 25344
        with ExitStack() as early:
            arena = early.enter_context(nc.sbuf_tensor("arena", [P, arena_n], F32))
            ring = early.enter_context(nc.sbuf_tensor("ring", [P, RING, SLOT], F32))

        def overlay(name, at, *dims):
            with ExitStack() as early:
                if at:
                    early.enter_context(nc.sbuf_tensor(name + "_at", [P, at], F32))
                return early.enter_context(nc.sbuf_tensor(name, [P] + list(dims), F32R))

        ring_hi, ring_lo = overlay("ring_hi", 13600, 2, SLOT), overlay("ring_lo", arena_n, RING, SLOT)
        ring_hi2 = overlay("ring_hi2", 14864, 2, 256 * KT)
        ffh_hi, ffh_lo = overlay("ffh_hi", 0, FFT, T), overlay("ffh_lo", 5984, FFT, T)
        xn_hi, xn_lo = overlay("xn_hi", 19232, KT, T), overlay("xn_lo", 21408, KT, T)
        with ExitStack() as early:
            raw = early.enter_context(nc.sbuf_tensor("raw", [P, 2, 3, 2048], F32))
        w_lo = sb("w_lo", [P, 2, 3, 2048], F32R)
        w_hi = sb("w_hi", [P, 2, 3, 2048], F32R)
        xg_hi = sb("xg_hi", [P, KT, CAP], F32R)
        xg_lo = sb("xg_lo", [P, KT, CAP], F32R)
        eh_hi = sb("eh_hi", [P, 2, 2, CAP], F32R)
        eh_lo = sb("eh_lo", [P, 2, 2, CAP], F32R)
        xtk_hi = sb("xtk_hi", [P, 2, D], F32R)
        xtk_lo = sb("xtk_lo", [P, 2, D], F32R)
        ye = sb("ye", [P, D])
        esg = sb("esg", [P, 2, 256])
        eh = sb("eh", [P, 2, 256])
        SEL = sb("SEL", [P, 2, CAP], F32R)
        SELG = sb("SELG", [P, 2, CAP])
        GT = sb("GT", [P, SEQ])
        rt = sb("rt", [P, 528])
        xtk = sq[:].rearrange("p k t -> p (k t)")[:, 0:2 * D].rearrange("p (t d) -> p t d", t=2)
        osb2 = raw[:, 0, 0, :].rearrange("p (t d) -> p t d", t=2)

        def const(name, *dims):
            at, n = K_AT[name]
            a = ktab[:, at:at + n]
            return a.rearrange("p (a b) -> p a b", a=dims[0]) if dims else a

        ident, perm, cosT, sinT = const("ident"), const("perm"), const("cos"), const("sin")
        UF, UB, CF, SF = (const(n, 3) for n in ("uf", "ub", "cf", "sf"))
        CI, SI, US = const("ci", 3), const("si", 3), const("us", 2)
        iota, tri, nth, expert = const("iota"), const("tri", NE), const("nth", LATER), const("expert", LATER)
        dt_bias, a_log, lam_in = bcast[:, 0:16], bcast[:, 16:32], bcast[:, 32:288]
        d_in, dskip = bcast[:, 288:304], bcast[:, 304:308]

        def area(at, a, b=None, c=None):
            n = a * (b or 1) * (c or 1)
            assert at + n <= arena_n, (at, n)
            v = arena[:, at:at + n]
            if c:
                return v.rearrange("p (a b c) -> p a b c", a=a, b=b)
            return v.rearrange("p (a b) -> p a b", a=a) if b else v

        xp = area(0, 8, T + 4)
        xbc = area(2208, 8, T)
        zs = area(4384, 4, T)
        qk = area(5472, 8, T)
        vf = area(7648, 4, T)
        xT = area(8736, 3, 512)
        vT = area(0, 3, 512)
        CB = area(10272, 6, T)
        M = area(11904, 4, 3, T)
        RB = area(15168, 2, 3, T)
        W = area(16800, 2, 3, T)
        W1 = area(18432, 2, 3, T)
        cat = area(20064, 8, T)
        ysb = area(22240, 4, T)
        dtw = area(23328, 8, 48)
        csr = area(23712, 2, T)
        convt = area(24256, 2, T)
        ropet = area(24800, 2, T)
        xtok = area(11904, 2, D)
        mtok = area(13952, D)
        pr = area(11904, 2, 2, T)
        at_ = area(12992, 2, 3, T)
        aT = area(14624, 2, 3, T)
        osb = area(16256, 4, T)
        stat = area(17344, 24, 4)
        sg = area(11968, 4, T)
        ffp = area(13056, 2, T)
        KR = area(0, 3, D)
        KI = area(3072, 3, D)
        kfb = area(6144, 3, 2 * D)
        KE = area(12288, 3, D)
        KO = area(15360, 3, D)
        win = area(19232, 3, D)
        fw4 = xn[:].rearrange("p k t -> p (k t)")[:, 0:2 * D]
        harg = area(24256, 4, T)
        hyc = area(6144, 24, T)
        pad = area(12672, 8, T + 2)
        vtok = area(14864, 3, D)
        YR = area(17936, 3, D)
        YI = area(21008, 3, D)
        prod = area(12672, 4, 512)
        invn = area(24080, 8)
        ytmp = area(24088, 2, SEQ)
        def ready(eng, group, k):
            n = NUMBER[(group, k)]
            eng.wait_ge(sem("tile_ready"), n + 1)
            return ps[n % 8]

        def used(group):
            return sem("used_" + group)

        block = ctx.enter_context(nc.Block())

        w_in = A["w_in_ab"][0].rearrange("(k p) n -> p k n", p=P)
        stream = []
        for c in [512 + 256 * b for b in range(4)] + [0, 256] + [1552 + 256 * b for b in range(6)]:
            stream.append((w_in[:, :, c:c + 256], KT))
        w_out = A["w_out_ab"][0].rearrange("(k p) n -> p k n", p=P)
        for b in range(4):
            stream.append((w_out[:, :, 256 * b:256 * b + 256], KT))
        wg0 = A["ffn_w_gate"][0].rearrange("(k p) n -> p k n", p=P)
        wu0 = A["ffn_w_up"][0].rearrange("(k p) n -> p k n", p=P)
        for b in range(FFT // 2):
            stream.append((wg0[:, :, 256 * b:256 * b + 256], KT))
            stream.append((wu0[:, :, 256 * b:256 * b + 256], KT))
        wd0 = A["ffn_w_down"][0].rearrange("(k p) n -> p k n", p=P)
        for b in range(4):
            for half in range(2):
                stream.append((wd0[:, 11 * half:11 * half + 11, 256 * b:256 * b + 256], 11))
        hwi = A["hy_w_in"][0].rearrange("(k p) n -> p k n", p=P)
        for c in [D + 256 * b for b in range(8)] + [256 * b for b in range(4)]:
            stream.append((hwi[:, :, c:c + 256], KT))
        hwo = A["hy_w_out"][0].rearrange("(k p) n -> p k n", p=P)
        for b in range(4):
            stream.append((hwo[:, :, 256 * b:256 * b + 256], KT))
        B_WO, B_FF, B_DN, B_HY, B_HO = 12, 16, 38, 46, 58

        def last_tile(n):
            if n < B_WO:
                return ("proj", 2 * n + 1)
            if n < B_FF:
                return ("wo", 2 * (n - B_WO) + 1)
            if n < B_DN:
                b = n - B_FF
                return ("up" if b % 2 else "gate", b // 2 * 2 + 1)
            if n < B_HY:
                return ("down", (n - B_DN) // 2 * 2 + (n - B_DN) % 2)
            return ("hy", 2 * (n - B_HY) + 1) if n < B_HO else ("ho", 2 * (n - B_HO) + 1)

        slot_in = [sem(f"slot{i}_in") for i in range(RING)]

        def slot(n, k=KT):
            return ring[:, n % RING, 0:k * 256].rearrange("p (k n) -> p k n", k=k)

        moe = {n: A[n] for n in ("moe_w_gate", "moe_w_up", "moe_w_down")}

        @block.sync
        def _(sp):
            rows = [(0, C_NME, A["norm_mix_even"].rearrange("e (t p) -> (e t) p", p=P)),
                    (0, C_CW, A["ssd_conv_w"].rearrange("e k (t p) -> (e k t) p", p=P)),
                    (0, C_CB, A["ssd_conv_b"].rearrange("e (t p) -> (e t) p", p=P)),
                    (0, C_SNW, A["ssd_norm_w"].rearrange("e (t p) -> (e t) p", p=P)),
                    (0, C_SUB, A["diff_subln_w"]),
                    (0, C_NFE, A["norm_ffn_even"].rearrange("e (t p) -> (e t) p", p=P)),
                    (0, C_NMO, A["norm_mix_odd"].rearrange("e (t p) -> (e t) p", p=P)),
                    (0, C_BIN, A["hy_b_in"][:, D:].rearrange("e (t p) -> (e t) p", p=P)),
                    (0, C_BIN + 16, A["hy_b_in"][:, 0:D].rearrange("e (t p) -> (e t) p", p=P)),
                    (0, C_SKIP, A["hy_skip"].rearrange("e (t p) -> (e t) p", p=P)),
                    (0, C_BOUT, A["hy_b_out"].rearrange("e (t p) -> (e t) p", p=P)),
                    (1, C_HCB - P, A["hy_conv_b"][:, D:].rearrange("e (t p) -> (e t) p", p=P)),
                    (1, C_HCB - P + 16, A["hy_conv_b"][:, 0:D].rearrange("e (t p) -> (e t) p", p=P)),
                    (1, C_NFO - P, A["norm_ffn_odd"].rearrange("e (t p) -> (e t) p", p=P)),
                    (1, C_FIN - P, A["final_norm"].rearrange("(t p) -> t p", p=P))]
            for k in range(SHORT):
                rows.append((1, 24 * k, A["hy_conv_w"][0, k:k + 1, D:].rearrange("e (t p) -> (e t) p", p=P)))
                rows.append((1, 24 * k + 16, A["hy_conv_w"][0, k:k + 1, 0:D].rearrange("e (t p) -> (e t) p", p=P)))
            for which, at, src in rows:
                sp.dma_start(prow[at:at + src.shape[0], which, :], src).then_inc(sem("param_in"), 16)
            for k, name in enumerate(("hy_f_b1", "hy_f_b2", "hy_f_b3")):
                sp.dma_start(prow[k:k + 1, 2, 0:64], A[name]).then_inc(sem("param_in"), 16)
            sp.dma_start(prow[3:6, 2, 0:64], A["hy_f_freq"][0]).then_inc(sem("param_in"), 16)
            assert len(rows) + 4 == 25
            sp.wait_ge(sem("x_in"), 32)
            sp.wait_ge(sem("param_in"), 16 * 25)
            for n, (src, k) in enumerate(stream):
                if n >= RING:
                    sp.wait_ge(sem("tile_ready"), NUMBER[last_tile(n - RING)] + 1)
                if n == B_DN + 4:
                    sp.dma_start(win, A["k_window"]).then_inc(sem("window_in"), 16)
                    sp.wait_ge(sem("xn2_ready"), KT)
                    sp.dma_start(fw4[0:64, :], A["hy_f_w4"][0]).then_inc(sem("window_in"), 16)
                sp.dma_start(slot(n, k), src).then_inc(slot_in[n % RING], 16)
            sp.wait_ge(sem("hyena_done"), 1)

            def load(part, i, e, q, p, wait):
                if wait:
                    sp.wait_ge(sem(f"{part}_used"), 14 * i + 2 * q + p - 1)
                c = bass.ds(512 * q + 256 * p, 256)
                name = {"g": "moe_w_gate", "u": "moe_w_up", "d": "moe_w_down"}[part]
                src = moe[name][0, bass.ds(e, 1), c, :] if part == "d" else moe[name][0, bass.ds(e, 1), :, c]
                at = "gud".index(part)
                dst = raw[:, p, at, :].rearrange("p (k n) -> p k n", k=2 if part == "d" else KT)
                sp.dma_start(dst, src.rearrange("e (k p) n -> p (e k) n", p=P)).then_inc(sem(f"{part}_in{p}"), 16)

            def item(i, e, first=False):
                for p in range(2):
                    load("g", i, e, 0, p, not first)
                    load("u", i, e, 0, p, not first)
                load("d", i, e, 0, 0, not first)
                load("g", i, e, 1, 0, True)
                load("u", i, e, 1, 0, True)
                load("d", i, e, 0, 1, not first)
                load("g", i, e, 1, 1, True)
                load("u", i, e, 1, 1, True)
                load("d", i, e, 1, 0, True)
                with sp.Fori(0, STAGES // 2 - 2) as q:
                    load("g", i, e, q + 2, 0, True)
                    load("u", i, e, q + 2, 0, True)
                    load("d", i, e, q + 1, 1, True)
                    load("g", i, e, q + 2, 1, True)
                    load("u", i, e, q + 2, 1, True)
                    load("d", i, e, q + 2, 0, True)
                load("d", i, e, STAGES // 2 - 1, 1, True)

            item(0, 0, True)
            with sp.Fori(1, NE) as i:
                item(i, i)
            sp.wait_ge(sem("later_table"), 1)
            more = sp.value_load(tab[0:1, 0:1], min_val=0, max_val=LATER)
            with sp.If(more > 0):
                with sp.Fori(0, more) as j:
                    e = sp.value_load(tab[0:1, bass.ds(j + 1, 1)], min_val=0, max_val=NE - 1)
                    item(j + NE, e)
            for half, name in enumerate(("out_ready_dve", "out_ready_act")):
                for tt in range(2):
                    sp.wait_ge(sem(name), tt + 1)
                    c = slice(512 * half, 512 * half + 512)
                    sp.dma_start(out[0, tt * P:(tt + 1) * P, c], osb2[:, tt, c]).then_inc(sem("out_done"), 16)
            sp.wait_ge(sem("out_done"), 64)

        @block.gpsimd
        def _(pool):
            g = Steps(pool, sem("pool_chain"))
            g(nc.gpsimd.memset(ones[:], 1.0), sem("pool_consts"))
            g(nc.gpsimd.memset(eps[:], EPS), sem("pool_consts"))
            g(nc.gpsimd.memset(zero16[:], 0.0), sem("pool_consts"))
            pool.wait_ge(sem("table_in"), 32)
            for h in range(HEADS):
                pool.wait_ge(sem("dt_ready"), 1)
                if h >= 2:
                    pool.wait_ge(sem("m_ready"), h - 1)
                for tt, (t0, n) in enumerate(TOKS):
                    g(nc.gpsimd.tensor_scalar(W1[0:n, h % 2, tt, :], UB[0:n, tt, :], dtw[0:n, 4, 16 * tt + 8 + h:16 * tt + 9 + h],
                                              None, ALU.mult), sem("w1_ready"))
            for j in range(4, 8):
                pool.wait_ge(used("proj"), 12 + j + 1)
                g(nc.gpsimd.tensor_tensor(cat[:, j, :], qk[:, j, :], cosT, ALU.mult), sem("k_by_cos"))
            for lt, (t0, n) in enumerate(TOKS):
                pool.wait_ge(sem("ke_ready"), lt + 1)
                g(nc.gpsimd.tensor_tensor(KO[0:n, lt, :], kfb[0:n, lt, 0:D], kfb[0:n, lt, D:2 * D], ALU.subtract), sem("ko_ready"))
            for k in range(6):
                half, ft = k // 3, k % 3
                n = TOKS[ft][1]
                c = slice(512 * half, 512 * half + 512)
                pool.wait_ge(sem("prod_ready"), 4 * k + 4)
                g(nc.gpsimd.tensor_tensor(YR[0:n, ft, c], prod[0:n, 0, :], prod[0:n, 1, :], ALU.subtract), sem("spec_ready"))
                g(nc.gpsimd.tensor_tensor(YI[0:n, ft, c], prod[0:n, 2, :], prod[0:n, 3, :], ALU.add), sem("spec_ready"))

            for k in range(4):
                pool.wait_ge(used("xk"), k + 1)
                at = (slice(None), k % 2, slice(512 * (k // 2), 512 * (k // 2) + 512))
                g(nc.gpsimd.tensor_tensor(xtk_lo[at], xtk[at], xtk_hi[at].bitcast(F32), ALU.subtract), sem("xtk_ready"))

        @block.scalar
        def _(act):
            a = Steps(act, sem("act_chain"))

            act.dma_start(ktab[:, 0:K_FIRST], A["k_table"][:, 0:K_FIRST]).then_inc(sem("ident_in"), 16)
            act.dma_start(xtok, A["x"][0].rearrange("(t p) d -> p t d", p=P)).then_inc(sem("x_in"), 16)
            act.dma_start(mtok[0:META, :], A["meta_tokens"]).then_inc(sem("x_in"), 16)
            def copy(group, k, dst, part=P, cols=slice(0, T), scale=1.0):
                t = ready(act, group, k)
                a(nc.scalar.activation(dst, t[0:part, cols], ACT.Copy, scale=scale), used(group))

            def sqrt_table():
                a(nc.scalar.activation(crd[:, 9:10], eps[:, 0:1], ACT.Sqrt))

            def root(group, k, n, cols=T, part=slice(0, P), sig="rms_ready"):
                t = ready(act, group, k)
                a(nc.scalar.activation(rstd[:, 0:cols], t[:, 0:cols], ACT.Sqrt, bias=eps[:, 0:1], scale=1.0 / n), used(group))

            def square(lo, hi, toks=slice(0, T)):
                a(nc.scalar.activation(sq[:, lo:hi, toks], hT[:, lo:hi, toks], ACT.Square), sem("act_squares"))

            for tt in range(2):
                for half in range(2):
                    t = ready(act, "xin", 2 * tt + half)
                    a(nc.scalar.activation(hT[:, 4 * half:4 * half + 4, META + P * tt:META + P * tt + P],
                                           t[:, :].rearrange("p (a b) -> p a b", a=4), ACT.Copy), used("xin"))
            t = ready(act, "xin", 4)
            a(nc.scalar.activation(hT[:, :, 0:META], t[:, 0:P].rearrange("p (a b) -> p a b", a=8), ACT.Copy), used("xin"))
            square(0, 4)
            t = ready(act, "param", 0)
            a(nc.scalar.activation(par[:, 0:C_A], t[:, 0:C_A], ACT.Copy))
            a(nc.scalar.activation(par[:, C_HCW:C_B], t[:, C_HCW:C_B], ACT.Copy))
            a(nc.scalar.activation(par[0:64, C_FV:C_FV + 6], t[0:64, C_FV:C_FV + 6], ACT.Copy), used("param"))
            act.wait_ge(sem("pool_consts"), 3)
            sqrt_table()
            root("ss1", 0, D)
            act.dma_start(wdt[:], w_in[:, :, 1536:1552]).then_inc(sem("dt_in"), 16)
            act.dma_start(dt_bias, A["ssd_dt_bias"].rearrange("e a h -> e (a h)").partition_broadcast(P)).then_inc(sem("dt_in"), 16)
            act.dma_start(a_log, A["ssd_a_log"].rearrange("e a h -> e (a h)").partition_broadcast(P)).then_inc(sem("dt_in"), 16)
            act.dma_start(lam_in, A["diff_lambda"].rearrange("e a h -> e (a h)").partition_broadcast(P)).then_inc(sem("dt_in"), 16)
            act.dma_start(d_in, A["ssd_d"].rearrange("e a h -> e (a h)").partition_broadcast(P)).then_inc(sem("dt_in"), 16)
            act.dma_start(ktab[:, K_FIRST:], A["k_table"][:, K_FIRST:]).then_inc(sem("table_in"), 16)
            act.dma_start(sel8[:], A["k_sel8"]).then_inc(sem("table_in"), 16)
            act.dma_start(zpos[:], A["k_zpos"]).then_inc(sem("filter_in"), 16)
            act.dma_start(fw1[:], A["hy_f_w1"][0]).then_inc(sem("filter_in"), 16)
            act.dma_start(fw23[:, 0, :], A["hy_f_w2"][0]).then_inc(sem("filter_in"), 16)
            act.dma_start(fw23[:, 1, :], A["hy_f_w3"][0]).then_inc(sem("filter_in"), 16)
            act.dma_start(router[:], A["moe_router"][0].rearrange("(k p) n -> p k n", p=P)).then_inc(sem("router_in"), 16)


            def ssd_silu(j):
                act.wait_ge(sem("conv_ready"), j + 1)
                a(nc.scalar.activation(xbc[:, j, :], convt[:, j % 2, :], ACT.Silu), sem("xbc_ready"))

            act.wait_ge(sem("xp_zero"), 1)
            for j in range(8):
                if j == 4:
                    act.wait_ge(sem("dt_raw"), 1)
                    act.wait_ge(sem("dt_in"), 16 * 5)
                    a(nc.scalar.activation(dtw[:, 7, 0:16], a_log, ACT.Exp))
                    a(nc.scalar.activation(dtw[:, 2, :], dtw[:, 1, :], ACT.Exp, scale=-1.0))
                    a(nc.scalar.activation(dtw[:, 3, :], dtw[:, 2, :], ACT.Ln, bias=1.0), sem("dt_log"))
                copy("proj", j, xp[:, j, 2:2 + T])
                if j >= 1:
                    ssd_silu(j - 1)
            ssd_silu(7)
            for j in range(4):
                t = ready(act, "proj", 8 + j)
                a(nc.scalar.activation(zs[:, j, :], t[:, 0:T], ACT.Silu), used("proj"))
            for k in range(2):
                copy("cs", k, csr[0:HEADS, k, :], HEADS)
            t = ready(act, "cs", 2)
            a(nc.scalar.activation(dtw[:, 6, 0:32], t[:, 0:32], ACT.Copy))
            a(nc.scalar.activation(dtw[0:META, 6, 32:48], t[0:META, 32:48], ACT.Copy), used("cs"))
            for tt, (t0, n) in enumerate(TOKS):
                copy("xs", tt, xT[0:n, tt, :], n, slice(0, 512))
            for k in range(6):
                n = TOKS[k % 3][1]
                copy("cb", k, CB[0:n, k, :], n)

            def decay_rows(h):
                for way, dst in ((0, M[:, h % 4]), (1, RB[:, h % 2])):
                    if way == 1 and h >= 2:
                        act.wait_ge(sem("decay_sum"), h - 1)
                    t = ready(act, "row", 2 * h + way)
                    for tt, (t0, n) in enumerate(TOKS):
                        a(nc.scalar.activation(dst[0:n, tt, :], t[0:n, 0:T], ACT.Relu, scale=-1.0,
                                               bias=dtw[0:n, 6, 16 * tt + 8 * way + h:16 * tt + 8 * way + h + 1]),
                          used("row") if tt == 2 else None)

            def decay_exp(h):
                act.wait_ge(sem("decay_sum"), h + 1)
                a(nc.scalar.activation(M[:, h % 4, 0:2, :], M[:, h % 4, 0:2, :], ACT.Exp, scale=-1.0))
                a(nc.scalar.activation(M[0:META, h % 4, 2, :], M[0:META, h % 4, 2, :], ACT.Exp, scale=-1.0), sem("decay_ready"))

            for s in range(9):
                if s < 8:
                    if s >= 4:
                        act.wait_ge(sem("tile_ready"), NUMBER[("y", (s - 4) // 2)] + 1)
                    decay_rows(s)
                if s < 6:
                    for j in range(12 + 2 * s, 14 + 2 * s):
                        if j < 16:
                            copy("proj", j, qk[:, j - 12, :], scale=64.0 ** -0.5)
                        elif j < 20:
                            copy("proj", j, qk[:, j - 12, :])
                        else:
                            copy("proj", j, vf[:, j - 20, :])
                if s < 8:
                    decay_exp(s)
            act.wait_ge(sem("yz_ready"), 4)
            a(nc.scalar.activation(sq[:, 0:4, :], ysb, ACT.Square), sem("act_squares"))
            for k in range(2):
                t = ready(act, "gss", k)
                a(nc.scalar.activation(sq[:, 4 + k, :], t[:, 0:T], ACT.Sqrt, bias=eps[:, 0:1], scale=1.0 / 256), used("gss"))
            for tt, (t0, n) in enumerate(TOKS):
                copy("vt", tt, vT[0:n, tt, :], n, slice(0, 512))

            act.wait_ge(sem("lam_sums"), 1)
            a(nc.scalar.activation(lam[:, 2:4], lam[:, 0:2], ACT.Exp), sem("lam_exp"))

            def exps(h):
                for tt, (t0, n) in enumerate(TOKS):
                    for m in range(2):
                        k = 6 * h + 2 * tt + m
                        act.wait_ge(sem("max_ready"), k + 1)
                        t = ready(act, "score", k)
                        if 3 * h + tt >= 2 and m == 0:
                            act.wait_ge(sem("a_ready"), 3 * h + tt - 1)
                        a(nc.scalar.activation(pr[0:n, (3 * h + tt) % 2, m, :], t[0:n, 0:T], ACT.Exp,
                                               bias=stat[0:n, k, 0:1], accum_out=stat[0:n, k, 1:2]), used("score"))

            exps(0)
            for h in range(ATT):
                if h + 1 < ATT:
                    exps(h + 1)
                for kt, (k0, n) in enumerate(TOKS):
                    copy("at", 3 * h + kt, aT[0:n, h % 2, kt, :], n)
            act.wait_ge(used("o"), ATT)
            a(nc.scalar.activation(sq[:, 0:4, :], osb, ACT.Square), sem("act_squares"))
            sqrt_table()
            for k in range(4):
                t = ready(act, "oss", k)
                a(nc.scalar.activation(sq[:, 4 + k, :], t[:, 0:T], ACT.Sqrt, bias=eps[:, 0:1], scale=1.0 / P), used("oss"))

            def filter_sine(k):
                act.wait_ge(sem("arg_ready"), k + 1)
                a(nc.scalar.activation(harg[0:64, 3, :], harg[0:64, 1, :], ACT.Sin), sem("sin_ready"))

            def squares(group, s, k, toks=slice(0, T)):
                act.wait_ge(used(group), k + 1)
                a(nc.scalar.activation(sq[:, k, toks], hT[:, k, toks], ACT.Square), sem(s))

            def ring_high(n, i=0, k=KT):
                act.wait_ge(slot_in[n % RING], 16 * (n // RING + 1) + 16 * i)
                nc.scalar.activation((ring_hi if n < B_HY else ring_hi2)[:, n % 2, 0:256 * k], ring[:, n % RING, 0:256 * k], ACT.Copy).then_inc(sem("ring_high"), 1)

            filter_sine(0)
            act.wait_ge(sem("cat_ready"), 8)
            for k in range(KT):
                if k == 4:
                    filter_sine(1)
                    sqrt_table()
                if k >= 6:
                    ring_high(B_FF + k - 6)
                squares("wo", "squares2", k)
            root("ss2", 0, D)

            def norm_high(first):
                for k in range(KT):
                    act.wait_ge(sem("xn_plain"), first + k + 1)
                    nc.scalar.activation(xn_hi[:, k, :], xn[:, k, :], ACT.Copy).then_inc(sem("xn_high"), 1)

            norm_high(0)
            base = NUMBER[("gate", 0)]
            a.credit(used("gate"), CREDIT["gate"])

            def gate(i, b):
                n = base + 4 * (b // 2) + b % 2
                act.wait_ge(sem("tile_ready"), 8 * i + n + 1)
                act.wait_ge(used("up"), 4 * i + b + 1)
                a(nc.scalar.activation(sg[:, b, :], ps[n % 8][:, 0:T], ACT.Silu), used("gate"))

            def gate_and_up(i, c, k):
                gate(i, 2 * c)
                gate(i, 2 * c + 1)
                ring_high(B_FF + 2 * c + 2, i, k)
                act.wait_ge(sem("tile_ready"), 8 * i + base + 4 * c + 4)
                ring_high(B_FF + 2 * c + 3, i, k)

            with act.Fori(0, 5) as i:
                a.loop(i, [(used("gate"), 4)])
                gate_and_up(i, 0, KT)
                gate_and_up(i, 1, KT)
                a.end(5)
            gate(5, 0)
            gate(5, 1)
            ring_high(B_DN, 0, 11)
            act.wait_ge(sem("tile_ready"), NUMBER[("up", FFT - 1)] + 1)
            ring_high(B_DN + 1, 0, 11)
            filter_sine(2)
            for d in range(8):
                if d % 2 == 0:
                    act.wait_ge(sem("half_done"), d // 2 + 1)
                else:
                    act.wait_ge(sem("tile_ready"), NUMBER[("down", d)] + 1)
                if d < 6:
                    ring_high(B_DN + d + 2, 0, 11)
                if d % 2:
                    squares("down", "squares3", d - 1)
                    squares("down", "squares3", d)
            root("ss3", 0, D)

            norm_high(KT)
            act.wait_ge(sem("ke_ready"), 3)
            act.wait_ge(sem("ko_ready"), 3)
            a(nc.scalar.activation(kfb[:, 0:2, :], kfb[:, 0:2, :], ACT.Abs))
            a(nc.scalar.activation(kfb[0:META, 2, :], kfb[0:META, 2, :], ACT.Abs), sem("kabs_ready"))
            for k in range(12):
                ft, half = k // 4, k % 2
                n = TOKS[ft][1]
                dst = KR if k % 4 < 2 else KI
                copy("kspec", k, dst[0:n, ft, 512 * half:512 * half + 512], n, slice(0, 512))

            ring_high(B_HY)
            ring_high(B_HY + 1)
            a.credit(used("hy"), CREDIT["hy"])
            base = NUMBER[("hy", 0)]
            act.wait_ge(sem("pad_zero"), 1)

            def first_tap(i, b):
                n = base + b
                act.wait_ge(sem("tile_ready"), 8 * i + n + 1)
                act.wait_ge(sem("taps_ready"), 8 * i + b + 1)
                j = 8 * i + b
                if isinstance(i, int):
                    column, o = (lambda at: par[:, at + j:at + j + 1]), hyc[:, j, :]
                else:
                    column, o = (lambda at: par[:, bass.ds(j + at, 1)]), hyc[:, bass.ds(j, 1), :].rearrange("p a t -> p (a t)")
                a(nc.scalar.activation(pad[:, b, 1:1 + T], ps[n % 8][:, 0:T], ACT.Identity, bias=column(C_BIN)), used("hy"))
                a(nc.scalar.activation(o, pad[:, b, 0:T], ACT.Identity, bias=column(C_HCB), scale=column(C_HCW)), sem("tap0_ready"))

            with act.Fori(0, 2) as i:
                a.loop(i, [(used("hy"), 8), (sem("tap0_ready"), 8)])
                for b in range(8):
                    first_tap(i, b)
                    if b % 2:
                        ring_high(B_HY + b // 2 + 2, i)
                a.end(2)
            for b in range(8):
                first_tap(2, b)
                if b in (1, 3):
                    ring_high(B_HY + b // 2 + 2, 2)
            for k in range(6):
                tt, half = k // 2, k % 2
                n = TOKS[tt][1]
                copy("vx", k, vtok[0:n, tt, 512 * half:512 * half + 512], n, slice(0, 512))

            def high(part, i, q, p):
                act.wait_ge(sem(f"{part}_in{p}"), 16 * (7 * i + q + 1))
                at = "gud".index(part)
                nc.scalar.activation(w_hi[:, p, at, :], raw[:, p, at, :], ACT.Copy).then_inc(sem(f"{part}_high"), 1)

            sqrt_table()
            for k in range(KT):
                squares("ho", "squares4", k, slice(META, T))
                if k in (5, 6):
                    high("gu"[k - 5], 0, 0, 0)
            t = ready(act, "ss4", 0)
            a(nc.scalar.activation(rstd[:, 0:SEQ], t[:, 0:SEQ], ACT.Sqrt, bias=eps[:, 0:1], scale=1.0 / D), used("ss4"))
            a(nc.scalar.activation(crd[:, 10:11], eps[:, 0:1], ACT.Exp))
            for k in range(4):
                if k == 2:
                    act.wait_ge(sem("logit_shift"), 1)
                    a(nc.scalar.activation(rt[:, 32:48], rt[:, 16:32], ACT.Exp), sem("gate_exp"))
                at = (slice(None), k % 2, slice(512 * (k // 2), 512 * (k // 2) + 512))
                a(nc.scalar.activation(xtk_hi[at], ready(act, "xk", k)[:, :], ACT.Copy))
                copy("xk", k, xtk[at], P, slice(0, 512))

            def silu(n, p):
                act.wait_ge(sem("u_used"), n + 1)
                nc.scalar.activation(esg[:, p, :], ps[p][:, 0:256], ACT.Silu).then_inc(sem("sg_ready"), 1)

            def turned_high(n, p):
                act.wait_ge(sem("turned"), n + 1)
                nc.scalar.activation(eh_hi[:, p].rearrange("p a b -> p (a b)"), ps[2 + p][:, 0:256], ACT.Copy).then_inc(sem("eh_high"), 1)

            def half_ye(i):
                act.wait_ge(sem("d_used"), 14 * i)
                nc.scalar.activation(ye[:, 512:1024], ps[5][:, :], ACT.Copy).then_inc(sem("ye_act"), 1)

            def item(i, first=False):
                if not first:
                    high("g", i, 0, 0)
                    turned_high(14 * i - 1, 1)
                    high("u", i, 0, 0)
                for half in range(2):
                    act.wait_ge(sem("gather_ready"), 2 * i + half + 1)
                    nc.scalar.activation(xg_hi[:, 4 * half:4 * half + 4, :].rearrange("p a b -> p (a b)"), ps[6 + half][:, :],
                                         ACT.Copy).then_inc(sem("xg_high"), 1)
                high("g", i, 0, 1)
                if not first:
                    half_ye(i)
                high("u", i, 0, 1)
                with act.Fori(0, STAGES // 2 - 1) as q:
                    for p in range(2):
                        silu(14 * i + 2 * q + p, p)
                        high("d", i, q, p)
                        turned_high(14 * i + 2 * q + p, p)
                        high("g", i, q + 1, p)
                        high("u", i, q + 1, p)
                silu(14 * i + 12, 0)
                high("d", i, 6, 0)
                act.wait_ge(sem("gt_turned"), i + 1)
                nc.scalar.activation(GT[:], ps[3][:, 256:512], ACT.Copy).then_inc(sem("gt_ready"), 1)
                turned_high(14 * i + 12, 0)
                high("d", i, 6, 1)
                silu(14 * i + 13, 1)

            item(0, True)
            with act.Fori(1, NE) as i:
                item(i)
            act.wait_ge(sem("later_table"), 1)
            more = act.value_load(tab[0:1, 0:1], min_val=0, max_val=LATER)
            with act.If(more > 0):
                with act.Fori(0, more) as j:
                    item(j + NE)
            turned_high(14 * more + (14 * NE - 1), 1)
            half_ye(more + NE)
            sqrt_table()
            for c in range(4):
                act.wait_ge(sem("comb_used"), 4 * more + (4 * NE - 3 + c))
                k = slice(2 * c, 2 * c + 2)
                nc.scalar.activation(sq[:, k, 0:SEQ], hT[:, k, META:T], ACT.Square).then_inc(sem("final_squares"), 1)
            for tt in range(2):
                act.wait_ge(sem("final_ss"), tt + 1)
                nc.scalar.activation(rstd[:, tt:tt + 1], ps[tt][:, 0:1], ACT.Sqrt, bias=eps[:, 0:1], scale=1.0 / D).then_inc(sem("final_root"), 1)
            act.wait_ge(sem("final_rstd"), 1)
            for tt in range(2):
                act.wait_ge(sem("final_turn"), 3 + tt)
                nc.scalar.activation(osb2[:, tt, 512:1024], ps[4 + tt][:, :], ACT.Identity, scale=rstd[:, tt:tt + 1]).then_inc(sem("out_ready_act"), 1)

        @block.vector
        def _(dve):
            v = Steps(dve, sem("dve_chain"))
            V = nc.vector

            def mult_add(out_, in0, scalar, in1, s=None, op0=ALU.mult, op1=ALU.add):
                v(V.scalar_tensor_tensor(out=out_, in0=in0, scalar=scalar, in1=in1, op0=op0, op1=op1), s)

            def norm(group, col, toks=slice(0, T), s=None, weights=par):
                n = toks.stop - toks.start
                dve.wait_ge(used(group), 1)
                v(V.reciprocal(rstd[:, 0:n], rstd[:, 0:n]))
                for k in range(KT):
                    mult_add(xn[:, k, 0:n], hT[:, k, toks], par[:, col + k:col + k + 1], rstd[:, 0:n], s, ALU.mult, ALU.mult)

            def square(lo, hi, s, toks=slice(0, T)):
                v(V.tensor_tensor(sq[:, lo:hi, toks], hT[:, lo:hi, toks], hT[:, lo:hi, toks], ALU.mult), s)

            v(V.memset(xp, 0.0), sem("xp_zero"))
            V.memset(crd[:, 0:1], 0.0).then_inc(used("up"), CREDIT["up"])
            V.memset(crd[:, 1:2], 0.0).then_inc(sem("taps_ready"), 8)
            v(V.memset(dtw, 0.0))
            dve.wait_ge(used("xin"), 5)
            square(4, 8, sem("dve_squares"))
            dve.wait_ge(used("param"), 1)
            norm("ss1", C_NME, s=sem("xn1_ready"))
            dve.wait_ge(sem("dt_in"), 16 * 5)
            v(V.tensor_tensor(lam_in[:, 0:64], lam_in[:, 0:64], lam_in[:, 64:128], ALU.mult))
            v(V.tensor_tensor(lam_in[:, 128:192], lam_in[:, 128:192], lam_in[:, 192:256], ALU.mult))
            v(V.tensor_reduce(lam[:, 0:1], lam_in[:, 0:64], AX.X, ALU.add))
            v(V.tensor_reduce(lam[:, 1:2], lam_in[:, 128:192], AX.X, ALU.add), sem("lam_sums"))
            for odd in range(2):
                r = slice(64 * odd, 64 * odd + 64)
                d2 = d_in[r, :].rearrange("p (w t o) -> p w t o", w=2, o=2)
                v(V.tensor_tensor(dskip[r, :], d2[:, 0, :, odd], d2[:, 1, :, odd], ALU.add))
            for j in range(8):
                if j == 4:
                    t = ready(dve, "dt", 0)
                    v(V.tensor_tensor(dtw[:, 0, 0:16], t[:, 0:16], dt_bias, ALU.add))
                    v(V.tensor_tensor(dtw[:, 0, 16:32], t[:, 16:32], dt_bias, ALU.add))
                    v(V.tensor_tensor(dtw[0:META, 0, 32:48], t[0:META, 32:48], dt_bias[0:META, :], ALU.add), used("dt"))
                    mult_add(dtw[:, 1, :], dtw[:, 0, :], -1.0, dtw[:, 0, :], sem("dt_raw"), ALU.mult, ALU.max)
                    dve.wait_ge(sem("dt_log"), 1)
                    mult_add(dtw[:, 4, :], dtw[:, 0, :], 0.0, dtw[:, 3, :], sem("dt_ready"), ALU.max, ALU.add)
                    for tt in range(3):
                        mult_add(dtw[:, 5, 16 * tt:16 * tt + 16], dtw[:, 4, 16 * tt:16 * tt + 16], -1.0, dtw[:, 7, 0:16], sem("a_vec_ready"), ALU.mult, ALU.mult)
                dve.wait_ge(used("proj"), j + 1)
                w = lambda k: par[:, C_CW + 8 * k + j:C_CW + 8 * k + j + 1]
                if j >= 2:
                    dve.wait_ge(sem("xbc_ready"), j - 1)
                c = convt[:, j % 2, :]
                v(V.tensor_scalar(c, xp[:, j, 0:T], w(0), par[:, C_CB + j:C_CB + j + 1], ALU.mult, ALU.add))
                for k in range(1, CONV):
                    mult_add(c, xp[:, j, k:k + T], w(k), c, sem("conv_ready") if k == CONV - 1 else None)
            def ssd_out(pair):
                t = ready(dve, "y", pair)
                mult_add(ysb[:, pair, :], xbc[:, pair, :], dskip[:, pair:pair + 1], t[:, 0:T], used("y"))
                v(V.tensor_tensor(ysb[:, pair, :], ysb[:, pair, :], zs[:, pair, :], ALU.mult), sem("yz_ready"))

            dve.wait_ge(sem("table_in"), 32)
            for h in range(HEADS):
                m, wt = M[:, h % 4], W[:, h % 2]
                for tt, (t0, n) in enumerate(TOKS):
                    dve.wait_ge(sem("w1_ready"), 3 * h + tt + 1)
                    mult_add(wt[0:n, tt, :], UF[0:n, tt, :], dtw[0:n, 4, 16 * tt + h:16 * tt + h + 1], W1[0:n, h % 2, tt, :])
                dve.wait_ge(used("row"), 2 * h + 2)
                v(V.tensor_tensor(m[:, 0:2, :], m[:, 0:2, :], RB[:, h % 2, 0:2, :], ALU.add))
                v(V.tensor_tensor(m[0:META, 2, :], m[0:META, 2, :], RB[0:META, h % 2, 2, :], ALU.add), sem("decay_sum"))
                if h == 0:
                    dve.wait_ge(used("cb"), 6)
                g3 = 3 * (h // 4)
                v(V.tensor_tensor(wt[:, 0:2, :], wt[:, 0:2, :], CB[:, g3:g3 + 2, :], ALU.mult))
                v(V.tensor_tensor(wt[0:META, 2, :], wt[0:META, 2, :], CB[0:META, g3 + 2, :], ALU.mult))
                dve.wait_ge(sem("decay_ready"), h + 1)
                v(V.tensor_tensor(m[:, 0:2, :], m[:, 0:2, :], wt[:, 0:2, :], ALU.mult))
                v(V.tensor_tensor(m[0:META, 2, :], m[0:META, 2, :], wt[0:META, 2, :], ALU.mult), sem("m_ready"))
                if h >= 4 and h % 2 == 0:
                    ssd_out((h - 4) // 2)
            for pair in (2, 3):
                ssd_out(pair)
            for j in range(8):
                t = ready(dve, "rope", j)
                v(V.tensor_tensor(ropet[:, 0, :], t[:, 0:T], sinT, ALU.mult), used("rope"))
                if j < 4:
                    v(V.tensor_tensor(ropet[:, 1, :], qk[:, j, :], cosT, ALU.mult))
                    by_cos = ropet[:, 1, :]
                else:
                    dve.wait_ge(sem("k_by_cos"), j - 3)
                    by_cos = cat[:, j, :]
                v(V.tensor_tensor(qk[:, j, :], ropet[:, 0, :], by_cos, ALU.add), sem("qk_ready"))

            def ssd_norm(g):
                dve.wait_ge(used("gss"), g + 1)
                v(V.reciprocal(sq[:, 4 + g, :], sq[:, 4 + g, :]))
                for k in range(2 * g, 2 * g + 2):
                    mult_add(cat[:, k, :], ysb[:, k, :], par[:, C_SNW + k:C_SNW + k + 1], sq[:, 4 + g, :], sem("cat_ready"), ALU.mult, ALU.mult)
            dve.wait_ge(sem("lam_exp"), 1)
            v(V.tensor_tensor(lam[:, 4:5], lam[:, 3:4], lam[:, 2:3], ALU.subtract))
            v(V.tensor_scalar(lam[:, 4:5], lam[:, 4:5], -LAMBDA_INIT, None, ALU.add))

            def row_max(k):
                n = TOKS[(k % 6) // 2][1]
                t = ready(dve, "score", k)
                v(V.tensor_reduce(stat[0:n, k, 0:1], t[0:n, 0:T], AX.X, ALU.max, negate=True), sem("max_ready"))

            def combine(h, tt):
                n = TOKS[tt][1]
                k = 6 * h + 2 * tt
                dve.wait_ge(used("score"), k + 2)
                v(V.reciprocal(stat[0:n, k:k + 2, 2:3], stat[0:n, k:k + 2, 1:2]))
                v(V.tensor_scalar(stat[0:n, k + 1, 3:4], stat[0:n, k + 1, 2:3], lam[0:n, 4:5], None, ALU.mult))
                pk = pr[0:n, (3 * h + tt) % 2]
                v(V.tensor_scalar(pk[:, 0, :], pk[:, 0, :], stat[0:n, k, 2:3], None, ALU.mult))
                mult_add(at_[0:n, h % 2, tt, :], pk[:, 1, :], stat[0:n, k + 1, 3:4], pk[:, 0, :], sem("a_ready"))

            v(V.tensor_scalar(lam[:, 5:6], par[:, C_SUB:C_SUB + 1], 1.0 - LAMBDA_INIT, None, ALU.mult))

            def softmaxes(h):
                if h >= 2:
                    dve.wait_ge(used("at"), 3 * (h - 1))
                for tt in range(3):
                    row_max(6 * h + 2 * tt)
                    row_max(6 * h + 2 * tt + 1)
                    if tt >= 1:
                        combine(h, tt - 1)
                combine(h, 2)

            softmaxes(0)
            for h in range(ATT):
                if h + 1 < ATT:
                    softmaxes(h + 1)
                if h < 2:
                    ssd_norm(h)
                t = ready(dve, "o", h)
                v(V.tensor_copy(osb[:, h, :], t[:, 0:T]), used("o"))
            for k in range(4):
                dve.wait_ge(used("oss"), k + 1)
                v(V.reciprocal(sq[:, 4 + k, :], sq[:, 4 + k, :]))
                mult_add(cat[:, 4 + k, :], osb[:, k, :], lam[:, 5:6], sq[:, 4 + k, :], sem("cat_ready"), ALU.mult, ALU.mult)
            def filter_argument(k):
                t = ready(dve, "mlp", k)
                x0, x1, x2 = harg[0:64, 0, :], harg[0:64, 1, :], harg[0:64, 2, :]
                v(V.tensor_scalar(x0, t[0:64, 0:T], par[0:64, C_FV + k:C_FV + k + 1], par[0:64, C_FV + 3 + k:C_FV + 4 + k], ALU.add, ALU.mult), used("mlp"))
                v(V.tensor_scalar(x1, x0, 1.0 / (2.0 * math.pi), ROUND, ALU.mult, ALU.add))
                v(V.tensor_scalar(x1, x1, ROUND, None, ALU.subtract))
                mult_add(x0, x1, -TWO_PI_A, x0)
                mult_add(x2, x1, -TWO_PI_B, x0)
                v(V.tensor_scalar(x1, x2, 3.1415925, -3.1415925, ALU.min, ALU.max), sem("arg_ready"))

            def ring_low(n, i=0, k=KT):
                dve.wait_ge(sem("ring_high"), n - B_FF + 1 + 4 * i)
                c = slice(0, 256 * k)
                high = (ring_hi if n < B_HY else ring_hi2)[:, n % 2, c]
                V.tensor_tensor(ring_lo[:, n % RING, c], ring[:, n % RING, c], high.bitcast(F32), ALU.subtract).then_inc(sem("ring_split"), 1)

            def add_to_stream(group, j):
                t = ready(dve, group, j)
                v(V.tensor_tensor(hT[:, j, :], hT[:, j, :], t[:, 0:T], ALU.add), used(group))

            def split_norm(col, s, first):
                for k in range(KT + 1):
                    if k < KT:
                        V.scalar_tensor_tensor(out=xn[:, k, :], in0=hT[:, k, :], scalar=par[:, col + k:col + k + 1], in1=rstd[:],
                                               op0=ALU.mult, op1=ALU.mult).then_inc(sem("xn_plain"), 1)
                    if k >= 1:
                        dve.wait_ge(sem("xn_high"), first + k)
                        V.tensor_tensor(xn_lo[:, k - 1, :], xn[:, k - 1, :], xn_hi[:, k - 1, :].bitcast(F32), ALU.subtract).then_inc(sem(s), 1)

            filter_argument(0)
            for j in range(8):
                if j == 4:
                    filter_argument(1)
                if j >= 6:
                    ring_low(B_FF + j - 6)
                add_to_stream("wo", j)
            v.credit(used("up"), CREDIT["up"])
            V.memset(crd[:, 2:3], 0.0).then_inc(used("gate"), CREDIT["gate"])
            dve.wait_ge(used("ss2"), 1)
            v(V.reciprocal(rstd[:], rstd[:]))
            split_norm(C_NFE, "xn2_ready", 0)
            base = NUMBER[("up", 0)]

            def up(i, b):
                n = base + 4 * (b // 2) + b % 2
                dve.wait_ge(used("gate"), 4 * i + b + 1 + CREDIT["gate"])
                dve.wait_ge(sem("tile_ready"), 8 * i + n + 1)
                h = ffp[:, b % 2, :]
                hi, lo = (a[:, 4 * i + b, :] if isinstance(i, int) else a[:, bass.ds(4 * i + b, 1), :].rearrange("p a t -> p (a t)")
                          for a in (ffh_hi, ffh_lo))
                v(V.tensor_tensor(h, sg[:, b, :], ps[n % 8][:, 0:T], ALU.mult), used("up"))
                v(V.tensor_copy(hi, h))
                v(V.tensor_tensor(lo, h, hi.bitcast(F32), ALU.subtract), sem("ffh_ready"))

            def gate_and_up(i, c, k):
                ring_low(B_FF + 2 * c + 2, i, k)
                up(i, 2 * c)
                up(i, 2 * c + 1)
                ring_low(B_FF + 2 * c + 3, i, k)

            with dve.Fori(0, 5) as i:
                v.loop(i, [(used("up"), 4), (sem("dve_chain"), 4), (sem("ffh_ready"), 4)])
                gate_and_up(i, 0, KT)
                gate_and_up(i, 1, KT)
                v.end(5)
            ring_low(B_DN, 0, 11)
            up(5, 0)
            up(5, 1)
            ring_low(B_DN + 1, 0, 11)
            filter_argument(2)
            for d in range(8):
                if d % 2:
                    add_to_stream("down", d - 1)
                    add_to_stream("down", d)
                if d < 6:
                    ring_low(B_DN + d + 2, 0, 11)

            dve.wait_ge(sem("window_in"), 32)
            for lt, (t0, n) in enumerate(TOKS):
                for c in range(4):
                    t = ready(dve, "kt", 4 * lt + c)
                    v(V.tensor_tensor(kfb[0:n, lt, 512 * c:512 * c + 512], t[0:n, :], win[0:n, lt, 512 * (c % 2):512 * (c % 2) + 512], ALU.mult), used("kt"))
                if lt == 0:
                    v(V.memset(kfb[0:1, 0, D:2 * D], 0.0))
                v(V.tensor_tensor(KE[0:n, lt, :], kfb[0:n, lt, 0:D], kfb[0:n, lt, D:2 * D], ALU.add), sem("ke_ready"))
            dve.wait_ge(used("ss3"), 1)
            v(V.reciprocal(rstd[:], rstd[:]))
            split_norm(C_NMO, "xn3_ready", KT)
            dve.wait_ge(sem("ko_ready"), 3)
            dve.wait_ge(sem("kabs_ready"), 1)
            for pp, ts in ((P, slice(0, 2)), (META, slice(2, 3))):
                v(V.tensor_tensor(kfb[0:pp, ts, 0:D], kfb[0:pp, ts, 0:D], kfb[0:pp, ts, D:2 * D], ALU.add), sem("kabs_sum"))
            t = ready(dve, "kn", 0)
            v(V.reciprocal(invn, t[:, 0:8]), used("kn"))
            dve.wait_ge(used("kspec"), 12)
            v(V.memset(pad[:, :, 0:1], 0.0))
            v(V.memset(pad[:, :, T + 1:T + 2], 0.0), sem("pad_zero"))
            V.memset(crd[:, 4:5], 0.0).then_inc(used("hy"), CREDIT["hy"])
            v.credit(sem("taps_ready"), 8)
            def taps(i, b):
                j = 8 * i + b
                dve.wait_ge(sem("tap0_ready"), 8 * i + b + 1)
                if isinstance(i, int):
                    o, w1, w2 = hyc[:, j, :], par[:, C_HCW + 24 + j:C_HCW + 25 + j], par[:, C_HCW + 48 + j:C_HCW + 49 + j]
                else:
                    o = hyc[:, bass.ds(j, 1), :].rearrange("p a t -> p (a t)")
                    w1, w2 = par[:, bass.ds(j + C_HCW + 24, 1)], par[:, bass.ds(j + C_HCW + 48, 1)]
                mult_add(o, pad[:, b, 1:1 + T], w1, o)
                mult_add(o, pad[:, b, 2:2 + T], w2, o, sem("taps_ready"))

            ring_low(B_HY)
            ring_low(B_HY + 1)
            with dve.Fori(0, 2) as i:
                v.loop(i, [(sem("taps_ready"), 8), (sem("dve_chain"), 8)])
                for b in range(8):
                    taps(i, b)
                    if b % 2:
                        ring_low(B_HY + b // 2 + 2, i)
                v.end(2)
            v(V.tensor_tensor(hyc[:, 8:16, :], hyc[:, 8:16, :], hyc[:, 0:8, :], ALU.mult), sem("v_ready"))
            for b in range(8):
                taps(2, b)
                if b in (1, 3):
                    ring_low(B_HY + b // 2 + 2, 2)
            for k in range(6):
                half, ft = k // 3, k % 3
                n = TOKS[ft][1]
                c = slice(512 * half, 512 * half + 512)
                if k >= 1:
                    dve.wait_ge(sem("spec_ready"), 2 * k)
                tr = ready(dve, "vspec", 2 * k)
                v(V.tensor_tensor(prod[0:n, 0, :], KR[0:n, ft, c], tr[0:n, :], ALU.mult), sem("prod_ready"))
                v(V.tensor_tensor(prod[0:n, 3, :], KI[0:n, ft, c], tr[0:n, :], ALU.mult), sem("prod_ready"))
                ti = ready(dve, "vspec", 2 * k + 1)
                v(V.tensor_tensor(prod[0:n, 1, :], KI[0:n, ft, c], ti[0:n, :], ALU.mult), sem("prod_ready"))
                v(V.tensor_tensor(prod[0:n, 2, :], KR[0:n, ft, c], ti[0:n, :], ALU.mult), sem("prod_ready"))
            for j in range(8):
                t = ready(dve, "inv", j)
                v(V.tensor_scalar(ytmp[:, 0, :], hyc[:, 8 + j, META:T], par[:, C_SKIP + j:C_SKIP + j + 1], None, ALU.mult))
                mult_add(ytmp[:, 1, :], t[:, 0:SEQ], invn[:, j:j + 1], ytmp[:, 0, :], used("inv"))
                v(V.tensor_tensor(xn[:, j, 0:SEQ], ytmp[:, 1, :], hyc[:, 16 + j, META:T], ALU.mult), sem("yh_ready"))
            v(V.memset(crd[:, 5:6], 0.0), sem("hyena_done"))
            def low(part, i, q, p):
                dve.wait_ge(sem(f"{part}_high"), 14 * i + 2 * q + p + 1)
                at = "gud".index(part)
                V.tensor_tensor(w_lo[:, p, at, :], raw[:, p, at, :], w_hi[:, p, at, :].bitcast(F32), ALU.subtract).then_inc(sem(f"{part}_split"), 1)

            for j in range(8):
                t = ready(dve, "ho", j)
                if j == 7:
                    low("g", 0, 0, 0)
                mult_add(hT[:, j, META:T], t[:, 0:SEQ], par[:, C_BOUT + j:C_BOUT + j + 1], hT[:, j, META:T], used("ho"), ALU.add, ALU.add)
            norm("ss4", C_NFO, slice(META, T), sem("xn4_ready"))
            low("u", 0, 0, 0)

            lg, sh, ex = rt[:, 0:16], rt[:, 16:32], rt[:, 32:48]
            rank, pick = rt[:, 48:64], rt[:, 64:80]
            m1 = rt[:, 112:128]
            NI = ITEMS + 1
            place, gatev = rt[:, 384:384 + 2 * NI], rt[:, 416:416 + 2 * NI]
            place3, gate3 = place.rearrange("p (t i) -> p t i", t=2), gatev.rearrange("p (t i) -> p t i", t=2)
            gt_, eq_ = rt[:, 128:256], rt[:, 256:384]
            t = ready(dve, "logit", 0)
            v(V.tensor_copy(lg, t[:, 0:16]), used("logit"))
            for tt in range(2):
                l = lg[:, NE * tt:NE * tt + NE]
                l_f = l.rearrange("p (a f) -> p a f", a=1).to_broadcast([P, NE, NE])
                l_e = l.rearrange("p (e a) -> p e a", a=1).to_broadcast([P, NE, NE])
                gv = gt_[:, 64 * tt:64 * tt + 64].rearrange("p (e f) -> p e f", e=NE)
                ev = eq_[:, 64 * tt:64 * tt + 64].rearrange("p (e f) -> p e f", e=NE)
                v(V.tensor_reduce(m1[:, tt:tt + 1], l, AX.X, ALU.max))
                v(V.tensor_scalar(sh[:, NE * tt:NE * tt + NE], l, m1[:, tt:tt + 1], None, ALU.subtract), sem("logit_shift") if tt == 1 else None)
                v(V.tensor_tensor(gv, l_f, l_e, ALU.is_gt))
                v(V.tensor_tensor(ev, l_f, l_e, ALU.is_equal))
                v(V.tensor_tensor(ev, ev, tri, ALU.mult))
                v(V.tensor_tensor(gv, gv, ev, ALU.add))
                v(V.tensor_reduce(rank[:, NE * tt:NE * tt + NE], gv, AX.X, ALU.add))
            v(V.tensor_scalar(pick, rank, 1.5, None, ALU.is_lt), sem("pick_ready"))
            dve.wait_ge(sem("gate_exp"), 1)
            v(V.tensor_tensor(ex, ex, pick, ALU.mult))
            for tt in range(2):
                e = slice(NE * tt, NE * tt + NE)
                v(V.tensor_reduce(m1[:, 2 + tt:3 + tt], ex[:, e], AX.X, ALU.add))
                v(V.reciprocal(m1[:, 4 + tt:5 + tt], m1[:, 2 + tt:3 + tt]))
                v(V.tensor_scalar(gatev[:, NI * tt:NI * tt + NE], ex[:, e], m1[:, 4 + tt:5 + tt], None, ALU.mult))
            t = ready(dve, "pos", 0)
            v(V.memset(place, -1.0))
            mult_add(place3[:, :, 0:NE], t[:, 0:16].rearrange("p (t e) -> p t e", t=2), 1.0,
                     pick.rearrange("p (t e) -> p t e", t=2), None, ALU.add, ALU.mult)
            v(V.tensor_scalar(place3[:, :, 0:NE], place3[:, :, 0:NE], -1.0, None, ALU.add))

            def column(table, tt, i):
                return table[:, NI * tt + i:NI * tt + i + 1] if isinstance(i, int) else table[:, bass.ds(i + NI * tt, 1)]

            def select(i):
                for tt in range(2):
                    V.tensor_scalar(SEL[:, tt, :], iota, column(place, tt, i), None, ALU.is_equal).then_inc(sem("sel_ready"), 1)

            select(0)
            flag, nth_at, hit, prod3, place2 = (rt[:, a:a + n] for a, n in ((448, 8), (456, 8), (464, 24), (488, 24), (512, 16)))
            hit3, prod3 = hit.rearrange("p (k e) -> p k e", k=LATER), prod3.rearrange("p (k e) -> p k e", k=LATER)

            def over_k(a):
                return a.rearrange("p (k e) -> p k e", k=1).to_broadcast([P, LATER, NE])

            v(V.tensor_scalar(flag, t[:, 16:24], float(CAP) + 0.5, None, ALU.is_gt), used("pos"))
            v(V.tensor_reduce(tabf[0:1, 0:1], flag[0:1, :], AX.X, ALU.add))
            v(V.tensor_tensor_scan(nth_at, flag, flag, 0.0, ALU.add, ALU.bypass))
            v(V.tensor_tensor(nth_at, nth_at, flag, ALU.subtract))
            v(V.tensor_tensor(hit3, over_k(nth_at), nth, ALU.is_equal))
            v(V.tensor_tensor(hit3, hit3, over_k(flag), ALU.mult))
            v(V.tensor_tensor(prod3, hit3, expert, ALU.mult))
            v(V.tensor_reduce(tabf[0:1, 1:1 + LATER], prod3[0:1], AX.X, ALU.add))
            v(V.tensor_copy(tab[0:1, 0:1 + LATER], tabf[0:1, 0:1 + LATER]), sem("later_table"))
            v(V.tensor_scalar(place2.rearrange("p (t e) -> p t e", t=2), place3[:, :, 0:NE], -float(CAP), None, ALU.add))
            for tt in range(2):
                v(V.tensor_tensor(prod3, hit3, over_k(place2[:, NE * tt:NE * tt + NE]), ALU.mult))
                v(V.tensor_reduce(place3[:, tt, NE:ITEMS], prod3, AX.X, ALU.add))
                v(V.tensor_tensor(prod3, hit3, over_k(gatev[:, NI * tt:NI * tt + NE]), ALU.mult))
                v(V.tensor_reduce(gate3[:, tt, NE:ITEMS], prod3, AX.X, ALU.add))

            def hidden(n, p):
                dve.wait_ge(sem("sg_ready"), n + 1)

                V.tensor_tensor(eh[:, p, :], esg[:, p, :], ps[p][:, 256:512], ALU.mult).then_inc(sem("h_ready"), 1)

            def turned_low(n, p):
                dve.wait_ge(sem("eh_high"), n + 1)
                V.tensor_tensor(eh_lo[:, p].rearrange("p a b -> p (a b)"), ps[2 + p][:, 0:256],
                                eh_hi[:, p].rearrange("p a b -> p (a b)").bitcast(F32), ALU.subtract).then_inc(sem("eh_split"), 1)

            def half_ye(i):
                dve.wait_ge(sem("d_used"), 14 * i)
                V.tensor_copy(ye[:, 0:512], ps[4][:, :]).then_inc(sem("ye_dve"), 1)

            def add_result(i, c):
                dve.wait_ge(sem("comb_ready"), 4 * i - 4 + c + 1)
                V.tensor_tensor(hT[:, 2 * c:2 * c + 2, META:T], hT[:, 2 * c:2 * c + 2, META:T],
                                ps[6 + c % 2][:, :].rearrange("p (a b) -> p a b", a=2), ALU.add).then_inc(sem("comb_used"), 1)

            def stage(i, q, p, ahead=True):
                low("d", i, q, p)
                turned_low(14 * i + 2 * q + p, p)
                if ahead:
                    low("g", i, q + 1, p)
                    low("u", i, q + 1, p)

            def item(i, first=False):
                if not first:
                    low("g", i, 0, 0)
                    turned_low(14 * i - 1, 1)
                    low("u", i, 0, 0)
                for half in range(2):
                    dve.wait_ge(sem("xg_high"), 2 * i + half + 1)
                    k = slice(4 * half, 4 * half + 4)
                    V.tensor_tensor(xg_lo[:, k, :].rearrange("p a b -> p (a b)"), ps[6 + half][:, :],
                                    xg_hi[:, k, :].rearrange("p a b -> p (a b)").bitcast(F32), ALU.subtract).then_inc(sem("xg_split"), 1)
                low("g", i, 0, 1)
                if not first:
                    half_ye(i)
                low("u", i, 0, 1)
                hidden(14 * i, 0)
                if not first:
                    add_result(i, 0)
                    add_result(i, 1)
                stage(i, 0, 0)
                hidden(14 * i + 1, 1)
                if not first:
                    add_result(i, 2)
                    add_result(i, 3)
                for tt in range(2):
                    V.tensor_scalar(SELG[:, tt, :], iota, column(place, tt, i), column(gatev, tt, i), ALU.is_equal, ALU.mult).then_inc(sem("selg_ready"), 1)
                select(i + 1)
                stage(i, 0, 1)
                with dve.Fori(0, STAGES // 2 - 2) as q:
                    for p in range(2):
                        hidden(14 * i + 2 * q + 2 + p, p)
                        stage(i, q + 1, p)
                hidden(14 * i + 12, 0)
                stage(i, 6, 0, ahead=False)
                low("d", i, 6, 1)
                hidden(14 * i + 13, 1)

            item(0, True)
            with dve.Fori(1, NE) as i:
                item(i)
            more = dve.value_load(tab[0:1, 0:1], min_val=0, max_val=LATER)
            with dve.If(more > 0):
                with dve.Fori(0, more) as j:
                    item(j + NE)
            turned_low(14 * more + (14 * NE - 1), 1)
            half_ye(more + NE)
            for c in range(4):
                add_result(more + NE, c)
                dve.wait_ge(sem("comb_used"), 4 * more + (4 * NE - 3 + c))
                for k in (2 * c, 2 * c + 1):
                    V.tensor_scalar(xn[:, k, 0:SEQ], hT[:, k, META:T], par[:, C_FIN + k:C_FIN + k + 1], None, ALU.mult).then_inc(sem("final_xn"), 1)
            dve.wait_ge(sem("final_root"), 2)
            V.reciprocal(rstd[:, 0:2], rstd[:, 0:2]).then_inc(sem("final_rstd"), 1)
            dve.wait_ge(sem("final_rstd"), 1)
            for tt in range(2):
                dve.wait_ge(sem("final_turn"), tt + 1)
                V.tensor_scalar(osb2[:, tt, 0:512], ps[2 + tt][:, :], rstd[:, tt:tt + 1], None, ALU.mult).then_inc(sem("out_ready_dve"), 1)

        @block.tensor
        def _(pe):
            def open_tile(group, k):
                n = NUMBER[(group, k)]
                if n >= 8:
                    g, j = ORDER[n - 8]
                    if g == "vspec":
                        pe.wait_ge(sem("prod_ready"), 2 * j + 2)
                    else:
                        pe.wait_ge(used(g), j + 1 + CREDIT.get(g, 0))
                return ps[n % 8]

            def close(ins):
                ins.then_inc(sem("tile_ready"), 1)

            def mm(o, l, r, start=True, stop=True):
                return nc.tensor.matmul(o, l, r, start=start, stop=stop)

            def product(o, hi, lo, moving, start, stop):
                mm(o, hi, moving[0], start, False)
                mm(o, hi, moving[1], False, False)
                return mm(o, lo, moving[0], False, stop)

            def split_block(n, k=KT):
                return [a.rearrange("p (k n) -> p k n", k=k) for a in ((ring_hi if n < B_HY else ring_hi2)[:, n % 2, 0:256 * k], ring_lo[:, n % RING, 0:256 * k])]

            def turn(o, src, n=P):
                return nc.tensor.transpose(o, src, ident[0:n, 0:n])

            def arrived(n):
                pe.wait_ge(slot_in[n % RING], 16 * (n // RING + 1))

            def linear(group, j0, n, rhs, cols=T, coming=None):
                arrived(n)
                w = slot(n)
                for j in range(2):
                    o = open_tile(group, j0 + j)
                    for k in range(KT):
                        if coming is not None and j == 0:
                            pe.wait_ge(coming, k + 1)
                        last = mm(o[:, 0:cols], w[:, k, 128 * j:128 * j + 128], rhs[:, k, 0:cols], k == 0, k == KT - 1)
                    close(last)

            def sum_squares(group, k, lo, hi, cols=slice(0, T)):
                o = open_tile(group, k)
                for q in range(lo, hi):
                    last = mm(o[:, 0:cols.stop - cols.start], ones[:], sq[:, q, cols], q == lo, q == hi - 1)
                close(last)

            def add_squares(group, s, k0, n, toks=slice(0, T)):
                o = open_tile(group, 0) if k0 == 0 else ps[NUMBER[(group, 0)] % 8]
                for k in range(k0, k0 + n):
                    pe.wait_ge(sem(s), k + 1)
                    last = mm(o[:, 0:toks.stop - toks.start], ones[:], sq[:, k, toks], k == 0, k == KT - 1)
                if k0 + n == KT:
                    close(last)

            pe.wait_ge(sem("ident_in"), 16)
            pe.wait_ge(sem("x_in"), 32)
            for tt in range(2):
                for half in range(2):
                    o = open_tile("xin", 2 * tt + half)
                    for c in range(4):
                        k = 4 * half + c
                        last = turn(o[:, P * c:P * c + P], xtok[:, tt, P * k:P * k + P])
                    close(last)
            o = open_tile("xin", 4)
            for k in range(KT):
                last = turn(o[:, META * k:META * k + META], mtok[0:META, P * k:P * k + P], META)
            close(last)
            pe.wait_ge(sem("param_in"), 16 * 25)
            o = open_tile("param", 0)
            turn(o[:, 0:C_A], prow[0:C_A, 0, :], C_A)
            turn(o[:, C_HCW:C_B], prow[0:C_B - P, 1, :], C_B - P)
            close(turn(o[0:64, C_FV:C_FV + 6], prow[0:6, 2, 0:64], 6))
            pe.wait_ge(sem("pool_consts"), 3)
            pe.wait_ge(sem("act_squares"), 1)
            pe.wait_ge(sem("dve_squares"), 1)
            sum_squares("ss1", 0, 0, KT)
            for n in range(6):
                linear("proj", 2 * n, n, xn, coming=sem("xn1_ready") if n == 0 else None)
                if n == 1:
                    pe.wait_ge(sem("dt_in"), 16 * 5)
                    o = open_tile("dt", 0)
                    for tt, (t0, m) in enumerate(TOKS):
                        for k in range(KT):
                            last = mm(o[0:m, 16 * tt:16 * tt + 16], xn[:, k, t0:t0 + m], wdt[:, k, :], k == 0, k == KT - 1)
                    close(last)
            pe.wait_ge(sem("a_vec_ready"), 3)
            pe.wait_ge(sem("table_in"), 32)
            for way, U in enumerate((UF, UB)):
                o = open_tile("cs", way)
                for tt, (t0, n) in enumerate(TOKS):
                    last = mm(o[0:HEADS, 0:T], dtw[0:n, 5, 16 * tt + 8 * way:16 * tt + 8 * way + 8], U[0:n, tt, :], tt == 0, tt == 2)
                close(last)
            o = open_tile("cs", 2)
            for tt, (t0, n) in enumerate(TOKS):
                for way, U in enumerate((UF, UB)):
                    for st, (s0, m) in enumerate(TOKS):
                        last = mm(o[0:n, 16 * tt + 8 * way:16 * tt + 8 * way + 8], U[0:m, st, t0:t0 + n],
                                  dtw[0:m, 5, 16 * st + 8 * way:16 * st + 8 * way + 8], st == 0, st == 2)
            close(last)
            pe.wait_ge(sem("xbc_ready"), 8)
            for tt, (t0, n) in enumerate(TOKS):
                o = open_tile("xs", tt)
                for c in range(4):
                    last = turn(o[0:n, P * c:P * c + P], xbc[:, c, t0:t0 + n])
                close(last)
            for g in range(2):
                for tt, (t0, n) in enumerate(TOKS):
                    o = open_tile("cb", 3 * g + tt)
                    close(mm(o[0:n, 0:T], xbc[:, 4 + g, t0:t0 + n], xbc[:, 6 + g, :]))
            pe.wait_ge(used("cs"), 3)
            pe.wait_ge(used("xs"), 3)
            for s in range(10):
                if s < 8:
                    for way in range(2):
                        o = open_tile("row", 2 * s + way)
                        close(mm(o[:, 0:T], sel8[:, P * s:P * s + P], csr[0:HEADS, way, :]))
                if s < 6:
                    linear("proj", 12 + 2 * s, 6 + s, xn)
                if s >= 3 and s % 2 == 1:
                    pair = (s - 3) // 2
                    o = open_tile("y", pair)
                    for h in (2 * pair, 2 * pair + 1):
                        pe.wait_ge(sem("m_ready"), h + 1)
                        r = 64 * (h % 2)
                        for tt, (t0, n) in enumerate(TOKS):
                            last = mm(o[r:r + 64, 0:T], xT[0:n, tt, 64 * h:64 * h + 64], M[0:n, h % 4, tt, :], tt == 0, tt == 2)
                    close(last)
            pe.wait_ge(used("proj"), 24)
            for j in range(8):
                o = open_tile("rope", j)
                close(mm(o[:, 0:T], perm, qk[:, j, :]))
            pe.wait_ge(sem("act_squares"), 2)
            for g in range(2):
                sum_squares("gss", g, 2 * g, 2 * g + 2)
            for tt, (t0, n) in enumerate(TOKS):
                o = open_tile("vt", tt)
                for c in range(4):
                    last = turn(o[0:n, P * c:P * c + P], vf[:, c, t0:t0 + n])
                close(last)
            pe.wait_ge(sem("qk_ready"), 8)
            pe.wait_ge(used("vt"), 3)

            def scores(h):
                for tt, (t0, n) in enumerate(TOKS):
                    for m in range(2):
                        o = open_tile("score", 6 * h + 2 * tt + m)
                        r = slice(64 * m, 64 * m + 64)
                        close(mm(o[0:n, 0:T], qk[r, h, t0:t0 + n], qk[r, 4 + h, :]))

            scores(0)
            for h in range(ATT):
                if h + 1 < ATT:
                    scores(h + 1)
                pe.wait_ge(sem("a_ready"), 3 * h + 3)
                for kt, (k0, m) in enumerate(TOKS):
                    o = open_tile("at", 3 * h + kt)
                    for tt, (t0, n) in enumerate(TOKS):
                        last = turn(o[0:m, t0:t0 + n], at_[0:n, h % 2, tt, k0:k0 + m], n)
                    close(last)
                o = open_tile("o", h)
                pe.wait_ge(used("at"), 3 * h + 3)
                for kt, (k0, m) in enumerate(TOKS):
                    last = mm(o[:, 0:T], vT[0:m, kt, P * h:P * h + P], aT[0:m, h % 2, kt, :], kt == 0, kt == 2)
                close(last)
            pe.wait_ge(sem("act_squares"), 3)
            for k in range(4):
                sum_squares("oss", k, k, k + 1)

            def filter_layer(k):
                o = open_tile("mlp", k)
                if k:
                    pe.wait_ge(sem("sin_ready"), k)
                close(mm(o[0:64, 0:T], fw23[:, k - 1, :] if k else fw1[:], harg[0:64, 3, :] if k else zpos[:]))

            pe.wait_ge(sem("filter_in"), 64)
            pe.wait_ge(sem("cat_ready"), 4)
            filter_layer(0)
            for part in range(2):
                for j in range(4):
                    n = B_WO + j // 2
                    if part == 0:
                        if j % 2 == 0:
                            arrived(n)
                        open_tile("wo", j)
                    o = ps[NUMBER[("wo", j)] % 8]
                    for k in range(4 * part, 4 * part + 4):
                        if j == 0:
                            pe.wait_ge(sem("cat_ready"), k + 1)
                        last = mm(o[:, 0:T], slot(n)[:, k, P * (j % 2):P * (j % 2) + P], cat[:, k, :], k == 0, k == KT - 1)
                    if part:
                        close(last)
            filter_layer(1)
            add_squares("ss2", "squares2", 0, 2)
            linear("wo", 4, B_WO + 2, cat)
            add_squares("ss2", "squares2", 2, 2)
            linear("wo", 6, B_WO + 3, cat)
            add_squares("ss2", "squares2", 4, 4)
            base = NUMBER[("gate", 0)]
            for n in range(base - 8, base):
                g, j = ORDER[n]
                pe.wait_ge(used(g), j + 1)

            def swiglu_columns(i, c):
                for part in range(2):
                    n = B_FF + 2 * c + part
                    pe.wait_ge(sem("ring_split"), 2 * c + part + 1 + 4 * i)
                    w_hi_, w_lo_ = split_block(n)
                    for j in range(2):
                        pe.wait_ge(used(("gate", "up")[part]), 4 * i + 2 * c + j + 1)
                        o = ps[(base + 4 * c + 2 * part + j) % 8]
                        for k in range(KT):
                            if c == 0 and part == 0 and j == 0:
                                pe.wait_ge(sem("xn2_ready"), k + 1)
                            m = slice(P * j, P * j + P)
                            last = product(o[:, 0:T], w_hi_[:, k, m], w_lo_[:, k, m], (xn_hi[:, k, :], xn_lo[:, k, :]), k == 0, k == KT - 1)
                        close(last)

            with pe.Fori(0, 5) as i:
                swiglu_columns(i, 0)
                swiglu_columns(i, 1)
            swiglu_columns(5, 0)
            filter_layer(2)
            for b in range(4):
                for half in range(2):
                    n = B_DN + 2 * b + half
                    pe.wait_ge(sem("ring_split"), n - B_FF + 1)
                    w_hi_, w_lo_ = split_block(n, 11)
                    if half == 0:
                        o2 = [open_tile("down", 2 * b + j) for j in range(2)]
                    for j in range(2):
                        for k in range(11):
                            if b == 0 and j == 0:
                                pe.wait_ge(sem("ffh_ready"), 11 * half + k + 1)
                            m = slice(P * j, P * j + P)
                            last = product(o2[j][:, 0:T], w_hi_[:, k, m], w_lo_[:, k, m], (ffh_hi[:, 11 * half + k, :], ffh_lo[:, 11 * half + k, :]),
                                           half == 0 and k == 0, half == 1 and k == 10)
                        if half:
                            close(last)
                    if half == 0:
                        last.then_inc(sem("half_done"), 1)
                if b:
                    add_squares("ss3", "squares3", 2 * b - 2, 2)
            add_squares("ss3", "squares3", 6, 2)
            pe.wait_ge(sem("sin_ready"), 3)
            pe.wait_ge(sem("window_in"), 32)
            for k in range(12):
                t0, n = TOKS[k // 4]
                o = open_tile("kt", k)
                close(mm(o[0:n, :], harg[0:64, 3, t0:t0 + n], fw4[0:64, 512 * (k % 4):512 * (k % 4) + 512]))
            for k in range(12):
                pe.wait_ge(sem("ke_ready" if k % 4 < 2 else "ko_ready"), 3)
                f0, nf = TOKS[k // 4]
                table, src = (CF, KE) if k % 4 < 2 else (SF, KO)
                o = open_tile("kspec", k)
                for tt, (t0, n) in enumerate(TOKS):
                    last = mm(o[0:nf, :], table[0:n, tt, f0:f0 + nf], src[0:n, tt, 512 * (k % 2):512 * (k % 2) + 512], tt == 0, tt == 2)
                close(last)
            pe.wait_ge(sem("kabs_sum"), 2)
            o = open_tile("kn", 0)
            for c in range(KT):
                for tt, (t0, n) in enumerate(TOKS):
                    last = mm(o[:, c:c + 1], kfb[0:n, tt, P * c:P * c + P], ones[0:n, 0:1], tt == 0, tt == 2)
            close(last)
            pe.wait_ge(sem("xn3_ready"), KT)
            base_hy = NUMBER[("hy", 0)]
            for n in range(base_hy - 8, base_hy):
                g, j = ORDER[n]
                pe.wait_ge(used(g), j + 1)
            with pe.Fori(0, 3) as i:
                for b in range(4):
                    n = B_HY + b
                    pe.wait_ge(sem("ring_split"), n - B_FF + 1 + 4 * i)
                    w_hi_, w_lo_ = split_block(n)
                    for j in range(2):
                        pe.wait_ge(used("hy"), 8 * i + 2 * b + j + 1)
                        o = ps[(base_hy + 2 * b + j) % 8]
                        for k in range(KT):
                            m = slice(P * j, P * j + P)
                            last = product(o[:, 0:T], w_hi_[:, k, m], w_lo_[:, k, m], (xn_hi[:, k, :], xn_lo[:, k, :]), k == 0, k == KT - 1)
                        close(last)
            pe.wait_ge(sem("v_ready"), 1)
            for k in range(6):
                t0, n = TOKS[k // 2]
                o = open_tile("vx", k)
                for c in range(4):
                    last = turn(o[0:n, P * c:P * c + P], hyc[:, 8 + 4 * (k % 2) + c, t0:t0 + n])
                close(last)
            pe.wait_ge(used("vx"), 6)
            for k in range(12):
                half, ft = k // 6, k // 2 % 3
                f0, nf = TOKS[ft]
                o = open_tile("vspec", k)
                for tt, (t0, n) in enumerate(TOKS):
                    last = mm(o[0:nf, :], (CF, SF)[k % 2][0:n, tt, f0:f0 + nf], vtok[0:n, tt, 512 * half:512 * half + 512], tt == 0, tt == 2)
                close(last)
            for j in range(8):
                pe.wait_ge(sem("spec_ready"), 6 if j < 4 else 12)
                o = open_tile("inv", j)
                for tt, (f0, nf) in enumerate(TOKS):
                    mm(o[:, 0:SEQ], YR[0:nf, tt, P * j:P * j + P], CI[0:nf, tt, :], tt == 0, False)
                    last = mm(o[:, 0:SEQ], YI[0:nf, tt, P * j:P * j + P], SI[0:nf, tt, :], False, tt == 2)
                close(last)
            for b in range(4):
                linear("ho", 2 * b, B_HO + b, xn, SEQ, coming=sem("yh_ready") if b == 0 else None)
                if b:
                    add_squares("ss4", "squares4", 2 * b - 2, 2, slice(META, T))
            add_squares("ss4", "squares4", 6, 2, slice(META, T))
            def turn_tokens(half):
                for tt in range(2):
                    o = open_tile("xk", 2 * half + tt)
                    for c in range(4):
                        last = turn(o[:, P * c:P * c + P], xn[:, 4 * half + c, P * tt:P * tt + P])
                    close(last)

            pe.wait_ge(sem("xn4_ready"), KT // 2)
            turn_tokens(0)
            pe.wait_ge(sem("router_in"), 16)
            o = open_tile("logit", 0)
            for tt in range(2):
                for k in range(KT):
                    if tt == 0:
                        pe.wait_ge(sem("xn4_ready"), k + 1)
                    last = mm(o[:, NE * tt:NE * tt + NE], xn[:, k, P * tt:P * tt + P], router[:, k, :], k == 0, k == KT - 1)
            close(last)
            turn_tokens(1)
            pe.wait_ge(sem("pick_ready"), 1)
            o = open_tile("pos", 0)
            pick = rt[:, 64:80]
            for tt in range(2):
                for st in range(2):
                    mm(o[:, NE * tt:NE * tt + NE], US[:, st, P * tt:P * tt + P], pick[:, NE * st:NE * st + NE], st == 0, st == 1)
            for st in range(2):
                last = mm(o[:, 16:24], ones[:], pick[:, NE * st:NE * st + NE], st == 0, st == 1)
            close(last)
            def columns(part, n, p):
                pe.wait_ge(sem(f"{part}_split"), n + 1)
                at = "gud".index(part)
                w = [a[:, p, at, :].rearrange("p (k n) -> p k n", k=KT) for a in (w_hi, w_lo)]
                for k in range(KT):
                    last = product(ps[p][:, 256 * at:256 * at + 256], xg_hi[:, k, :], xg_lo[:, k, :], [a[:, k, :] for a in w], k == 0, k == KT - 1)
                last.then_inc(sem(f"{part}_used"), 1)

            def turn_hidden(n, p):
                pe.wait_ge(sem("h_ready"), n + 1)
                for j in range(2):
                    last = turn(ps[2 + p][:, P * j:P * j + P], eh[:, p, P * j:P * j + P])
                last.then_inc(sem("turned"), 1)

            def down(n, p, end=False):
                pe.wait_ge(sem("d_split"), n + 1)
                pe.wait_ge(sem("eh_split"), n + 1)
                w = [a[:, p, 2, :].rearrange("p (k n) -> p k n", k=2) for a in (w_hi, w_lo)]
                for half in range(2):
                    for j in range(2):
                        last = product(ps[4 + half][:, :], eh_hi[:, p, j, :], eh_lo[:, p, j, :],
                                       [a[:, j, 512 * half:512 * half + 512] for a in w], False, end and j == 1)
                last.then_inc(sem("d_used"), 1)

            def add_result(i, c):
                if c >= 2:
                    pe.wait_ge(sem("comb_used"), 4 * i - 4 + c - 1)
                for d in range(2):
                    last = mm(ps[6 + c % 2][:, SEQ * d:SEQ * d + SEQ], ye[:, P * (2 * c + d):P * (2 * c + d) + P], GT[:])
                last.then_inc(sem("comb_ready"), 1)

            def gather(i):
                pe.wait_ge(sem("sel_ready"), 2 * i + 2)
                for d in range(KT):
                    for tt in range(2):
                        o = ps[6 + d // 4][:, CAP * (d % 4):CAP * (d % 4) + CAP]
                        if isinstance(i, int):
                            last = mm(o, xtk[:, tt, P * d:P * d + P], SEL[:, tt, :].bitcast(F32), tt == 0, tt == 1)
                            continue
                        mm(o, xtk_hi[:, tt, P * d:P * d + P], SEL[:, tt, :], tt == 0, False)
                        last = mm(o, xtk_lo[:, tt, P * d:P * d + P], SEL[:, tt, :], False, tt == 1)
                    if d % 4 == 3:
                        last.then_inc(sem("gather_ready"), 1)

            def step(n, p):
                columns("g", n, p)
                turn_hidden(n - 1, 1 - p)
                columns("u", n, p)
                down(n - 1, 1 - p)

            def item(i, first=False):
                if not first:
                    pe.wait_ge(sem("gt_ready"), i)
                    turn_hidden(14 * i - 1, 1)
                gather(i)
                if not first:
                    down(14 * i - 1, 1, end=True)
                pe.wait_ge(sem("xg_split"), 2 * i + 2)
                columns("g", 14 * i, 0)
                columns("u", 14 * i, 0)
                if not first:
                    pe.wait_ge(sem("ye_dve"), i)
                    pe.wait_ge(sem("ye_act"), i)
                    pe.wait_ge(sem("gt_ready"), i)
                    add_result(i, 0)
                    add_result(i, 1)
                columns("g", 14 * i + 1, 1)
                turn_hidden(14 * i, 0)
                columns("u", 14 * i + 1, 1)
                if not first:
                    add_result(i, 2)
                    add_result(i, 3)
                for bank in (4, 5):
                    nc.tensor.matmul(ps[bank][:, :], zero16[:, 0:CAP], zero16[:], start=True, stop=False)
                down(14 * i, 0)
                with pe.Fori(0, STAGES // 2 - 2) as q:
                    for p in range(2):
                        step(14 * i + 2 * q + 2 + p, p)
                step(14 * i + 12, 0)
                pe.wait_ge(sem("selg_ready"), 2 * i + 2)
                for tt in range(2):
                    last = turn(ps[3][:, SEQ + P * tt:SEQ + P * tt + P], SELG[:, tt, :])
                last.then_inc(sem("gt_turned"), 1)
                step(14 * i + 13, 1)

            pe.wait_ge(used("logit"), 1)
            pe.wait_ge(used("pos"), 1)
            pe.wait_ge(used("xk"), 4)
            item(0, True)
            pe.wait_ge(sem("xtk_ready"), 4)
            with pe.Fori(1, NE) as i:
                item(i)
            pe.wait_ge(sem("later_table"), 1)
            more = pe.value_load(tab[0:1, 0:1], min_val=0, max_val=LATER)
            with pe.If(more > 0):
                with pe.Fori(0, more) as j:
                    item(j + NE)
            turn_hidden(14 * more + (14 * NE - 1), 1)
            down(14 * more + (14 * NE - 1), 1, end=True)
            i = more + NE
            pe.wait_ge(sem("ye_dve"), i)
            pe.wait_ge(sem("ye_act"), i)
            pe.wait_ge(sem("gt_ready"), i)
            for c in range(4):
                add_result(i, c)
            for half in range(2):
                for c in (2 * half, 2 * half + 1):
                    pe.wait_ge(sem("final_squares"), c + 1)
                    for tt in range(2):
                        for k in (2 * c, 2 * c + 1):
                            last = mm(ps[tt][:, 0:1], sq[:, k, P * tt:P * tt + P], ones[:, 0:1], k == 0, k == KT - 1)
                        if c == 3:
                            last.then_inc(sem("final_ss"), 1)
                pe.wait_ge(sem("final_xn"), 4 * half + 4)
                for tt in range(2):
                    for k in range(4):
                        last = turn(ps[2 + 2 * half + tt][:, P * k:P * k + P], xn[:, 4 * half + k, P * tt:P * tt + P])
                    last.then_inc(sem("final_turn"), 1)


_INS = ["x", "meta_tokens", "norm_mix_even", "w_in_ab", "ssd_conv_w", "ssd_conv_b", "ssd_a_log", "ssd_dt_bias", "ssd_d",
        "ssd_norm_w", "diff_lambda", "diff_subln_w", "w_out_ab", "norm_ffn_even", "ffn_w_gate", "ffn_w_up", "ffn_w_down",
        "norm_mix_odd", "hy_w_in", "hy_b_in", "hy_conv_w", "hy_conv_b", "hy_f_w1", "hy_f_b1", "hy_f_w2", "hy_f_b2",
        "hy_f_w3", "hy_f_b3", "hy_f_w4", "hy_f_freq", "hy_skip", "hy_w_out", "hy_b_out", "norm_ffn_odd", "moe_router",
        "moe_w_gate", "moe_w_up", "moe_w_down", "final_norm"]


def kernel(**inputs):
    import numpy as _np
    import concourse.bacc as _bacc
    from concourse import mybir as _mybir
    from concourse.bass_utils import run_bass_kernel_spmd as _run

    nc = _bacc.Bacc("TRN2", target_bir_lowering=False, num_devices=1)
    arrays, args = {}, {}
    given = {name: _np.ascontiguousarray(inputs[name]) for name in _INS}
    for name, a in list(given.items()) + list(shape_constants().items()):
        arrays[f"in_{name}_dram"] = a
        args[name] = nc.dram_tensor(f"in_{name}_dram", a.shape, _mybir.dt.from_np(a.dtype), kind="ExternalInput").ap()
    out = nc.dram_tensor("out_0_dram", (1, SEQ, D), _mybir.dt.float32, kind="ExternalOutput").ap()
    trunk(nc, args, out)
    r = _run(nc, [arrays], core_ids=[0])
    return r.results[0]["out_0_dram"]
```
